# Optimizing a Trainium2 kernel written in Bass

```python
import math
import jax, jax.numpy as jnp
from jax import lax
import numpy as np

D_MODEL = 1024
BATCH = 1
SEQ = 1024
DEPTH = 1

D_MIX = D_MODEL
N_HEADS_A = 8
HEAD_DIM_A = 64
D_A = N_HEADS_A * HEAD_DIM_A
KV_RANK = 128
N_IDX_HEADS = 8
IDX_DIM = 32
TOPK_MAX = 256
Q_BLOCK = 128
N_POOL_GROUPS = 4
POOL_GROUP_DIM = 64
D_B = N_POOL_GROUPS * POOL_GROUP_DIM
POOL_WINDOWS = (2, 4, 8, 16)
D_C = D_MIX - D_A - D_B
CONV_WIDTH = 31
COL_Q = D_A
COL_KV = COL_Q + KV_RANK
COL_IQ = COL_KV + N_IDX_HEADS * IDX_DIM
COL_IK = COL_IQ + IDX_DIM
COL_IW = COL_IK + N_IDX_HEADS
COL_POOL = COL_IW + D_B
D_IN = COL_POOL + 2 * D_C
SPLIT_POINTS = (COL_Q, COL_KV, COL_IQ, COL_IK, COL_IW, COL_POOL)
N_EXPERTS = 16
N_EXPERT_GROUPS = 4
EXPERTS_PER_GROUP = N_EXPERTS // N_EXPERT_GROUPS
TOP_K = 2
D_EXPERT = 512
MOE_CHUNK = 2048
ALPHA = (2 * DEPTH) ** 0.25
BETA = (8 * DEPTH) ** -0.25
LN_EPS = 1e-5

kernel_name = "hymba_dsa_pool_conformer_groupmoe_deepnorm"

def layer_norm(x, g, b):
    xf = x.astype(jnp.float32)
    mu = jnp.mean(xf, axis=-1, keepdims=True)
    var = jnp.mean(jnp.square(xf - mu), axis=-1, keepdims=True)
    return ((xf - mu) * lax.rsqrt(var + LN_EPS) * g.astype(jnp.float32) + b.astype(jnp.float32)).astype(x.dtype)

def rms_norm(x, g):
    xf = x.astype(jnp.float32)
    ms = jnp.mean(jnp.square(xf), axis=-1, keepdims=True)
    return (xf * lax.rsqrt(ms + LN_EPS) * g.astype(jnp.float32)).astype(x.dtype)

def dsa_attention(q, c_kv, iq, ik, iw, w_uk, w_uv):
    B, S = q.shape[0], q.shape[1]
    topk = min(TOPK_MAX, S // 4)
    nb = S // Q_BLOCK
    q_lat = jnp.einsum('bshd,hrd->bshr', q, w_uk) * (HEAD_DIM_A ** -0.5)
    key_pos = jnp.arange(S)

    def to_blocks(a):
        return a.reshape((B, nb, Q_BLOCK) + a.shape[2:]).swapaxes(0, 1)

    def block_fn(args):
        blk, q_b, iq_b, iw_b = args
        q_pos = blk * Q_BLOCK + jnp.arange(Q_BLOCK)
        logits = jnp.einsum('bqhd,bsd->bqhs', iq_b, ik).astype(jnp.float32)
        idx_score = jnp.einsum('bqhs,bqh->bqs', jax.nn.relu(logits), iw_b.astype(jnp.float32))
        causal = key_pos[None, :] <= q_pos[:, None]
        idx_score = jnp.where(causal[None], idx_score, -jnp.inf)
        _, sel = lax.top_k(idx_score, topk)
        c_sel = jax.vmap(lambda c, i: c[i])(c_kv, sel)
        s = jnp.einsum('bqhr,bqkr->bqhk', q_b, c_sel).astype(jnp.float32)
        valid = sel <= q_pos[None, :, None]
        s = jnp.where(valid[:, :, None, :], s, -jnp.inf)
        p = jax.nn.softmax(s, axis=-1).astype(c_sel.dtype)
        return jnp.einsum('bqhk,bqkr->bqhr', p, c_sel)

    o_lat = lax.map(block_fn, (jnp.arange(nb), to_blocks(q_lat), to_blocks(iq), to_blocks(iw)))
    o_lat = o_lat.swapaxes(0, 1).reshape(B, S, N_HEADS_A, KV_RANK)
    o = jnp.einsum('bshr,hrd->bshd', o_lat, w_uv)
    return o.reshape(B, S, D_A)

def multi_scale_pool(u, w_pool, scale):
    B, S = u.shape[0], u.shape[1]
    ug = u.reshape(B, S, N_POOL_GROUPS, POOL_GROUP_DIM).astype(jnp.float32)
    cs = jnp.cumsum(ug, axis=1)
    t = jnp.arange(1, S + 1, dtype=jnp.float32)
    outs = []
    for gi, w in enumerate(POOL_WINDOWS):
        c = cs[:, :, gi]
        prev = jnp.pad(c, ((0, 0), (w, 0), (0, 0)))[:, :S]
        cnt = jnp.minimum(t, float(w))[None, :, None]
        outs.append((c - prev) / cnt - ug[:, :, gi])
    pooled = jnp.stack(outs, axis=2).astype(u.dtype)
    y = jnp.einsum('bsgc,gcd->bsgd', pooled, w_pool)
    return y.reshape(B, S, D_B) * scale

def conformer_conv(u, conv_w, conv_b, ln_g, ln_b):
    a, gate = jnp.split(u, 2, axis=-1)
    h = a * jax.nn.sigmoid(gate)
    h = lax.conv_general_dilated(h, conv_w, window_strides=(1,), padding=[(CONV_WIDTH - 1, 0)],
                                 dimension_numbers=('NWC', 'WIO', 'NWC'),
                                 feature_group_count=D_C) + conv_b
    h = layer_norm(h, ln_g, ln_b)
    return jax.nn.silu(h)

def grouped_moe(x, router_w, router_bias, w_gate, w_up, w_down):
    B, S, D = x.shape
    N = B * S
    xt = x.reshape(N, D)
    aff = jax.nn.sigmoid(jnp.dot(xt, router_w).astype(jnp.float32))
    sel_score = aff + router_bias.astype(jnp.float32)
    grp_score = lax.top_k(sel_score.reshape(N, N_EXPERT_GROUPS, EXPERTS_PER_GROUP), TOP_K)[0].sum(-1)
    best = jnp.argmax(grp_score, axis=-1)
    in_group = (jnp.arange(N_EXPERTS) // EXPERTS_PER_GROUP)[None, :] == best[:, None]
    _, top_idx = lax.top_k(jnp.where(in_group, sel_score, -jnp.inf), TOP_K)
    top_aff = jnp.take_along_axis(aff, top_idx, axis=-1)
    gates_k = top_aff / jnp.sum(top_aff, axis=-1, keepdims=True)
    gates = jnp.sum(jax.nn.one_hot(top_idx, N_EXPERTS, dtype=jnp.float32) * gates_k[..., None], axis=1)
    chunk = math.gcd(N, MOE_CHUNK)

    def chunk_fn(args):
        xc, gc = args
        h = jax.nn.silu(jnp.einsum('cd,edf->cef', xc, w_gate)) * jnp.einsum('cd,edf->cef', xc, w_up)
        h = h * gc[:, :, None].astype(h.dtype)
        return jnp.einsum('cef,efd->cd', h, w_down)

    y = lax.map(chunk_fn, (xt.reshape(-1, chunk, D), gates.reshape(-1, chunk, N_EXPERTS)))
    return y.reshape(B, S, D)

def setup_inputs(seed: int = 0) -> dict:
    key = jax.random.key(seed)
    ks = jax.random.split(key, 24)
    L = DEPTH
    nrm = lambda k, shape, s: jax.random.normal(k, shape, jnp.float32) * s
    return {
        "x": nrm(ks[0], (BATCH, SEQ, D_MODEL), 1.0),
        "w_in": nrm(ks[1], (L, D_MODEL, D_IN), D_MODEL ** -0.5),
        "kv_norm_g": 1.0 + nrm(ks[2], (L, KV_RANK), 0.02),
        "w_uk": nrm(ks[3], (L, N_HEADS_A, KV_RANK, HEAD_DIM_A), KV_RANK ** -0.5),
        "w_uv": nrm(ks[4], (L, N_HEADS_A, KV_RANK, HEAD_DIM_A), KV_RANK ** -0.5),
        "w_pool": nrm(ks[5], (L, N_POOL_GROUPS, POOL_GROUP_DIM, POOL_GROUP_DIM), POOL_GROUP_DIM ** -0.5),
        "pool_scale": 1.0 + nrm(ks[6], (L, D_B), 0.02),
        "conv_w": nrm(ks[7], (L, CONV_WIDTH, 1, D_C), CONV_WIDTH ** -0.5),
        "conv_b": nrm(ks[8], (L, D_C), 0.02),
        "conv_ln_g": 1.0 + nrm(ks[9], (L, D_C), 0.02),
        "conv_ln_b": nrm(ks[10], (L, D_C), 0.02),
        "w_o": nrm(ks[11], (L, D_MIX, D_MODEL), BETA * D_MIX ** -0.5),
        "ln1_g": 1.0 + nrm(ks[12], (L, D_MODEL), 0.02),
        "ln1_b": nrm(ks[13], (L, D_MODEL), 0.02),
        "router_w": nrm(ks[14], (D_MODEL, N_EXPERTS), D_MODEL ** -0.5),
        "router_bias": nrm(ks[15], (N_EXPERTS,), 0.01),
        "w_gate": nrm(ks[16], (L, N_EXPERTS, D_MODEL, D_EXPERT), D_MODEL ** -0.5),
        "w_up": nrm(ks[17], (L, N_EXPERTS, D_MODEL, D_EXPERT), D_MODEL ** -0.5),
        "w_down": nrm(ks[18], (L, N_EXPERTS, D_EXPERT, D_MODEL), BETA * D_EXPERT ** -0.5),
        "ln2_g": 1.0 + nrm(ks[19], (L, D_MODEL), 0.02),
        "ln2_b": nrm(ks[20], (L, D_MODEL), 0.02),
    }

def reference(x, w_in, kv_norm_g, w_uk, w_uv, w_pool, pool_scale, conv_w, conv_b, conv_ln_g,
              conv_ln_b, w_o, ln1_g, ln1_b, router_w, router_bias, w_gate, w_up, w_down,
              ln2_g, ln2_b):
    B, S = x.shape[0], x.shape[1]
    for l in range(DEPTH):
        proj = jnp.einsum('bsd,de->bse', x, w_in[l])
        q, c_kv, iq, ik, iw, u_pool, u_conv = jnp.split(proj, SPLIT_POINTS, axis=-1)
        q = q.reshape(B, S, N_HEADS_A, HEAD_DIM_A)
        c_kv = rms_norm(c_kv, kv_norm_g[l])
        iq = iq.reshape(B, S, N_IDX_HEADS, IDX_DIM) * (IDX_DIM ** -0.5)
        iw = iw * (N_IDX_HEADS ** -0.5)
        y_a = dsa_attention(q, c_kv, iq, ik, iw, w_uk[l], w_uv[l])
        y_b = multi_scale_pool(u_pool, w_pool[l], pool_scale[l])
        y_c = conformer_conv(u_conv, conv_w[l], conv_b[l], conv_ln_g[l], conv_ln_b[l])
        mix = jnp.einsum('bse,ed->bsd', jnp.concatenate([y_a, y_b, y_c], axis=-1), w_o[l])
        x = layer_norm(ALPHA * x + mix, ln1_g[l], ln1_b[l])
        ffn = grouped_moe(x, router_w, router_bias, w_gate[l], w_up[l], w_down[l])
        x = layer_norm(ALPHA * x + ffn, ln2_g[l], ln2_b[l])
    return x


_drawn_inputs = setup_inputs


def setup_inputs(seed=0):
    import zlib

    import numpy as np

    out = dict(_drawn_inputs(seed))
    spreads = {}
    factors = {'kv_norm_g': 8.0,
     'pool_scale': 12.993,
     'conv_b': 4.867,
     'conv_ln_g': 15.833,
     'conv_ln_b': 13.565,
     'ln2_g': 8.053,
     'ln2_b': 8.366}
    for name, (base, spread) in spreads.items():
        noise = np.random.default_rng([zlib.crc32(name.encode()), seed]).standard_normal(out[name].shape)
        drawn = base * np.exp(spread * noise) if base else spread * noise
        out[name] = __import__('jax').numpy.asarray(drawn.astype(out[name].dtype))
    for name, factor in factors.items():
        out[name] = (out[name] * factor).astype(out[name].dtype)
    return out
```

```python
from contextlib import ExitStack

import numpy as np
import concourse.bass as bass
from concourse import mybir

F32, F32R, I32, BF16 = mybir.dt.float32, mybir.dt.float32r, mybir.dt.int32, mybir.dt.bfloat16
ALU, ACT, AX = mybir.AluOpType, mybir.ActivationFunctionType, mybir.AxisListType

P = 128
S, D = 1024, 1024
NT, KT = S // P, D // P
HEADS, HD, RANK = 8, 64, 128
IHEADS, IDIM, TOPK = 8, 32, 256
FIRST_TOPK = TOPK // P
TAPS = 31
WINDOWS = (2, 4, 8, 16)
EXPERTS, GROUPS, PER_GROUP, DE = 16, 4, 4, 512
FT = DE // P
ALPHA = 2.0 ** 0.25
EPS = 1e-5
COL_KV, COL_IQ, COL_IK, COL_POOL, COL_CONV = 512, 640, 896, 936, 1192
TILES = 2 * S // P + EXPERTS - 1
SLOTS = (TILES + 1) * P
BIG = 1e30
ROUNDS = 27
PAD_H, PAD_U = TAPS - 1, 16
KB = 1024

HALVES = [(0, 512), (512, 512)]
COLS = ([("kv", COL_KV, HALVES), ("ikw", COL_IK, HALVES)]
        + [(f"iq{i}", COL_IQ + P * i, [(256, 256), (512, 512)]) for i in range(2)]
        + [(f"gate{i}", COL_CONV + 256 + P * i, HALVES) for i in range(2)]
        + [(f"a{i}", COL_CONV + P * i, HALVES) for i in range(2)]
        + [(f"pool{i}", COL_POOL + P * i, HALVES) for i in range(2)]
        + [(f"q{i}", P * i, HALVES) for i in range(4)])
UNITS = []
for _j, (_n, _c, _r) in enumerate(COLS):
    UNITS += [(_n, i, _j) for i in range(len(_r))]
    if _n == "iq1":
        UNITS += [("ms", 0, None), ("ms", 1, None), ("iwT", 0, None), ("iwT", 1, None),
                  ("cT", 0, None), ("cT", 1, None)]
BY_ACT = [n[:2] in ("kv", "ik", "iq", "ga", "po", "ms", "cT") or n[0] == "q" for n, _, _ in UNITS]
BY_DVE = [n[:2] in ("iq", "a0", "a1", "iw") for n, _, _ in UNITS]
MIX_ORDER = [4, 5, 6, 7, 0, 1, 2, 3]
WIDTH = [(b + 1) * P for b in range(NT)]
AT = [sum(WIDTH[:b]) for b in range(NT)]
BLOCKS = [7, 6, 5, 4, 3, 2]
COLUMN = {b: i for i, b in enumerate(BLOCKS)}
COUNT_DVE, COUNT_ACT = [7], [6, 5, 4, 3, 2]
IDX_PER_UNIT, IDX_FROM = 6, 2
IDX = [(b, h) for b in BLOCKS for h in range(IHEADS)]


def attention_steps():
    pairs = [(b, j) for b in range(NT) for j in range(HEADS // 2)]
    steps, ring, r_of = [], [], {}

    def unit(*step, act, dve):
        r_of[step] = len(ring)
        steps.append((*step, len(ring)))
        ring.append((act, dve))

    def scores(p):
        b, j = pairs[p]
        if j == 0 and b >= FIRST_TOPK:
            steps.append(("choose", b))
        if j == 0 and b % 4 == 0:
            for h in range(HEADS):
                unit("ql", b // 4, h, act=True, dve=True)
        for h in range(2):
            steps.append(("qk", b, 2 * j + h))

    for i in range(2):
        for c in range(2):
            unit("pw", i, c, act=True, dve=False)
    scores(0)
    turn = 0
    for p, (b, j) in enumerate(pairs):
        if p + 1 < len(pairs):
            scores(p + 1)
        groups = range(b // 2 + 1)
        for n in groups:
            turn += 1
            unit("pt", b, j, n, act=turn % 2 == 0, dve=turn % 2 == 1)
            if n:
                steps.append(("pv", b, j, n - 1))
        steps.append(("pv", b, j, groups[-1]))
        if j == HEADS // 2 - 1:
            steps.append(("rl_set", b))
            unit("rl", b, act=True, dve=False)
            if b % 2:
                for jj in range(4):
                    unit("uv", b // 2, jj, act=False, dve=True)
        if (b, j) == (NT - 1, 0):
            for c in range(2):
                unit("cm", c, act=False, dve=True)
                steps.append(("csq", c))
            for c in range(2):
                unit("cv", c, act=True, dve=False)
            steps.append(("cn",))
    return steps, [x for x, _ in ring], [x for _, x in ring], r_of


STEPS, RING_ACT, RING_DVE, RING_OF = attention_steps()
RING = {"ql", "pt", "rl", "uv", "pw", "cm", "cv"}
PT = [x for x in STEPS if x[0] == "pt"]
PT_NO = {x[1:4]: i for i, x in enumerate(PT)}


def seen(flags, k):
    return sum(flags[:k + 1])


def program(nc, a):
    ctx = ExitStack()
    with ctx:
        base = 16640

        def at(name, shape, dt, kb):
            return nc.alloc_sbuf_tensor_at(name, shape, dt, offset=base + int(kb * KB))

        def sem(name):
            return ctx.enter_context(nc.semaphore(name))

        CST, CC, SC, R1, R2, R3, END = 0, 13, 29, 47, 80, 116, 204
        ident = at("ident", [P, P], F32, CST)
        ones_rank = at("ones_rank", [P, P], F32, CST + 0.5)
        ones_conv = at("ones_conv", [P, P], F32, CST + 1)
        wuk = at("wuk", [P, HEADS, P], F32, CST + 1.5)
        wuv = at("wuv", [P, HEADS, P], F32, CST + 5.5)
        wpool = at("wpool", [P, 2, P], F32, CST + 9.5)
        par = at("par", [P, 112], F32, CST + 10.5)
        junk_dve = at("junk_dve", [P, S], BF16, CST + 11)
        kvg, pscale, convw = par[:, 0:1], par[:, 1:3], par[:, 3:65]
        convb, cvg, cvb = par[:, 65:67], par[:, 67:69], par[:, 69:71]
        invw, wnd, corr = par[:, 72:74], par[:, 74:76], par[:, 76:108].rearrange("p (i c) -> p i c", i=2)
        cT_hi = at("cT_hi", [P, S], F32R, CC)
        cT_lo = at("cT_lo", [P, S], F32R, CC + 4)
        c_nat = at("c_nat", [P, NT, P], F32, CC + 8)
        cT = at("cT", [P, S], F32, CC + 12)
        rlT = at("rlT", [P, 4, 256], F32, CC + 12)
        bias = at("bias", [P, sum(WIDTH)], F32, SC)
        iqT_hi = at("iqT_hi", [P, 2, 768], F32R, SC)
        iqT_lo = at("iqT_lo", [P, 2, 768], F32R, SC + 6)
        x_tok = at("x_tok", [P, NT, D], F32, R1)
        kvT = at("kvT", [P, S], F32, R1)
        sq = at("sq", [P, S], F32, R1 + 4)
        rstd_kv = at("rstd_kv", [P, S], F32, R1 + 8)
        iT = at("iT", [P, S], F32, R1 + 12)
        ikT_hi = at("ikT_hi", [P, S], F32R, R1 + 16.25)
        ikT_lo = at("ikT_lo", [P, S], F32R, R1 + 20.25)
        uT = at("uT", [P, 2, PAD_U + S], F32, R1)
        sums = at("sums", [P, 2, PAD_U + S], F32, R1 + 8.125)
        sig = at("sig", [P, 2, S], F32, R1 + 8.125)
        hpad = at("hpad", [P, 2, 1056], F32, R1 + 16.25)
        conv = at("conv", [P, 2, S], F32, R1 + 24.5)
        csq = at("csq", [P, 2, S], F32, R2 + 16)
        crstd = at("crstd", [P, S], F32, R2 + 24)
        probs = at("probs", [P, 4, S], F32, R1)
        stack_iq = at("stack_iq", [P, IHEADS, 768], F32R, R2)
        stack_ik = at("stack_ik", [P, S], F32R, R2 + 24)
        relu = at("relu", [P, 2, S], F32, R2 + 28)
        tapped = at("tapped", [P, S], F32, R2 + 32)
        above = at("above", [P, S], F32, R2 + 16)
        tied = at("tied", [P, S], F32, R2 + 20)
        tie_no = at("tie_no", [P, S], F32, R2 + 24)
        qT = at("qT", [P, 4, S], F32, R2)
        wuk_raw = at("wuk_raw", [P, HEADS, HD], F32, R2)
        doubled = [at(f"doubled{i}", [P, PAD_U + S], F32, R2 + 16 + 4.25 * i) for i in range(2)]
        xT_hi = at("xT_hi", [P, KT, S], F32R, R3)
        xT_lo = at("xT_lo", [P, KT, S], F32R, R3 + 32)
        w_raw = at("w_raw", [P, 2, KT, P], F32, R3 + 64)
        w_hi = at("w_hi", [P, 2, KT, P], F32R, R3 + 72)
        w_lo = at("w_lo", [P, 2, KT, P], F32R, R3 + 80)
        ql_hi = at("ql_hi", [P, HEADS, 512], F32R, R3)
        ql_lo = at("ql_lo", [P, HEADS, 512], F32R, R3 + 16)
        mix = at("mix", [P, KT, S], F32, R3 + 32)
        olat = at("olat", [P, 2, HEADS, 256], F32, R3 + 64)
        pT = at("pT", [P, 2, 512], F32, R3 + 80)
        rlrep = at("rlrep", [P, HEADS, HD], F32, R3 + 84)
        mix_hi = at("mix_hi", [P, KT, S], F32R, R1)
        mix_lo = at("mix_lo", [P, KT, S], F32R, 96)
        wo_hi = [at("wo_hi0", [P, KT, 512], F32R, 128), at("wo_hi1", [P, KT, 512], F32R, 148)]
        wo_lo = [at("wo_lo0", [P, KT, 512], F32R, 180), at("wo_lo1", [P, KT, 512], F32R, 164)]
        wo_raw = at("wo_raw", [P, 4, 512], F32, SC)
        x_res = at("x_res", [P, 4, 512], F32, SC + 8)
        ln_g = at("ln_g", [P, D], F32, R3 + 80)
        ln_b = at("ln_b", [P, D], F32, R3 + 84)
        xa = at("xa", [P, 4, D], F32, CC)
        xb = at("xb", [P, 4, D], F32, R2)
        x1T = at("x1T", [P, KT, S], F32, R3)
        raw = at("raw", [P, 6, 4 * DE], F32, SC)
        whi = at("whi", [P, 6, 4 * DE], F32R, 96)
        wlo = at("wlo", [P, 6, 4 * DE], F32R, 144)
        xg = at("xg", [P, D], F32, 192)
        xgT_hi = at("xgT_hi", [P, KT, P], F32R, 196)
        xgT_lo = at("xgT_lo", [P, KT, P], F32R, 200)
        silu = at("silu", [P, DE], F32, CST + 0.5)
        hid = at("hid", [P, DE], F32, CST + 2.5)
        hT_hi = at("hT_hi", [P, FT, P], F32R, CST + 4.5)
        hT_lo = at("hT_lo", [P, FT, P], F32R, CST + 6.5)
        ysb = at("ysb", [P, D], F32, CST + 8.5)
        ya = at("ya", [P, 2, D], F32, 96)
        yb = at("yb", [P, 2, D], F32, 104)
        ln2_g = at("ln2_g", [P, D], F32, 112)
        ln2_b = at("ln2_b", [P, D], F32, 116)
        junk_act = at("junk_act", [P, S], BF16, END)
        sm = at("sm", [P, 432], F32, END + 2)
        iw = sm[:, 0:64].rearrange("p (t h) -> p t h", t=NT)
        lo, hi, cand, res, thr, below = (sm[:, 64 + 6 * i:70 + 6 * i] for i in range(6))
        need = sm[:, 100:106]
        negmax = sm[:, 106:170]
        rowsum = sm[:, 170:234]
        stats = sm[:, 234:246].rearrange("p (c s) -> p c s", c=2)
        mv = sm[:, 246:248]
        rstd = sm[:, 248:249]
        eps = sm[:, 249:250]
        gate = sm[:, 250:266].rearrange("p (t k) -> p t k", t=NT)
        m32 = at("m32", [P, 12], I32, END + 3.6875)
        passed, failed = m32[:, 0:6], m32[:, 6:12]

        RT = SC
        rt = at("rt", [P, 1536], F32, RT)
        rbias, aff, score = rt[:, 0:16], rt[:, 16:144], rt[:, 144:272]
        pairs = rt[:, 272:464].rearrange("p (n c) -> p n c", c=6)
        gs, gv, first_g = rt[:, 464:496], rt[:, 496:528], rt[:, 528:560]
        gm = rt[:, 560:568]
        w4, w16 = rt[:, 568:572], rt[:, 572:588]
        masked, pick, oh1, oh2 = (rt[:, 588 + 128 * i:716 + 128 * i] for i in range(4))
        top = rt[:, 1100:1108]
        ga, gb, gsum = rt[:, 1108:1116], rt[:, 1116:1124], rt[:, 1124:1132]
        slotf = rt[:, 1132:1148]
        rw = at("rw", [P, KT, EXPERTS], F32, RT + 6)
        lgT = at("lgT", [EXPERTS, S], F32, RT + 7)
        mT = at("mT", [EXPERTS, S], F32, RT + 11)
        rank = at("rank", [EXPERTS, S], F32, RT + 15)
        rk = at("rk", [P, 96], F32, RT + 19)
        ones_row = at("ones_row", [EXPERTS, S], F32, RT + 20)
        thr8, upper, tcol = rk[0:16, 0:8], rk[0:16, 8:24], rk[0:16, 24:56]
        ntile, cum, slot0, cmp = rk[0:16, 56:57], rk[0:16, 57:58], rk[0:16, 58:59], rk[0:16, 64:96]
        ones16 = rk[0:16, 59:60]
        ri = at("ri", [P, 88], I32, CST + 12.5)
        slot_i, where_i = ri[:, 0:16], ri[:, 16:32]
        tokid, expert_of, tmp_i = ri[:, 32:40], ri[0:1, 40:72], ri[:, 72:88]
        idx_all = at("idx_all", [P, TILES + 1], I32, END)
        idx_now = at("idx_now", [P, 1], I32, END + 0.25)
        zero_i = at("zero_i", [P, TILES + 1], I32, END + 0.5)


        ps = ctx.enter_context(nc.psum_tensor("ps", [P, 8, 512], F32))

        def pair(i):
            return ps[:, 2 * i:2 * i + 2, :].rearrange("p b n -> p (b n)")

        x1_d = nc.dram_tensor("x1_d", (S, D), F32, kind="Internal").ap()
        slots_d = nc.dram_tensor("slots_d", (SLOTS, 1), I32, kind="Internal").ap()
        y_d = nc.dram_tensor("y_d", (TILES * P, D), F32, kind="Internal").ap()

        par_in, wuk_in, wuv_in, wpool_in = sem("par_in"), sem("wuk_in"), sem("wuv_in"), sem("wpool_in")
        x_in = [sem(f"x_in{i}") for i in range(NT)]
        w_in_s = [sem(f"w_in{i}") for i in range(2)]
        ident_set, zeros_set, dve_set = sem("ident_set"), sem("zeros_set"), sem("dve_set")
        x_tr, x_hi, x_lo, w_hi_s, w_lo_s = (sem(n) for n in ("x_tr", "x_hi", "x_lo", "w_hi_s", "w_lo_s"))
        wuk_tr, wuk_set = sem("wuk_tr"), sem("wuk_set")
        unit_mm, unit_act, unit_dve = sem("unit_mm"), sem("unit_act"), sem("unit_dve")
        kv_sq, kv_sd, kv_norm, c_hi, c_lo = (sem(n) for n in ("kv_sq", "kv_sd", "kv_norm", "c_hi", "c_lo"))
        ik_hi, ik_lo, stack_in = sem("ik_hi"), sem("ik_lo"), sem("stack_in")
        idx_mm, idx_relu, idx_sum = sem("idx_mm"), sem("idx_relu"), sem("idx_sum")
        bound, masked_s, cand_set = sem("bound"), sem("masked_s"), sem("cand_set")
        counted_dve, counted_act, dve_chain = sem("counted_dve"), sem("counted_act"), sem("dve_chain")
        tri_set, pads_set = sem("tri_set"), sem("pads_set")
        conv0, conv1, conv1_mul, pooled = sem("conv0"), sem("conv1"), sem("conv1_mul"), sem("pooled")
        ring_mm, ring_act, ring_dve = sem("ring_mm"), sem("ring_act"), sem("ring_dve")
        qk_mm, masked_max, exped, rl_set = sem("qk_mm"), sem("masked_max"), sem("exped"), sem("rl_set")
        pv_mm, olat_set = sem("pv_mm"), sem("olat_set")
        conv_c, conv_sq, conv_n, conv_y = (sem(n) for n in ("conv_c", "conv_sq", "conv_n", "conv_y"))
        mix_hi_s, mix_lo_s = sem("mix_hi_s"), sem("mix_lo_s")
        wo_in = [sem(f"wo_in{i}") for i in range(4)]
        xr_in = [sem(f"xr_in{i}") for i in range(4)]
        ln_in, wo_hi_s, wo_lo_s, wo_mm = sem("ln_in"), sem("wo_hi_s"), sem("wo_lo_s"), sem("wo_mm")
        y1_set, stat, ln_sd, ln_scaled, x1_set = (sem(n) for n in ("y1_set", "stat", "ln_sd", "ln_scaled", "x1_set"))
        x1_tr, x1T_set, x1_out = sem("x1_tr"), sem("x1T_set"), sem("x1_out")
        route_in, lg_mm, lgT_set, lg_tr, aff_set = (sem(n) for n in ("route_in", "lg_mm", "lgT_set", "lg_tr", "aff_set"))
        routed, oh_set, m_tr, mT_set, ntile_set = (sem(n) for n in ("routed", "oh_set", "m_tr", "mT_set", "ntile_set"))
        cum_mm, slotT_set, cmp_set, te_mm, s_tr = (sem(n) for n in ("cum_mm", "slotT_set", "cmp_set", "te_mm", "s_tr"))
        experts_set, places_set, rconst = sem("experts_set"), sem("places_set"), sem("rconst")
        table_set, idx0_set = sem("table_set"), sem("idx0_set")
        table_zero, scattered, table_in = sem("table_zero"), sem("scattered"), sem("table_in")
        raw_in = [sem(f"raw_in{i}") for i in range(6)]
        idx_set, xg_in, xg_tr, xgT_hi_s, xgT_lo_s = (sem(n) for n in ("idx_set", "xg_in", "xg_tr", "xgT_hi_s", "xgT_lo_s"))
        gu_hi, gu_lo, dn_hi, dn_lo = (sem(n) for n in ("gu_hi", "gu_lo", "dn_hi", "dn_lo"))
        gu_used, dn_used = sem("gu_used"), sem("dn_used")
        silu_set, hid_set, h_tr, hT_hi_s, hT_lo_s = (sem(n) for n in ("silu_set", "hid_set", "h_tr", "hT_hi_s", "hT_lo_s"))
        y_set, y_out = sem("y_set"), sem("y_out")
        ya_in = [sem(f"ya_in{i}") for i in range(2)]
        yb_in = [sem(f"yb_in{i}") for i in range(2)]
        ln2_in, yb_set, summed, fin_done, out_done = (sem(n) for n in ("ln2_in", "yb_set", "summed", "fin_done", "out_done"))

        def f32(t):
            return t.bitcast(F32)

        def three(pe, out, l_hi, l_lo, r_hi, r_lo, start, stop):
            pe.matmul(out, l_hi, r_hi, start=start, stop=False)
            pe.matmul(out, l_hi, r_lo, start=False, stop=False)
            return pe.matmul(out, l_lo, r_hi, start=False, stop=stop)

        def x1_tile(t):
            return xa[:, t, :] if t < 4 else xb[:, t - 4, :]

        N_UNITS = len(UNITS)
        LATER = [k for k, u in enumerate(UNITS) if u[0] == "gate0"][0]

        def plan():
            u = 0
            for k in range(N_UNITS):
                yield "unit", k
                if k >= LATER + IDX_FROM - 1:
                    for _ in range(IDX_PER_UNIT):
                        if u < len(IDX):
                            yield "idx", u
                            u += 1
        PLAN = list(plan())
        LAST_IDX = max(i for i, p in enumerate(PLAN) if p[0] == "idx")

        block = ctx.enter_context(nc.Block())

        @block.sync
        def _(sp):
            def w_tile(j):
                if j >= 2:
                    sp.wait_ge(w_lo_s, j - 1)
                c = COLS[j][1]
                sp.dma_start(w_raw[:, j % 2], a["w_in"][0].rearrange("(k p) n -> p k n", p=P)[:, :, c:c + P]
                             ).then_inc(w_in_s[j % 2], 16)

            for t in range(NT):
                sp.dma_start(x_tok[:, t], a["x"][0, t * P:(t + 1) * P, :]).then_inc(x_in[t], 16)
                if t in (3, 7):
                    w_tile(t // 4)
            for j in range(2, 6):
                w_tile(j)
            sp.wait_ge(unit_dve, seen(BY_DVE, UNITS.index(("iq1", 1, 3))))
            sp.wait_ge(ik_lo, 1)
            for part in range(4):
                rows = slice(part * IDIM, (part + 1) * IDIM)
                src = iqT_hi if part < 2 else iqT_lo
                for h4 in range(4):
                    sp.dma_start(f32(stack_iq[rows]).rearrange("p (i h) n -> p i h n", i=2)[:, :, h4, :],
                                 f32(src[h4 * IDIM:(h4 + 1) * IDIM, :, :])).then_inc(stack_in, 16)
                sp.dma_start(f32(stack_ik[rows, :]), f32((ikT_lo if part % 2 else ikT_hi)[0:IDIM, :])
                             ).then_inc(stack_in, 16)
            for j in range(6, len(COLS)):
                w_tile(j)
            sp.wait_ge(masked_max, NT * HEADS)
            for hf in range(2):
                for k in range(KT):
                    n = hf * KT + k
                    if n >= 4:
                        sp.wait_ge(wo_lo_s, n - 3)
                    kk = MIX_ORDER[k]
                    sp.dma_start(wo_raw[:, n % 4], a["w_o"][0, kk * P:(kk + 1) * P, hf * 512:(hf + 1) * 512]
                                 ).then_inc(wo_in[n % 4], 16)
            for hf in range(2):
                for t in range(NT):
                    n = hf * NT + t
                    if n >= 4:
                        sp.wait_ge(y1_set, n - 3)
                    sp.dma_start(x_res[:, n % 4], a["x"][0, t * P:(t + 1) * P, hf * 512:(hf + 1) * 512]
                                 ).then_inc(xr_in[n % 4], 16)
            sp.wait_ge(wo_mm, 2 * NT)
            sp.wait_ge(y1_set, 2 * NT)
            sp.dma_start(rbias, a["router_bias"].partition_broadcast(P)).then_inc(route_in, 16)
            sp.dma_start(rw[:], a["router_w"].rearrange("(k p) e -> p k e", p=P)).then_inc(route_in, 16)
            for t in range(NT):
                sp.wait_ge(x1_set, t + 1)
                sp.dma_start(x1_d[t * P:(t + 1) * P, :], x1_tile(t)).then_inc(x1_out, 16)
            sp.wait_ge(experts_set, 1)
            sp.wait_ge(places_set, 2)

            def gate_up(t, first):
                e = sp.value_load(expert_of[0:1, bass.ds(t, 1)], min_val=0, max_val=EXPERTS - 1)
                for n, (w, half) in enumerate((("w_gate", 0), ("w_up", 0), ("w_gate", 1), ("w_up", 1))):
                    if not first:
                        sp.wait_ge(gu_lo, t * 4 + (n - 3))
                    src = a[w][0].rearrange("e (p k) n -> e p (k n)", p=P)[
                        bass.ds(e, 1), :, half * 4 * DE:(half + 1) * 4 * DE]
                    sp.dma_start(raw[:, n, :], src.rearrange("e p n -> (e p) n")).then_inc(raw_in[n], 16)

            def down(t, first):
                e = sp.value_load(expert_of[0:1, bass.ds(t, 1)], min_val=0, max_val=EXPERTS - 1)
                for n in range(2):
                    if not first:
                        sp.wait_ge(dn_lo, t * 2 + (n - 1))
                    src = a["w_down"][0].rearrange("e (p k) n -> e p (k n)", p=P)[
                        bass.ds(e, 1), :, n * 4 * DE:(n + 1) * 4 * DE]
                    sp.dma_start(raw[:, 4 + n, :], src.rearrange("e p n -> (e p) n")).then_inc(raw_in[4 + n], 16)

            gate_up(0, True)
            gate_up(1, False)
            down(0, True)
            with sp.Fori(2, TILES) as t:
                gate_up(t, False)
                down(t - 1, False)
            down(TILES - 1, False)
            sp.wait_ge(y_set, TILES)
            sp.dma_start(ln2_g[:], a["ln2_g"][0].partition_broadcast(P)).then_inc(ln2_in, 16)
            sp.dma_start(ln2_b[:], a["ln2_b"][0].partition_broadcast(P)).then_inc(ln2_in, 16)
            for t in range(NT):
                sp.wait_ge(fin_done, t + 1)
                sp.dma_start(a["out"][0, t * P:(t + 1) * P, :], x1_tile(t)).then_inc(out_done, 16)
            sp.wait_ge(out_done, 16 * NT)

        @block.tensor
        def _(pe):
            pe.wait_ge(ident_set, 2)
            for g in range(2 * NT):
                t, half = divmod(g, 2)
                if half == 0:
                    pe.wait_ge(x_in[t], 16)
                if g >= 4:
                    pe.wait_ge(x_lo, g - 3)
                for k in range(4):
                    kk = half * 4 + k
                    last = pe.transpose(ps[:, g % 4, k * P:(k + 1) * P], x_tok[:, t, kk * P:(kk + 1) * P], ident[:])
                last.then_inc(x_tr, 1)
            pe.wait_ge(wuk_in, 16)
            pe.wait_ge(x_lo, 2 * NT)
            for j in range(4):
                last = pe.transpose(ps[:, 0, j * P:(j + 1) * P],
                                    wuk_raw[:, 2 * j:2 * j + 2, :].rearrange("p h d -> p (h d)"), ident[:])
            last.then_inc(wuk_tr, 1)
            pe.wait_ge(dve_set, 1)

            def bank_free(k):
                if k >= 4:
                    if seen(BY_ACT, k - 4):
                        pe.wait_ge(unit_act, seen(BY_ACT, k - 4))
                    if seen(BY_DVE, k - 4):
                        pe.wait_ge(unit_dve, seen(BY_DVE, k - 4))

            def unit(k):
                name, i, j = UNITS[k]
                out = ps[:, 4 + k % 4, :]
                bank_free(k)
                if j is not None:
                    t0, n = COLS[j][2][i]
                    pe.wait_ge(w_lo_s, j + 1)
                    for kk in range(KT):
                        last = three(pe, out[:, 0:n], w_hi[:, j % 2, kk, :], w_lo[:, j % 2, kk, :],
                                     xT_hi[:, kk, t0:t0 + n], xT_lo[:, kk, t0:t0 + n], kk == 0, kk == KT - 1)
                elif name == "ms":
                    pe.wait_ge(kv_sq, 2)
                    last = pe.matmul(out, ones_rank[:], sq[:, i * 512:(i + 1) * 512], start=True, stop=True)
                elif name == "cT":
                    pe.wait_ge(kv_norm, 2 + 2)
                    for t in range(4):
                        c = (4 * i + t) * P
                        last = pe.transpose(out[:, t * P:(t + 1) * P], cT[:, c:c + P], ident[:])
                elif name == "iwT":
                    for t in range(4):
                        c = (4 * i + t) * P
                        last = pe.transpose(out[:, t * P:(t + 1) * P], iT[:, c:c + P], ident[:])
                last.then_inc(unit_mm, 1)

            def index(u):
                b, h = IDX[u]
                if u == 0:
                    pe.wait_ge(stack_in, 16 * 20)
                    pe.wait_ge(wuk_set, 8)
                if u >= 2:
                    pe.wait_ge(idx_relu, u - 1)
                for c in range(0, WIDTH[b], 512):
                    n = min(512, WIDTH[b] - c)
                    last = pe.matmul(pair(u % 2)[:, c:c + n], stack_iq[:, h, (b - 2) * P:(b - 1) * P],
                                     stack_ik[:, c:c + n], start=True, stop=True)
                last.then_inc(idx_mm, 1)

            for what, n in PLAN:
                (unit if what == "unit" else index)(n)

            pe.wait_ge(unit_act, sum(BY_ACT))
            pe.wait_ge(unit_dve, sum(BY_DVE))
            pe.wait_ge(idx_relu, len(IDX))
            for step in STEPS:
                kind = step[0]
                if kind in RING:
                    r = step[-1]
                    out = ps[:, 4 + r % 3, :]
                    if r >= 3:
                        if seen(RING_ACT, r - 3):
                            pe.wait_ge(ring_act, seen(RING_ACT, r - 3))
                        if seen(RING_DVE, r - 3):
                            pe.wait_ge(ring_dve, seen(RING_DVE, r - 3))
                if kind == "ql":
                    _, half, h, r = step
                    pe.matmul(out, wuk[:, h, :], qT[:, h // 2, half * 512:(half + 1) * 512],
                              start=True, stop=True).then_inc(ring_mm, 1)
                elif kind == "qk":
                    _, b, h = step
                    u = b * HEADS + h
                    if u >= 2:
                        pe.wait_ge(masked_max, u - 1)
                    pe.wait_ge(ring_dve, seen(RING_DVE, RING_OF["ql", b // 4, h]))
                    q0 = (b % 4) * P
                    for c in range(0, WIDTH[b], 512):
                        n = min(512, WIDTH[b] - c)
                        last = three(pe, pair(u % 2)[:, c:c + n], ql_hi[:, h, q0:q0 + P], ql_lo[:, h, q0:q0 + P],
                                     cT_hi[:, c:c + n], cT_lo[:, c:c + n], True, True)
                    last.then_inc(qk_mm, 1)
                elif kind == "pt":
                    _, b, j, n, r = step
                    pe.wait_ge(exped, b * HEADS + 2 * j + 2)
                    for k in range(2 * n, min(2 * n + 2, b + 1)):
                        for h in range(2):
                            c = (k - 2 * n) * 256 + h * P
                            last = pe.transpose(out[:, c:c + P],
                                                probs[:, (2 * j + h) % 4, k * P:(k + 1) * P], ident[:])
                    last.then_inc(ring_mm, 1)
                elif kind == "pv":
                    _, b, j, n = step
                    acc = ps[:, 7, 0:256]
                    if n == 0 and b * 4 + j:
                        pe.wait_ge(olat_set, b * 4 + j)
                    r = RING_OF["pt", b, j, n]
                    if RING_ACT[r]:
                        pe.wait_ge(ring_act, seen(RING_ACT, r))
                    else:
                        pe.wait_ge(ring_dve, seen(RING_DVE, r))
                    for k in range(2 * n, min(2 * n + 2, b + 1)):
                        c = (k - 2 * n) * 256
                        last = pe.matmul(acc, c_nat[:, k, :], pT[:, PT_NO[b, j, n] % 2, c:c + 256],
                                         start=k == 0, stop=k == b)
                    last.then_inc(pv_mm, 1)
                elif kind == "rl":
                    _, b, r = step
                    pe.wait_ge(rl_set, b + 1)
                    for j in range(4):
                        last = pe.transpose(out[:, j * P:(j + 1) * P],
                                            rlrep[:, 2 * j:2 * j + 2, :].rearrange("p h d -> p (h d)"), ident[:])
                    last.then_inc(ring_mm, 1)
                elif kind == "uv":
                    _, q, j, r = step
                    if j == 0:
                        pe.wait_ge(olat_set, 4 * (2 * q + 2))
                        pe.wait_ge(wuv_in, 32)
                    for h in range(2):
                        last = pe.matmul(out[:, 0:256], wuv[:, 2 * j + h, :], olat[:, q % 2, 2 * j + h, :],
                                         start=h == 0, stop=h == 1)
                    last.then_inc(ring_mm, 1)
                elif kind == "pw":
                    _, i, c, r = step
                    pe.wait_ge(pooled, 4)
                    pe.wait_ge(wpool_in, 32)
                    pe.matmul(out, wpool[:, i, :], sums[:, i, PAD_U + c * 512:PAD_U + (c + 1) * 512],
                              start=True, stop=True).then_inc(ring_mm, 1)
                elif kind in ("cm", "cv"):
                    _, c, r = step
                    if kind == "cm":
                        pe.wait_ge(conv0, TAPS)
                        pe.wait_ge(conv1, TAPS)
                    else:
                        pe.wait_ge(conv_sq, 2 * c + 2)
                    src = conv if kind == "cm" else csq
                    for i in range(2):
                        last = pe.matmul(out, ones_conv[:], src[:, i, c * 512:(c + 1) * 512], start=i == 0, stop=i == 1)
                    last.then_inc(ring_mm, 1)

            pe.wait_ge(olat_set, 4 * NT)
            pe.wait_ge(ring_act, sum(RING_ACT))
            pe.wait_ge(ring_dve, sum(RING_DVE))
            for n in range(2 * NT):
                hf, t = divmod(n, NT)
                if n >= 8:
                    pe.wait_ge(y1_set, n - 7)
                for i, k in enumerate(MIX_ORDER):
                    if t == 0:
                        pe.wait_ge(wo_lo_s, hf * KT + i + 1)
                        if hf == 0:
                            pe.wait_ge(mix_lo_s, i + 1)
                    last = three(pe, ps[:, n % 8, :], mix_hi[:, k, t * P:(t + 1) * P], mix_lo[:, k, t * P:(t + 1) * P],
                                 wo_hi[hf][:, k, :], wo_lo[hf][:, k, :], i == 0, i == KT - 1)
                last.then_inc(wo_mm, 1)

            pe.wait_ge(y1_set, NT + 4)
            for g in range(2 * NT):
                t, half = divmod(g, 2)
                if half == 0:
                    pe.wait_ge(x1_set, t + 1)
                if g >= 4:
                    pe.wait_ge(x1T_set, g - 3)
                for k in range(4):
                    kk = half * 4 + k
                    last = pe.transpose(ps[:, g % 4, k * P:(k + 1) * P], x1_tile(t)[:, kk * P:(kk + 1) * P], ident[:])
                last.then_inc(x1_tr, 1)
            pe.wait_ge(route_in, 32)
            pe.wait_ge(y1_set, 2 * NT)
            for c in range(2):
                pe.wait_ge(x1T_set, 8 * (c + 1))
                for k in range(KT):
                    last = pe.matmul(ps[0:EXPERTS, 4 + c, :], rw[:, k, :], x1T[:, k, c * 512:(c + 1) * 512],
                                     start=k == 0, stop=k == KT - 1)
                last.then_inc(lg_mm, 1)
            pe.wait_ge(lgT_set, 2)
            for t in range(NT):
                last = pe.transpose(ps[:, 6, t * 16:(t + 1) * 16], lgT[:, t * P:(t + 1) * P], ident[0:16, 0:16])
            last.then_inc(lg_tr, 1)
            pe.wait_ge(oh_set, 1)
            for t in range(NT):
                last = pe.transpose(pair(0)[0:16, t * P:(t + 1) * P], pick[:, t * 16:(t + 1) * 16], ident[:])
            last.then_inc(m_tr, 1)
            pe.wait_ge(ntile_set, 1)
            pe.wait_ge(rconst, 4)
            pe.matmul(ps[0:16, 4, 0:1], upper, ntile, start=True, stop=True).then_inc(cum_mm, 1)
            pe.wait_ge(cmp_set, 1)
            pe.matmul(ps[0:1, 5, 0:TILES + 1], ones16, cmp, start=True, stop=True).then_inc(te_mm, 1)
            pe.wait_ge(slotT_set, 1)
            for t in range(NT):
                last = pe.transpose(ps[:, 7, t * 16:(t + 1) * 16], rank[:, t * P:(t + 1) * P], ident[0:16, 0:16])
            last.then_inc(s_tr, 1)

            def xgT(t):
                pe.wait_ge(xg_in, t * 16 + 16)
                for k in range(KT):
                    last = pe.transpose(pair(2)[:, k * P:(k + 1) * P], xg[:, k::KT], ident[:])
                last.then_inc(xg_tr, 1)

            def gate_up(t):
                pe.wait_ge(xgT_lo_s, t + 1)
                for n in range(4):
                    out = ps[:, n % 2, :]
                    pe.wait_ge(gu_lo, t * 4 + (n + 1))
                    for k in range(4):
                        kk = 4 * (n // 2) + k
                        last = three(pe, out, xgT_hi[:, kk, :], xgT_lo[:, kk, :], whi[:, n, k * DE:(k + 1) * DE],
                                     wlo[:, n, k * DE:(k + 1) * DE], kk == 0, kk == KT - 1)
                    last.then_inc(gu_used, 1)

            def down(t):
                pe.wait_ge(hT_lo_s, t + 1)
                if not (isinstance(t, int) and t == 0):
                    pe.wait_ge(y_set, t)
                for n in range(2):
                    pe.wait_ge(dn_lo, t * 2 + (n + 1))
                    for k in range(2):
                        for c in range(2):
                            col = k * D + c * 512
                            ft = 2 * n + k
                            last = three(pe, pair(1)[:, c * 512:(c + 1) * 512], hT_hi[:, ft, :], hT_lo[:, ft, :],
                                         whi[:, 4 + n, col:col + 512], wlo[:, 4 + n, col:col + 512],
                                         ft == 0, ft == FT - 1)
                    last.then_inc(dn_used, 1)

            def hidT(t):
                pe.wait_ge(hid_set, t + 1)
                for f in range(FT):
                    last = pe.transpose(ps[:, 6, f * P:(f + 1) * P], hid[:, f::FT], ident[:])
                last.then_inc(h_tr, 1)

            pe.wait_ge(places_set, 2)
            xgT(0)
            gate_up(0)
            xgT(1)
            hidT(0)

            def tile(t):
                gate_up(t)
                xgT(t + 1)
                down(t - 1)
                hidT(t)

            tile(1)
            with pe.Fori(2, TILES) as t:
                tile(t)
            down(TILES - 1)

        @block.scalar
        def _(act):
            with nc.allow_non_contiguous_dma(reason="small parameters, one element to a partition"):
                act.dma_start(kvg, a["kv_norm_g"][0].rearrange("(p o) -> p o", o=1)).then_inc(par_in, 16)
                act.dma_start(pscale, a["pool_scale"][0].rearrange("(i p) -> p i", p=P)).then_inc(par_in, 16)
                for i in range(2):
                    act.dma_start(convw[:, i * TAPS:(i + 1) * TAPS],
                                  a["conv_w"][0, :, 0, i * P:(i + 1) * P].rearrange("w p -> p w")).then_inc(par_in, 16)
                act.dma_start(convb, a["conv_b"][0].rearrange("(i p) -> p i", p=P)).then_inc(par_in, 16)
                act.dma_start(cvg, a["conv_ln_g"][0].rearrange("(i p) -> p i", p=P)).then_inc(par_in, 16)
                act.dma_start(cvb, a["conv_ln_b"][0].rearrange("(i p) -> p i", p=P)).then_inc(par_in, 16)
            act.dma_start(wuk_raw[:], a["w_uk"][0].rearrange("h r d -> r h d")).then_inc(wuk_in, 16)
            act.wait_ge(zeros_set, 2)
            for h in range(2):
                act.dma_start(wuv[:, h::2, h * HD:(h + 1) * HD], a["w_uv"][0, h::2].rearrange("h r d -> r h d")
                              ).then_inc(wuv_in, 16)
                act.dma_start(wpool[h * HD:(h + 1) * HD, :, h * HD:(h + 1) * HD],
                              a["w_pool"][0, h::2].rearrange("g c d -> c g d")).then_inc(wpool_in, 16)

            def w_split(j):
                act.wait_ge(w_in_s[j % 2], 16 * (j // 2 + 1))
                if j >= 2:
                    act.wait_ge(unit_mm, max(k for k, u in enumerate(UNITS) if u[2] == j - 2) + 1)
                act.copy(w_hi[:, j % 2], w_raw[:, j % 2]).then_inc(w_hi_s, 1)

            w_split(0)
            for g in range(2 * NT):
                t, half = divmod(g, 2)
                act.wait_ge(x_tr, g + 1)
                act.copy(xT_hi[:, half * 4:half * 4 + 4, t * P:(t + 1) * P],
                         ps[:, g % 4, :].rearrange("p (k n) -> p k n", k=4)).then_inc(x_hi, 1)

            def unit(k):
                name, i, j = UNITS[k]
                if not BY_ACT[k]:
                    return
                src = ps[:, 4 + k % 4, :]
                act.wait_ge(unit_mm, k + 1)
                t0, n = COLS[j][2][i] if j is not None else (i * 512, 512)
                tok = slice(t0, t0 + n)
                if name == "kv":
                    if i == 0:
                        act.wait_ge(x_tr, 2 * NT)
                    act.activation(sq[:, tok], src, ACT.Square).then_inc(kv_sq, 1)
                    act.copy(kvT[:, tok], src).then_inc(unit_act, 1)
                elif name == "ikw":
                    act.copy(iT[:, tok], src).then_inc(unit_act, 1)
                    if i == 1:
                        act.wait_ge(unit_act, seen(BY_ACT, k))
                        act.copy(ikT_hi[0:IDIM, :], iT[0:IDIM, :]).then_inc(ik_hi, 1)
                elif name[:2] == "iq":
                    act.copy(iqT_hi[:, int(name[2]), t0 - 256:t0 - 256 + n], src[:, 0:n]).then_inc(unit_act, 1)
                elif name == "ms":
                    act.activation(rstd_kv[:, tok], src, ACT.Sqrt, bias=eps).then_inc(unit_act, 1)
                elif name == "cT":
                    act.copy(c_nat[:, 4 * i:4 * i + 4, :].rearrange("p t r -> p (t r)"), src).then_inc(unit_act, 1)
                    if i == 1:
                        act.copy(cT_hi[:], cT[:]).then_inc(c_hi, 1)
                elif name[:4] == "gate":
                    if name == "gate0" and i == 0:
                        act.wait_ge(kv_norm, 4)
                        act.wait_ge(unit_mm, UNITS.index(("iwT", 1, None)) + 1)
                        act.wait_ge(ik_lo, 1)
                    act.activation(sig[:, int(name[4]), tok], src, ACT.Sigmoid).then_inc(unit_act, 1)
                elif name[:4] == "pool":
                    if name == "pool0" and i == 0:
                        act.wait_ge(c_hi, 1)
                        act.wait_ge(c_lo, 1)
                    act.copy(uT[:, int(name[4]), PAD_U + t0:PAD_U + t0 + n], src).then_inc(unit_act, 1)
                elif name[0] == "q":
                    act.copy(qT[:, int(name[1]), tok], src).then_inc(unit_act, 1)

            def index(u):
                b, h = IDX[u]
                act.wait_ge(idx_mm, u + 1)
                if u >= 2:
                    act.wait_ge(idx_sum, u - 1)
                act.activation(relu[:, u % 2, 0:WIDTH[b]], pair(u % 2)[:, 0:WIDTH[b]], ACT.Relu).then_inc(idx_relu, 1)

            def item(what, n):
                if what == "idx":
                    index(n)
                else:
                    j = UNITS[n][2]
                    if j is not None and UNITS[n][1] == 0 and j + 1 < len(COLS):
                        w_split(j + 1)
                    unit(n)

            for p in PLAN[:LAST_IDX + 1]:
                item(*p)
            rest = PLAN[LAST_IDX + 1:]

            def count(r):
                act.wait_ge(cand_set, r + 1)
                for i, b in enumerate(COUNT_ACT):
                    c = COLUMN[b]
                    if r + i:
                        act.wait_ge(counted_act, len(COUNT_ACT) * r + i)
                    act.activation(junk_act[:, 0:WIDTH[b]], bias[:, AT[b]:AT[b] + WIDTH[b]], ACT.Sign,
                                   bias=cand[:, c:c + 1], scale=-1.0, accum_out=res[:, c:c + 1]
                                   ).then_inc(counted_act, 1)

            act.wait_ge(masked_s, len(BLOCKS))
            act.wait_ge(table_zero, 16)
            for r in range(ROUNDS):
                count(r)
                if rest:
                    item(*rest.pop(0))
            for p in rest:
                item(*p)

            for step in STEPS:
                kind = step[0]
                if kind in RING:
                    r = step[-1]
                    src = ps[:, 4 + r % 3, :]
                    if not RING_ACT[r]:
                        continue
                    act.wait_ge(ring_mm, r + 1)
                if kind == "ql":
                    _, half, h, r = step
                    act.copy(ql_hi[:, h, :], src).then_inc(ring_act, 1)
                elif kind == "qk":
                    _, b, h = step
                    u = b * HEADS + h
                    act.wait_ge(masked_max, u + 1)
                    act.activation(probs[:, u % 4, 0:WIDTH[b]], probs[:, u % 4, 0:WIDTH[b]], ACT.Exp,
                                   bias=negmax[:, u:u + 1], scale=-1.0, accum_out=rowsum[:, u:u + 1]).then_inc(exped, 1)
                elif kind == "pt":
                    _, b, j, n, r = step
                    no = PT_NO[b, j, n]
                    if no >= 2:
                        act.wait_ge(pv_mm, no - 1)
                    w = 256 * (min(2 * n + 2, b + 1) - 2 * n)
                    act.copy(pT[:, no % 2, 0:w], src[:, 0:w]).then_inc(ring_act, 1)
                elif kind == "pv" and step[3] == step[1] // 2:
                    _, b, j, n = step
                    q = b // 2
                    act.wait_ge(pv_mm, PT_NO[b, j, n] + 1)
                    if q >= 2:
                        act.wait_ge(ring_mm, RING_OF["uv", q - 2, 3] + 1)
                    act.copy(olat[:, q % 2, 2 * j:2 * j + 2, (b % 2) * P:(b % 2) * P + P],
                             ps[:, 7, 0:256].rearrange("p (h n) -> p h n", h=2)
                             ).then_inc(olat_set, 1)
                elif kind == "rl":
                    _, b, r = step
                    if b >= 2:
                        act.wait_ge(ring_dve, seen(RING_DVE, RING_OF["uv", b // 2 - 1, 3]))
                    act.copy(rlT[:, :, (b % 2) * P:(b % 2) * P + P],
                             src.rearrange("p (j n) -> p j n", j=4)).then_inc(ring_act, 1)
                elif kind == "pw":
                    _, i, c, r = step
                    act.activation(mix[:, 4 + i, c * 512:(c + 1) * 512], src, ACT.Copy, scale=pscale[:, i:i + 1]
                                   ).then_inc(ring_act, 1)
                elif kind == "csq":
                    _, c = step
                    act.wait_ge(ring_dve, seen(RING_DVE, RING_OF["cm", c]))
                    for i in range(2):
                        act.activation(csq[:, i, c * 512:(c + 1) * 512], conv[:, i, c * 512:(c + 1) * 512], ACT.Square
                                       ).then_inc(conv_sq, 1)
                elif kind == "cv":
                    _, c, r = step
                    act.activation(crstd[:, c * 512:(c + 1) * 512], src, ACT.Sqrt, bias=eps).then_inc(ring_act, 1)
                elif kind == "cn":
                    for i in range(2):
                        act.wait_ge(conv_n, i + 2)
                        act.activation(mix[:, 6 + i, :], conv[:, i, :], ACT.Silu, bias=cvb[:, i:i + 1],
                                       scale=cvg[:, i:i + 1]).then_inc(conv_y, 1)

            act.wait_ge(conv_y, 2)
            act.wait_ge(ring_act, sum(RING_ACT))
            act.wait_ge(ring_dve, sum(RING_DVE))
            for n in range(2 * KT):
                k = MIX_ORDER[n % KT]
                if n < KT:
                    if n == 0:
                        act.wait_ge(ring_mm, len(RING_ACT))
                    act.copy(mix_hi[:, k, :], mix[:, k, :]).then_inc(mix_hi_s, 1)
                if n == KT:
                    act.wait_ge(mix_lo_s, KT)
                act.wait_ge(wo_in[n % 4], 16 * (n // 4 + 1))
                act.copy(wo_hi[n // KT][:, k, :], wo_raw[:, n % 4]).then_inc(wo_hi_s, 1)
            act.dma_start(ln_g[:], a["ln1_g"][0].partition_broadcast(P)).then_inc(ln_in, 16)
            act.dma_start(ln_b[:], a["ln1_b"][0].partition_broadcast(P)).then_inc(ln_in, 16)
            def x1T_copy(t):
                for g in (2 * t, 2 * t + 1):
                    act.wait_ge(x1_tr, g + 1)
                    act.copy(x1T[:, (g % 2) * 4:(g % 2) * 4 + 4, t * P:(t + 1) * P],
                             ps[:, g % 4, :].rearrange("p (k n) -> p k n", k=4)).then_inc(x1T_set, 1)

            for t in range(NT):
                act.wait_ge(stat, 3 * t + 3)
                act.activation(rstd, mv[:, 1:2], ACT.Sqrt, bias=eps).then_inc(ln_sd, 1)
                if t >= 4:
                    x1T_copy(t - 4)
            for t in range(NT - 4, NT):
                x1T_copy(t)
            for c in range(2):
                act.wait_ge(lg_mm, c + 1)
                act.copy(lgT[:, c * 512:(c + 1) * 512], ps[0:EXPERTS, 4 + c, :]).then_inc(lgT_set, 1)
            act.wait_ge(lg_tr, 1)
            act.activation(aff, ps[:, 6, 0:128], ACT.Sigmoid).then_inc(aff_set, 1)

            def split(t, n):
                act.wait_ge(raw_in[n], t * 16 + 16)
                if n < 4:
                    if not (isinstance(t, int) and t == 0):
                        act.wait_ge(gu_used, t * 4 + (n - 3))
                    done = gu_hi
                else:
                    if not (isinstance(t, int) and t == 0):
                        act.wait_ge(dn_used, t * 2 + (n - 5))
                    done = dn_hi
                act.copy(whi[:, n, :], raw[:, n, :]).then_inc(done, 1)

            def x_hi_part(t):
                act.wait_ge(xg_tr, t + 1)
                if not (isinstance(t, int) and t == 0):
                    act.wait_ge(gu_used, t * 4)
                act.copy(xgT_hi[:].rearrange("p k n -> p (k n)"), pair(2)).then_inc(xgT_hi_s, 1)

            def gated(t):
                act.wait_ge(gu_used, t * 4 + 4)
                if not (isinstance(t, int) and t == 0):
                    act.wait_ge(hid_set, t)
                act.activation(silu[:], ps[:, 0, :], ACT.Silu).then_inc(silu_set, 1)

            def h_hi_part(t):
                act.wait_ge(h_tr, t + 1)
                act.copy(hT_hi[:].rearrange("p f n -> p (f n)"), ps[:, 6, :]).then_inc(hT_hi_s, 1)

            def y_part(t):
                act.wait_ge(dn_used, t * 2 + 2)
                if not (isinstance(t, int) and t == 0):
                    act.wait_ge(y_out, t * 16)
                act.copy(ysb[:], pair(1)).then_inc(y_set, 1)

            def y_store(t):
                act.wait_ge(y_set, t + 1)
                act.dma_start(y_d[bass.ds(t * P, P), :], ysb[:]).then_inc(y_out, 16)

            act.wait_ge(places_set, 2)
            x_hi_part(0)
            for n in range(4):
                split(0, n)
            for n in range(3):
                split(1, n)
            gated(0)
            x_hi_part(1)
            split(1, 3)
            h_hi_part(0)
            def tile(t):
                split(t - 1, 4)
                split(t - 1, 5)
                for n in range(3):
                    split(t + 1, n)
                gated(t)
                x_hi_part(t + 1)
                split(t + 1, 3)
                y_part(t - 1)
                h_hi_part(t)
                y_store(t - 1)

            tile(1)
            with act.Fori(2, TILES - 1) as t:
                tile(t)
            T = TILES - 1
            split(T - 1, 4)
            split(T - 1, 5)
            gated(T)
            y_part(T - 1)
            h_hi_part(T)
            y_store(T - 1)
            split(T, 4)
            split(T, 5)
            y_part(T)
            y_store(T)
            for t in range(NT):
                act.wait_ge(yb_in[t % 2], 16 * (t // 2 + 1))
                act.activation(yb[:, t % 2], yb[:, t % 2], ACT.Copy, scale=gate[:, t, 1:2]).then_inc(yb_set, 1)
                act.wait_ge(stat, 3 * (NT + t) + 3)
                act.activation(rstd, mv[:, 1:2], ACT.Sqrt, bias=eps).then_inc(ln_sd, 1)

        @block.vector
        def _(dve):
            own = [0]

            def link(ins):
                own[0] += 1
                ins.then_inc(dve_chain, 1)
                dve.wait_ge(dve_chain, own[0])

            dve.memset(ones_rank[:], 1.0 / RANK)
            dve.memset(ones_conv[:], 1.0 / 256).then_inc(dve_set, 1)
            dve.memset(wuv[:], 0.0).then_inc(zeros_set, 1)
            dve.memset(wpool[:], 0.0).then_inc(zeros_set, 1)
            link(dve.memset(wuk[:], 0.0))
            link(dve.memset(eps, EPS))
            for i in range(2):
                for h in range(2):
                    rows, w = slice(h * HD, (h + 1) * HD), WINDOWS[2 * i + h]
                    link(dve.memset(invw[rows, i:i + 1], 1.0 / w))
                    if w < 16:
                        dve.memset(corr[rows, i, w:16], 1.0)
                    for c in range(w):
                        last = dve.memset(corr[rows, i, c:c + 1], w / (c + 1.0))
                    link(last)

            def w_split(j):
                dve.wait_ge(w_hi_s, j + 1)
                dve.tensor_tensor(w_lo[:, j % 2], w_raw[:, j % 2], f32(w_hi[:, j % 2]), ALU.subtract).then_inc(w_lo_s, 1)

            w_split(0)
            for g in range(2 * NT):
                t, half = divmod(g, 2)
                part = (slice(None), slice(half * 4, half * 4 + 4), slice(t * P, (t + 1) * P))
                dve.wait_ge(x_hi, g + 1)
                dve.tensor_tensor(xT_lo[part], ps[:, g % 4, :].rearrange("p (k n) -> p k n", k=4), f32(xT_hi[part]),
                                  ALU.subtract).then_inc(x_lo, 1)
            dve.wait_ge(wuk_tr, 1)
            for h in range(HEADS):
                rows = slice((h % 2) * HD, (h % 2 + 1) * HD)
                dve.tensor_scalar(wuk[rows, h, :], ps[rows, 0, (h // 2) * P:(h // 2 + 1) * P], HD ** -0.5, None,
                                  ALU.mult).then_inc(wuk_set, 1)
            dve.wait_ge(par_in, 16 * 7)

            def unit(k):
                name, i, j = UNITS[k]
                if name == "cT" and i == 1:
                    dve.wait_ge(c_hi, 1)
                    dve.tensor_tensor(cT_lo[:], cT[:], f32(cT_hi[:]), ALU.subtract).then_inc(c_lo, 1)
                if name == "ms" and i == 1:
                    dve.wait_ge(unit_act, seen(BY_ACT, k))
                    dve.reciprocal(rstd_kv[:], rstd_kv[:]).then_inc(kv_norm, 1)
                    dve.wait_ge(kv_norm, 1)
                    dve.scalar_tensor_tensor(cT[:], kvT[:], kvg, rstd_kv[:], ALU.mult, ALU.mult).then_inc(kv_norm, 3)
                if name == "ikw" and i == 1:
                    dve.wait_ge(ik_hi, 1)
                    dve.tensor_tensor(ikT_lo[0:IDIM, :], iT[0:IDIM, :], f32(ikT_hi[0:IDIM, :]), ALU.subtract
                                      ).then_inc(ik_lo, 1)
                if not BY_DVE[k]:
                    return
                src = ps[:, 4 + k % 4, :]
                t0, n = COLS[j][2][i] if j is not None else (i * 512, 512)
                if name[:2] == "iq":
                    part = (slice(None), int(name[2]), slice(t0 - 256, t0 - 256 + n))
                    dve.wait_ge(unit_act, seen(BY_ACT, k))
                    dve.tensor_tensor(iqT_lo[part], src[:, 0:n], f32(iqT_hi[part]), ALU.subtract).then_inc(unit_dve, 1)
                elif name == "iwT":
                    dve.wait_ge(unit_mm, k + 1)
                    dve.tensor_scalar(iw[:, 4 * i:4 * i + 4, :],
                                      src.rearrange("p (t c) -> p t c", t=4)[:, :, IDIM:IDIM + IHEADS],
                                      (IHEADS * IDIM) ** -0.5, None, ALU.mult).then_inc(unit_dve, 1)
                elif name[0] == "a":
                    ti = int(name[1])
                    if k == UNITS.index(("a0", 0, 6)):
                        dve.memset(hpad[:, :, 0:PAD_H], 0.0).then_inc(pads_set, 1)
                    dve.wait_ge(unit_mm, k + 1)
                    dve.wait_ge(unit_act, seen(BY_ACT, [q for q, u in enumerate(UNITS) if u[0] == "gate1"][1]))
                    dve.tensor_tensor(hpad[:, ti, PAD_H + t0:PAD_H + t0 + n], src, sig[:, ti, t0:t0 + n], ALU.mult
                                      ).then_inc(unit_dve, 1)

            def index(u):
                b, h = IDX[u]
                acc, r = bias[:, AT[b]:AT[b] + WIDTH[b]], relu[:, u % 2, 0:WIDTH[b]]
                dve.wait_ge(idx_relu, u + 1)
                if h == 0:
                    dve.wait_ge(unit_dve, seen(BY_DVE, UNITS.index(("iwT", 1, None))))
                    dve.tensor_scalar(acc, r, iw[:, b, h:h + 1], None, ALU.mult).then_inc(idx_sum, 1)
                else:
                    dve.wait_ge(idx_sum, u)
                    dve.scalar_tensor_tensor(acc, r, iw[:, b, h:h + 1], acc, ALU.mult, ALU.add).then_inc(idx_sum, 1)
                if h == IHEADS - 1:
                    c = COLUMN[b]
                    dve.wait_ge(idx_sum, u + 1)
                    dve.tensor_reduce(hi[:, c:c + 1], acc, AX.X, ALU.max, apply_absolute_value=True).then_inc(bound, 1)

            def item(what, n):
                if what == "idx":
                    index(n)
                else:
                    j = UNITS[n][2]
                    if j is not None and UNITS[n][1] == 0 and j + 1 < len(COLS):
                        w_split(j + 1)
                    unit(n)

            for p in PLAN[:LAST_IDX + 1]:
                item(*p)
            rest = PLAN[LAST_IDX + 1:]

            def tap(w):
                src = hpad[:, 0, w:w + S]
                if w == 0:
                    dve.wait_ge(pads_set, 1)
                    dve.wait_ge(unit_dve, sum(BY_DVE))
                    dve.tensor_scalar(conv[:, 0, :], src, convw[:, w:w + 1], convb[:, 0:1], ALU.mult, ALU.add
                                      ).then_inc(conv0, 1)
                else:
                    dve.wait_ge(conv0, w)
                    dve.scalar_tensor_tensor(conv[:, 0, :], src, convw[:, w:w + 1], conv[:, 0, :], ALU.mult, ALU.add
                                             ).then_inc(conv0, 1)

            dve.wait_ge(bound, len(BLOCKS))
            for b in BLOCKS:
                c = COLUMN[b]
                dve.memset(thr[:, c:c + 1], float(WIDTH[b] - (TOPK if b in COUNT_DVE else 2 * TOPK)))
            dve.tensor_scalar(lo, hi, -1.0, None, ALU.mult)
            dve.memset(cand, 0.0).then_inc(cand_set, 1)
            dve.wait_ge(cand_set, 1)
            dve.wait_ge(masked_s, len(BLOCKS))
            taps = 0
            for r in range(ROUNDS):
                b = COUNT_DVE[0]
                c = COLUMN[b]
                dve.tensor_scalar(junk_dve[:, 0:WIDTH[b]], bias[:, AT[b]:AT[b] + WIDTH[b]], cand[:, c:c + 1], 0.0,
                                  ALU.is_lt, ALU.add, accum_out=res[:, c:c + 1]).then_inc(counted_dve, 1)
                if rest:
                    item(*rest.pop(0))
                if not rest or UNITS[rest[0][1]][0][0] in "pq":
                    for _ in range(2 if r > ROUNDS // 4 else 1):
                        if taps < TAPS:
                            tap(taps)
                            taps += 1
                dve.wait_ge(counted_dve, r + 1)
                dve.wait_ge(counted_act, len(COUNT_ACT) * (r + 1))
                link(dve.tensor_tensor(passed, res, thr, ALU.is_le))
                link(dve.tensor_tensor(failed, res, thr, ALU.is_gt))
                link(dve.copy_predicated(lo, passed, cand))
                link(dve.copy_predicated(hi, failed, cand))
                if r + 1 < ROUNDS:
                    link(dve.tensor_tensor(below, lo, hi, ALU.add))
                    dve.tensor_scalar(cand, below, 0.5, None, ALU.mult).then_inc(cand_set, 1)
                    dve.wait_ge(cand_set, r + 2)
            for p in rest:
                item(*p)
            while taps < TAPS:
                tap(taps)
                taps += 1

            dve.wait_ge(unit_act, sum(BY_ACT))
            dve.memset(uT[:, :, 0:PAD_U], 0.0)
            dve.memset(doubled[0][:, 0:PAD_U], 0.0)
            link(dve.memset(doubled[1][:, 0:PAD_U], 0.0))
            for i in range(2):
                token, cur, w = uT[:, i, :], uT[:, i, :], 1
                for turn in range(2 * i + 2):
                    rows = slice(0, P) if 2 * w <= WINDOWS[2 * i] else slice(HD, P)
                    out = doubled[turn % 2]
                    link(dve.tensor_tensor(out[rows, w:], cur[rows, w:], cur[rows, 0:PAD_U + S - w], ALU.add))
                    cur, w = out, 2 * w
                    if w in WINDOWS[2 * i:2 * i + 2]:
                        h = WINDOWS[2 * i:2 * i + 2].index(w)
                        hr = slice(h * HD, (h + 1) * HD)
                        link(dve.tensor_tensor(cur[hr, PAD_U:PAD_U + 16], cur[hr, PAD_U:PAD_U + 16], corr[hr, i, :], ALU.mult))
                        dve.scalar_tensor_tensor(sums[hr, i, PAD_U:], cur[hr, PAD_U:], invw[hr, i:i + 1],
                                                 token[hr, PAD_U:], ALU.mult, ALU.subtract).then_inc(pooled, 1)
                        dve.wait_ge(pooled, 2 * i + h + 1)

            def choose(b):
                c, w = COLUMN[b], WIDTH[b]
                x = bias[:, AT[b]:AT[b] + w]
                A, T, N = above[:, 0:w], tied[:, 0:w], tie_no[:, 0:w]
                link(dve.tensor_scalar(A, x, hi[:, c:c + 1], 0.0, ALU.is_gt, ALU.add, accum_out=need[:, c:c + 1]))
                link(dve.tensor_scalar(need[:, c:c + 1], need[:, c:c + 1], -1.0, float(TOPK), ALU.mult, ALU.add))
                link(dve.scalar_tensor_tensor(T, x, lo[:, c:c + 1], A, ALU.is_ge, ALU.subtract))
                link(dve.tensor_tensor_scan(N, T, T, 0.0, ALU.add, ALU.max))
                link(dve.scalar_tensor_tensor(T, N, need[:, c:c + 1], T, ALU.is_le, ALU.mult))
                link(dve.scalar_tensor_tensor(T, T, -1.0, A, ALU.add, ALU.add))
                link(dve.tensor_scalar(x, T, BIG, None, ALU.mult))

            for step in STEPS:
                kind = step[0]
                if kind in RING:
                    r = step[-1]
                    src = ps[:, 4 + r % 3, :]
                    if not RING_DVE[r]:
                        continue
                    dve.wait_ge(ring_mm, r + 1)
                if kind == "choose":
                    choose(step[1])
                elif kind == "ql":
                    _, half, h, r = step
                    dve.wait_ge(ring_act, seen(RING_ACT, r))
                    dve.tensor_tensor(ql_lo[:, h, :], src, f32(ql_hi[:, h, :]), ALU.subtract).then_inc(ring_dve, 1)
                elif kind == "qk":
                    _, b, h = step
                    u = b * HEADS + h
                    dve.wait_ge(qk_mm, u + 1)
                    if u == 0:
                        dve.wait_ge(tri_set, 3)
                        dve.wait_ge(ring_mm, RING_OF["pw", 1, 1] + 1)
                    if u >= 4:
                        bb, jj = divmod((u - 4) // 2, 4)
                        dve.wait_ge(ring_mm, RING_OF["pt", bb, jj, bb // 2] + 1)
                    dve.tensor_tensor_reduce(out=probs[:, u % 4, 0:WIDTH[b]], in0=pair(u % 2)[:, 0:WIDTH[b]],
                                             in1=bias[:, AT[b]:AT[b] + WIDTH[b]], scale=-1.0, scalar=3.0e38,
                                             op0=ALU.add, op1=ALU.min, accum_out=negmax[:, u:u + 1]).then_inc(masked_max, 1)
                elif kind == "pt":
                    _, b, j, n, r = step
                    no = PT_NO[b, j, n]
                    if no >= 2:
                        dve.wait_ge(pv_mm, no - 1)
                    w = 256 * (min(2 * n + 2, b + 1) - 2 * n)
                    dve.tensor_copy(pT[:, no % 2, 0:w], src[:, 0:w]).then_inc(ring_dve, 1)
                elif kind == "rl_set":
                    _, b = step
                    dve.wait_ge(exped, HEADS * (b + 1))
                    if b:
                        dve.wait_ge(ring_mm, RING_OF["rl", b - 1] + 1)
                    dve.reciprocal(rlrep[:], rowsum[:, b * HEADS:(b + 1) * HEADS].unsqueeze(2).to_broadcast([P, HEADS, HD])
                                   ).then_inc(rl_set, 1)
                elif kind == "uv":
                    _, q, j, r = step
                    dve.wait_ge(ring_act, seen(RING_ACT, RING_OF["rl", 2 * q + 1]))
                    dve.tensor_tensor(mix[:, j, q * 256:(q + 1) * 256], src[:, 0:256], rlT[:, j, :], ALU.mult
                                      ).then_inc(ring_dve, 1)
                elif kind == "cm":
                    _, c, r = step
                    for i in range(2):
                        ch = conv[:, i, c * 512:(c + 1) * 512]
                        dve.tensor_tensor(ch, ch, src, ALU.subtract).then_inc(ring_dve if i else conv_c, 1)
                elif kind == "cn":
                    dve.wait_ge(ring_act, seen(RING_ACT, RING_OF["cv", 1]))
                    dve.wait_ge(conv_sq, 4)
                    dve.reciprocal(crstd[:], crstd[:]).then_inc(conv_n, 1)
                    dve.wait_ge(conv_n, 1)
                    for i in range(2):
                        dve.tensor_tensor(conv[:, i, :], conv[:, i, :], crstd[:], ALU.mult).then_inc(conv_n, 1)

            def wo_split(n):
                k = MIX_ORDER[n % KT]
                if n < KT:
                    dve.wait_ge(mix_hi_s, n + 1)
                    dve.tensor_tensor(mix_lo[:, k, :], mix[:, k, :], f32(mix_hi[:, k, :]), ALU.subtract).then_inc(mix_lo_s, 1)
                dve.wait_ge(wo_hi_s, n + 1)
                dve.tensor_tensor(wo_lo[n // KT][:, k, :], wo_raw[:, n % 4], f32(wo_hi[n // KT][:, k, :]), ALU.subtract
                                  ).then_inc(wo_lo_s, 1)

            def norm(t, first, g, b_done):
                x = x1_tile(t)
                n = t if first else NT + t
                for c in range(2):
                    dve.bn_stats(stats[:, c, :], x[:, c * 512:(c + 1) * 512]).then_inc(stat, 1)
                dve.wait_ge(stat, 3 * n + 2)
                dve.bn_aggr(mv, stats).then_inc(stat, 1)
                dve.wait_ge(stat, 3 * n + 3)
                dve.wait_ge(ln_sd, n + 1)
                link(dve.reciprocal(rstd, rstd))
                link(dve.tensor_scalar(x, x, mv[:, 0:1], rstd, ALU.subtract, ALU.mult))
                dve.tensor_tensor(x, x, g[:], ALU.mult).then_inc(ln_scaled, 1)

            dve.wait_ge(ring_mm, len(RING_ACT))
            dve.wait_ge(ring_act, sum(RING_ACT))
            for n in range(2 * KT):
                wo_split(n)
            for n in range(2 * NT):
                hf, t = divmod(n, NT)
                y = x1_tile(t)[:, hf * 512:(hf + 1) * 512]
                dve.wait_ge(wo_mm, n + 1)
                dve.wait_ge(xr_in[n % 4], 16 * (n // 4 + 1))
                dve.scalar_tensor_tensor(y, x_res[:, n % 4], ALPHA, ps[:, n % 8, :], ALU.mult, ALU.add).then_inc(y1_set, 1)
                if hf:
                    dve.wait_ge(y1_set, n + 1)
                    if t == 0:
                        dve.wait_ge(ln_in, 32)
                    norm(t, True, ln_g, None)

            dve.wait_ge(route_in, 32)
            dve.wait_ge(rconst, 5)
            dve.wait_ge(aff_set, 1)
            aff3 = aff.rearrange("p (t e) -> p t e", t=NT)
            score3 = score.rearrange("p (t e) -> p t e", t=NT)
            link(dve.tensor_tensor(score3, aff3, rbias.unsqueeze(1).to_broadcast([P, NT, EXPERTS]), ALU.add))
            s4 = score.rearrange("p (n c) -> p n c", c=PER_GROUP)
            dve.tensor_tensor(pairs[:, :, 0:3], s4[:, :, 0:3], s4[:, :, 1:4], ALU.add)
            dve.tensor_tensor(pairs[:, :, 3:5], s4[:, :, 0:2], s4[:, :, 2:4], ALU.add)
            link(dve.tensor_tensor(pairs[:, :, 5:6], s4[:, :, 0:1], s4[:, :, 3:4], ALU.add))
            link(dve.tensor_reduce(gs, pairs, AX.X, ALU.max))
            gs3, gv3 = gs.rearrange("p (t g) -> p t g", t=NT), gv.rearrange("p (t g) -> p t g", t=NT)
            fg3 = first_g.rearrange("p (t g) -> p t g", t=NT)

            def first_best(values, weights, scratch, onehot, n):
                wide = [P, NT, n]
                link(dve.tensor_reduce(top, values, AX.X, ALU.max))
                link(dve.tensor_tensor(scratch, values, top.unsqueeze(2).to_broadcast(wide), ALU.is_equal))
                link(dve.tensor_tensor(scratch, scratch, weights.unsqueeze(1).to_broadcast(wide), ALU.mult))
                link(dve.tensor_reduce(top, scratch, AX.X, ALU.max))
                link(dve.tensor_tensor(onehot, scratch, top.unsqueeze(2).to_broadcast(wide), ALU.is_equal))

            first_best(gs3, w4, gv3, fg3, GROUPS)
            link(dve.tensor_scalar(first_g, first_g, BIG, -BIG, ALU.mult, ALU.add))
            link(dve.tensor_tensor(masked.rearrange("p (n c) -> p n c", c=PER_GROUP), s4,
                                   first_g.unsqueeze(2).to_broadcast([P, NT * GROUPS, PER_GROUP]), ALU.add))
            masked3, pick3 = masked.rearrange("p (t e) -> p t e", t=NT), pick.rearrange("p (t e) -> p t e", t=NT)
            oh3 = [oh.rearrange("p (t e) -> p t e", t=NT) for oh in (oh1, oh2)]
            first_best(masked3, w16, pick3, oh3[0], EXPERTS)
            link(dve.scalar_tensor_tensor(masked, oh1, -BIG, masked, ALU.mult, ALU.add))
            first_best(masked3, w16, pick3, oh3[1], EXPERTS)
            for oh, g_ in ((oh3[0], ga), (oh3[1], gb)):
                link(dve.tensor_tensor(pick3, aff3, oh, ALU.mult))
                link(dve.tensor_reduce(g_, pick3, AX.X, ALU.add))
            dve.tensor_tensor(pick, oh1, oh2, ALU.add).then_inc(oh_set, 1)
            link(dve.tensor_tensor(gsum, ga, gb, ALU.add))
            link(dve.reciprocal(gsum, gsum))
            link(dve.tensor_tensor(gate[:, :, 0], ga, gsum, ALU.mult))
            link(dve.tensor_tensor(gate[:, :, 1], gb, gsum, ALU.mult))
            dve.wait_ge(m_tr, 1)
            link(dve.tensor_copy(mT[:], pair(0)[0:16, :]))
            link(dve.tensor_tensor_scan(rank[:], ones_row[:], mT[:], 0.0, ALU.mult, ALU.add))
            dve.tensor_scalar(cmp[:, 0:8], thr8, rank[:, S - 1:S], 0.0, ALU.is_lt, ALU.add, accum_out=ntile
                              ).then_inc(ntile_set, 1)
            dve.wait_ge(ntile_set, 1)
            dve.wait_ge(cum_mm, 1)
            link(dve.tensor_scalar(slot0, ps[0:16, 4, 0:1], float(P), -1.0, ALU.mult, ALU.add))
            link(dve.tensor_tensor(cum, ps[0:16, 4, 0:1], ntile, ALU.add))
            dve.tensor_scalar(cmp, tcol, cum, None, ALU.is_ge).then_inc(cmp_set, 1)
            dve.tensor_scalar(rank[:], rank[:], slot0, None, ALU.add).then_inc(slotT_set, 1)
            dve.wait_ge(te_mm, 1)
            dve.tensor_scalar(expert_of[0:1, 0:TILES + 1], ps[0:1, 5, 0:TILES + 1], float(EXPERTS - 1), None, ALU.min
                              ).then_inc(experts_set, 1)
            dve.wait_ge(s_tr, 1)
            for i in range(2):
                link(dve.tensor_tensor(pick3, ps[:, 7, 0:128].rearrange("p (t e) -> p t e", t=NT), oh3[i], ALU.mult))
                link(dve.tensor_reduce(slotf[:, i * NT:(i + 1) * NT], pick3, AX.X, ALU.add))
            dve.tensor_copy(slot_i, slotf).then_inc(places_set, 1)
            dve.wait_ge(places_set, 1)
            link(dve.tensor_scalar(where_i, slot_i, P - 1, 5, ALU.bitwise_and, ALU.logical_shift_left))
            link(dve.tensor_scalar(tmp_i, slot_i, 7, None, ALU.logical_shift_right))
            dve.tensor_tensor(where_i, where_i, tmp_i, ALU.bitwise_or).then_inc(places_set, 1)
            dve.wait_ge(places_set, 2)

            def split(t, n):
                hi_s, lo_s, k = (gu_hi, gu_lo, t * 4 + (n + 1)) if n < 4 else (dn_hi, dn_lo, t * 2 + (n - 3))
                dve.wait_ge(hi_s, k)
                dve.tensor_tensor(wlo[:, n, :], raw[:, n, :], f32(whi[:, n, :]), ALU.subtract).then_inc(lo_s, 1)

            def x_lo_part(t):
                dve.wait_ge(xgT_hi_s, t + 1)
                dve.tensor_tensor(xgT_lo[:].rearrange("p k n -> p (k n)"), pair(2),
                                  f32(xgT_hi[:]).rearrange("p k n -> p (k n)"), ALU.subtract).then_inc(xgT_lo_s, 1)

            def hidden(t):
                dve.wait_ge(silu_set, t + 1)
                if not (isinstance(t, int) and t == 0):
                    dve.wait_ge(h_tr, t)
                dve.tensor_tensor(hid[:], silu[:], ps[:, 1, :], ALU.mult).then_inc(hid_set, 1)

            def h_lo_part(t):
                dve.wait_ge(hT_hi_s, t + 1)
                dve.tensor_tensor(hT_lo[:].rearrange("p f n -> p (f n)"), ps[:, 6, :],
                                  f32(hT_hi[:]).rearrange("p f n -> p (f n)"), ALU.subtract).then_inc(hT_lo_s, 1)

            x_lo_part(0)
            for n in range(4):
                split(0, n)
            for n in range(3):
                split(1, n)
            hidden(0)
            x_lo_part(1)
            split(1, 3)
            h_lo_part(0)
            with dve.Fori(1, TILES - 1) as t:
                split(t - 1, 4)
                split(t - 1, 5)
                for n in range(3):
                    split(t + 1, n)
                hidden(t)
                x_lo_part(t + 1)
                split(t + 1, 3)
                h_lo_part(t)
            T = TILES - 1
            split(T - 1, 4)
            split(T - 1, 5)
            hidden(T)
            h_lo_part(T)
            split(T, 4)
            split(T, 5)

            dve.wait_ge(ln2_in, 32)
            for t in range(NT):
                x = x1_tile(t)
                dve.wait_ge(ya_in[t % 2], 16 * (t // 2 + 1))
                dve.wait_ge(yb_set, t + 1)
                link(dve.scalar_tensor_tensor(ya[:, t % 2], ya[:, t % 2], gate[:, t, 0:1], yb[:, t % 2], ALU.mult, ALU.add))
                dve.scalar_tensor_tensor(x, x, ALPHA, ya[:, t % 2], ALU.mult, ALU.add).then_inc(summed, 1)
                dve.wait_ge(summed, t + 1)
                norm(t, False, ln2_g, None)

        @block.gpsimd
        def _(pool):
            small = dict(allow_small_or_imprecise_dtypes=True)
            pool.memset(ident[:], 0.0).then_inc(ident_set, 1)
            pool.wait_ge(ident_set, 1)
            pool.affine_select(ident[:], ident[:], [[-1, P]], ALU.not_equal, 1.0, 0, 1).then_inc(ident_set, 1)
            pool.memset(zero_i[:], 0).then_inc(table_set, 1)
            pool.wait_ge(table_set, 1)
            pool.dma_start(slots_d.rearrange("(p t) o -> p (t o)", p=P), zero_i[:]).then_inc(table_zero, 16)
            pool.wait_ge(stack_in, 16 * 20)
            pool.memset(bias[:, 0:AT[2]], 0.0).then_inc(tri_set, 1)
            pool.wait_ge(tri_set, 1)
            for b in range(FIRST_TOPK):
                diag = bias[:, AT[b] + b * P:AT[b] + (b + 1) * P]
                pool.affine_select(diag, diag, [[-1, P]], ALU.is_ge, -BIG, 0, 1).then_inc(tri_set, 1)
            for i, b in enumerate(BLOCKS):
                diag = bias[:, AT[b] + b * P:AT[b] + (b + 1) * P]
                pool.wait_ge(bound, i + 1)
                pool.affine_select(diag, diag, [[-1, P]], ALU.is_ge, -3.0e38, 0, 1).then_inc(masked_s, 1)
            pool.wait_ge(unit_dve, sum(BY_DVE))
            pool.wait_ge(pads_set, 1)
            pool.wait_ge(idx_sum, len(IDX))
            pool.wait_ge(par_in, 16 * 7)
            for w in range(TAPS):
                src, by = hpad[:, 1, w:w + S], convw[:, TAPS + w:TAPS + w + 1]
                if w == 0:
                    pool.tensor_scalar(conv[:, 1, :], src, by, convb[:, 1:2], ALU.mult, ALU.add).then_inc(conv1, 1)
                else:
                    pool.wait_ge(conv1, w)
                    pool.tensor_scalar(tapped[:], src, by, None, ALU.mult).then_inc(conv1_mul, 1)
                    pool.wait_ge(conv1_mul, w)
                    pool.tensor_tensor(conv[:, 1, :], conv[:, 1, :], tapped[:], ALU.add).then_inc(conv1, 1)
            for t in range(NT):
                if t == NT - 1:
                    pool.wait_ge(y1_set, 2 * NT)
                    pool.iota(w4, [[-1, GROUPS]], GROUPS, 0, **small).then_inc(rconst, 1)
                    pool.iota(w16, [[-1, EXPERTS]], EXPERTS, 0, **small)
                    pool.iota(thr8, [[P, NT]], 0, 0, **small)
                    pool.iota(tcol, [[1, TILES + 1]], 0, 0, **small)
                    pool.memset(ones16, 1.0)
                    pool.memset(ones_row[:], 1.0)
                    pool.iota(tokid, [[P, NT]], 0, 1).then_inc(rconst, 1)
                    pool.memset(upper, 1.0).then_inc(rconst, 1)
                    pool.wait_ge(rconst, 3)
                    pool.affine_select(upper, upper, [[1, EXPERTS]], ALU.is_gt, 0.0, 0, -1).then_inc(rconst, 2)
                pool.wait_ge(ln_scaled, t + 1)
                pool.wait_ge(ln_in, 32)
                pool.tensor_tensor(x1_tile(t), x1_tile(t), ln_b[:], ALU.add).then_inc(x1_set, 1)
            pool.wait_ge(places_set, 2)
            pool.wait_ge(table_zero, 16)
            for i in range(2):
                for t in range(NT):
                    n = i * NT + t
                    pool.indirect_dma_start(slots_d, bass.IndirectOffsetOnAxis(ap=where_i[:, n:n + 1], axis=0),
                                            tokid[:, t:t + 1], None).then_inc(scattered, 16)
            pool.wait_ge(scattered, 16 * 2 * NT)
            pool.dma_start(idx_all[:], slots_d.rearrange("(p t) o -> p (t o)", p=P)).then_inc(table_in, 16)
            pool.wait_ge(table_in, 16)

            pool.tensor_copy(idx_now[:], idx_all[:, 0:1]).then_inc(idx0_set, 1)
            pool.wait_ge(x1_out, 16 * NT)
            pool.wait_ge(idx0_set, 1)
            pool.indirect_dma_start(xg[:], None, x1_d, bass.IndirectOffsetOnAxis(ap=idx_now[:], axis=0)
                                    ).then_inc(xg_in, 16)
            with pool.Fori(1, TILES + 1) as t:
                pool.wait_ge(xg_tr, t)
                pool.tensor_copy(idx_now[:], idx_all[:, bass.ds(t, 1)]).then_inc(idx_set, 1)
                pool.wait_ge(x1_out, 16 * NT)
                pool.wait_ge(idx_set, t)
                pool.indirect_dma_start(xg[:], None, x1_d, bass.IndirectOffsetOnAxis(ap=idx_now[:], axis=0)
                                        ).then_inc(xg_in, 16)
            pool.wait_ge(y_out, 16 * TILES)

            def experts_rows(t):
                if t >= 2:
                    pool.wait_ge(summed, t - 1)
                for buf, i, done in ((ya, 0, ya_in), (yb, 1, yb_in)):
                    n = i * NT + t
                    pool.indirect_dma_start(buf[:, t % 2], None, y_d,
                                            bass.IndirectOffsetOnAxis(ap=slot_i[:, n:n + 1], axis=0)).then_inc(done[t % 2], 16)

            experts_rows(0)
            experts_rows(1)
            pool.wait_ge(ln2_in, 32)
            for t in range(NT):
                pool.wait_ge(ln_scaled, NT + t + 1)
                pool.tensor_tensor(x1_tile(t), x1_tile(t), ln2_b[:], ALU.add).then_inc(fin_done, 1)
                if t + 2 < NT:
                    experts_rows(t + 2)


_INS = ["x", "w_in", "kv_norm_g", "w_uk", "w_uv", "w_pool", "pool_scale", "conv_w", "conv_b", "conv_ln_g",
        "conv_ln_b", "w_o", "ln1_g", "ln1_b", "router_w", "router_bias", "w_gate", "w_up", "w_down", "ln2_g", "ln2_b"]


def kernel(**inputs):
    import concourse.bacc as bacc
    from concourse.bass_utils import run_bass_kernel_spmd

    nc = bacc.Bacc("TRN2", target_bir_lowering=False, num_devices=1)
    arrays, a = {}, {}
    for name in _INS:
        array = np.ascontiguousarray(inputs[name])
        arrays[f"in_{name}"] = array
        a[name] = nc.dram_tensor(f"in_{name}", array.shape, mybir.dt.from_np(array.dtype), kind="ExternalInput").ap()
    a["out"] = nc.dram_tensor("out_0", (1, S, D), F32, kind="ExternalOutput").ap()
    program(nc, a)
    return run_bass_kernel_spmd(nc, [arrays], core_ids=[0]).results[0]["out_0"]
```

```python
from contextlib import ExitStack

import numpy as np
import concourse.bass as bass
from concourse import mybir

F32, F32R, I32, BF16 = mybir.dt.float32, mybir.dt.float32r, mybir.dt.int32, mybir.dt.bfloat16
ALU, ACT, AX = mybir.AluOpType, mybir.ActivationFunctionType, mybir.AxisListType

P = 128
S, D = 1024, 1024
NT, KT = S // P, D // P
HEADS, HD, RANK = 8, 64, 128
IHEADS, IDIM, TOPK = 8, 32, 256
FIRST_TOPK = TOPK // P
TAPS = 31
WINDOWS = (2, 4, 8, 16)
EXPERTS, GROUPS, PER_GROUP, DE = 16, 4, 4, 512
FT = DE // P
ALPHA = 2.0 ** 0.25
EPS = 1e-5
COL_KV, COL_IQ, COL_IK, COL_POOL, COL_CONV = 512, 640, 896, 936, 1192
TILES = 2 * S // P + EXPERTS - 1
MIN_TILES = 2 * S // P
SLOTS = (TILES + 1) * P
BIG = 1e30
ROUNDS = 25
PAD_H, PAD_U = TAPS - 1, 16
KB = 1024

HALVES = [(0, 512), (512, 512)]
COLS = ([("kv", COL_KV, HALVES), ("ikw", COL_IK, HALVES)]
        + [(f"iq{i}", COL_IQ + P * i, [(256, 256), (512, 512)]) for i in range(2)]
        + [(f"gate{i}", COL_CONV + 256 + P * i, HALVES) for i in range(2)]
        + [(f"a{i}", COL_CONV + P * i, HALVES) for i in range(2)]
        + [(f"pool{i}", COL_POOL + P * i, HALVES) for i in range(2)]
        + [(f"q{i}", P * i, HALVES) for i in range(4)])
UNITS = []
for _j, (_n, _c, _r) in enumerate(COLS):
    UNITS += [(_n, i, _j) for i in range(len(_r))]
    if _n == "iq1":
        UNITS += [("ms", 0, None), ("ms", 1, None), ("iwT", 0, None), ("iwT", 1, None),
                  ("cT", 0, None), ("cT", 1, None)]
BY_ACT = [n[:2] in ("kv", "ik", "iq", "ga", "po", "ms", "cT") or n[0] == "q" for n, _, _ in UNITS]
BY_DVE = [n[:2] in ("iq", "a0", "a1", "iw") for n, _, _ in UNITS]
MIX_ORDER = [4, 5, 6, 7, 0, 1, 2, 3]
WIDTH = [(b + 1) * P for b in range(NT)]
AT = [sum(WIDTH[:b]) for b in range(NT)]
BLOCKS = [7, 6, 5, 4, 3, 2]
COLUMN = {b: i for i, b in enumerate(BLOCKS)}
COUNT_DVE, COUNT_ACT = [7, 6], [5, 4, 3, 2]
TAPS_FIRST = 8
IDX_PER_UNIT, IDX_FROM = 6, 2
IDX = [(b, h) for b in BLOCKS for h in range(IHEADS)]


def attention_steps():
    pairs = [(b, j) for b in range(NT) for j in range(HEADS // 2)]
    steps, ring, r_of = [], [], {}

    def unit(*step, act, dve):
        r_of[step] = len(ring)
        steps.append((*step, len(ring)))
        ring.append((act, dve))

    def scores(p):
        b, j = pairs[p]
        if j == 0 and b >= FIRST_TOPK:
            steps.append(("choose", b))
        if j == 0 and b % 4 == 0:
            for h in range(HEADS):
                unit("ql", b // 4, h, act=True, dve=True)
        for h in range(2):
            steps.append(("qk", b, 2 * j + h))

    for i in range(2):
        for c in range(2):
            unit("pw", i, c, act=True, dve=False)
    scores(0)
    turn = 0
    for p, (b, j) in enumerate(pairs):
        if p + 1 < len(pairs):
            scores(p + 1)
        groups = range(b // 2 + 1)
        for n in groups:
            turn += 1
            unit("pt", b, j, n, act=turn % 2 == 0, dve=turn % 2 == 1)
            if n:
                steps.append(("pv", b, j, n - 1))
        steps.append(("pv", b, j, groups[-1]))
        if j == HEADS // 2 - 1:
            steps.append(("rl_set", b))
            unit("rl", b, act=True, dve=False)
            if b % 2:
                for jj in range(4):
                    unit("uv", b // 2, jj, act=False, dve=True)
        if (b, j) == (NT - 1, 0):
            for c in range(2):
                unit("cm", c, act=False, dve=True)
                steps.append(("csq", c))
            for c in range(2):
                unit("cv", c, act=True, dve=False)
            steps.append(("cn",))
    return steps, [x for x, _ in ring], [x for _, x in ring], r_of


STEPS, RING_ACT, RING_DVE, RING_OF = attention_steps()
RING = {"ql", "pt", "rl", "uv", "pw", "cm", "cv"}
PT = [x for x in STEPS if x[0] == "pt"]
PT_NO = {x[1:4]: i for i, x in enumerate(PT)}


def seen(flags, k):
    return sum(flags[:k + 1])


def program(nc, a):
    ctx = ExitStack()
    with ctx:
        base = 16640

        def at(name, shape, dt, kb):
            return nc.alloc_sbuf_tensor_at(name, shape, dt, offset=base + int(kb * KB))

        def sem(name):
            return ctx.enter_context(nc.semaphore(name))

        CST, CC, SC, R1, R2, R3, END = 0, 13, 29, 47, 80, 116, 204
        ident = at("ident", [P, P], F32, CST)
        ones_rank = at("ones_rank", [P, P], F32, CST + 0.5)
        ones_conv = at("ones_conv", [P, P], F32, CST + 1)
        wuk = at("wuk", [P, HEADS, P], F32, CST + 1.5)
        wuv = at("wuv", [P, HEADS, P], F32, CST + 5.5)
        wpool = at("wpool", [P, 2, P], F32, CST + 9.5)
        par = at("par", [P, 112], F32, CST + 10.5)
        junk_dve = at("junk_dve", [P, S], BF16, CST + 11)
        kvg, pscale, convw = par[:, 0:1], par[:, 1:3], par[:, 3:65]
        convb, cvg, cvb = par[:, 65:67], par[:, 67:69], par[:, 69:71]
        invw, wnd, corr = par[:, 72:74], par[:, 74:76], par[:, 76:108].rearrange("p (i c) -> p i c", i=2)
        cT_hi = at("cT_hi", [P, S], F32R, CC)
        cT_lo = at("cT_lo", [P, S], F32R, CC + 4)
        c_nat = at("c_nat", [P, NT, P], F32, CC + 8)
        cT = at("cT", [P, S], F32, CC + 12)
        rlT = at("rlT", [P, 4, 256], F32, CC + 12)
        bias = at("bias", [P, sum(WIDTH)], F32, SC)
        iqT_hi = at("iqT_hi", [P, 2, 768], F32R, SC)
        iqT_lo = at("iqT_lo", [P, 2, 768], F32R, SC + 6)
        x_tok = at("x_tok", [P, NT, D], F32, R1)
        kvT = at("kvT", [P, S], F32, R1)
        sq = at("sq", [P, S], F32, R1 + 4)
        rstd_kv = at("rstd_kv", [P, S], F32, R1 + 8)
        iT = at("iT", [P, S], F32, R1 + 12)
        ikT_hi = at("ikT_hi", [P, S], F32R, R1 + 16.25)
        ikT_lo = at("ikT_lo", [P, S], F32R, R1 + 20.25)
        uT = at("uT", [P, 2, PAD_U + S], F32, R1)
        sums = at("sums", [P, 2, PAD_U + S], F32, R1 + 8.125)
        sig = at("sig", [P, 2, S], F32, R1 + 8.125)
        hpad = at("hpad", [P, 2, 1056], F32, R1 + 16.25)
        conv = at("conv", [P, 2, S], F32, R1 + 24.5)
        csq = at("csq", [P, 2, S], F32, R2 + 16)
        crstd = at("crstd", [P, S], F32, R2 + 24)
        probs = at("probs", [P, 4, S], F32, R1)
        stack_iq = at("stack_iq", [P, IHEADS, 768], F32R, R2)
        stack_ik = at("stack_ik", [P, S], F32R, R2 + 24)
        relu = at("relu", [P, 2, S], F32, R2 + 28)
        tapped = at("tapped", [P, S], F32, R2 + 32)
        above = at("above", [P, S], F32, R2 + 16)
        tied = at("tied", [P, S], F32, R2 + 20)
        tie_no = at("tie_no", [P, S], F32, R2 + 24)
        qT = at("qT", [P, 4, S], F32, R2)
        wuk_raw = at("wuk_raw", [P, HEADS, HD], F32, R2)
        doubled = [at(f"doubled{i}", [P, PAD_U + S], F32, R2 + 16 + 4.25 * i) for i in range(2)]
        xT_hi = at("xT_hi", [P, KT, S], F32R, R3)
        xT_lo = at("xT_lo", [P, KT, S], F32R, R3 + 32)
        w_raw = at("w_raw", [P, 2, KT, P], F32, R3 + 64)
        w_hi = at("w_hi", [P, 2, KT, P], F32R, R3 + 72)
        w_lo = at("w_lo", [P, 2, KT, P], F32R, R3 + 80)
        ql_hi = at("ql_hi", [P, HEADS, 512], F32R, R3)
        ql_lo = at("ql_lo", [P, HEADS, 512], F32R, R3 + 16)
        diag = at("diag", [P, TAPS, P], F32, R3 + 32)
        mix = at("mix", [P, KT, S], F32, R3 + 32)
        olat = at("olat", [P, 2, HEADS, 256], F32, R3 + 64)
        pT = at("pT", [P, 2, 512], F32, R3 + 80)
        rlrep = at("rlrep", [P, HEADS, HD], F32, R3 + 84)
        mix_hi = at("mix_hi", [P, KT, S], F32R, R1)
        mix_lo = at("mix_lo", [P, KT, S], F32R, 96)
        wo_hi = [at("wo_hi0", [P, KT, 512], F32R, 128), at("wo_hi1", [P, KT, 512], F32R, 148)]
        wo_lo = [at("wo_lo0", [P, KT, 512], F32R, 180), at("wo_lo1", [P, KT, 512], F32R, 164)]
        wo_raw = at("wo_raw", [P, 4, 512], F32, SC)
        x_res = at("x_res", [P, 4, 512], F32, SC + 8)
        ln_g = at("ln_g", [P, D], F32, R3 + 80)
        ln_b = at("ln_b", [P, D], F32, R3 + 84)
        xa = at("xa", [P, 4, D], F32, CC)
        xb = at("xb", [P, 4, D], F32, R2)
        x1T = at("x1T", [P, KT, S], F32, R3)
        raw = at("raw", [P, 6, 4 * DE], F32, SC)
        whi = at("whi", [P, 6, 4 * DE], F32R, 96)
        wlo = at("wlo", [P, 6, 4 * DE], F32R, 144)
        xg = at("xg", [P, D], F32, 192)
        xgT_hi = at("xgT_hi", [P, KT, P], F32R, 196)
        xgT_lo = at("xgT_lo", [P, KT, P], F32R, 200)
        silu = at("silu", [P, DE], F32, CST + 0.5)
        hid = at("hid", [P, DE], F32, CST + 2.5)
        hT_hi = at("hT_hi", [P, FT, P], F32R, CST + 4.5)
        hT_lo = at("hT_lo", [P, FT, P], F32R, CST + 6.5)
        ysb = at("ysb", [P, D], F32, CST + 8.5)
        ln2_g = at("ln2_g", [P, D], F32, 112)
        ln2_b = at("ln2_b", [P, D], F32, 116)
        junk_act = at("junk_act", [P, S], BF16, END)
        sm = at("sm", [P, 432], F32, END + 2)
        iw = sm[:, 0:64].rearrange("p (t h) -> p t h", t=NT)
        lo, hi, cand, res, thr, low = (sm[:, 64 + 6 * i:70 + 6 * i] for i in range(6))
        passed, top_score = sm[:, 266:272], sm[:, 272:278]
        need = sm[:, 100:106]
        negmax = sm[:, 106:170]
        rowsum = sm[:, 170:234]
        stats = sm[:, 234:246].rearrange("p (c s) -> p c s", c=2)
        mv = sm[:, 246:248]
        rstd = sm[:, 248:249]
        eps = sm[:, 249:250]
        shift = sm[:, 250:251]

        RT = SC
        rt = at("rt", [P, 1536], F32, RT)
        rbias, aff, score = rt[:, 0:16], rt[:, 16:144], rt[:, 144:272]
        pairs = rt[:, 272:464].rearrange("p (n c) -> p n c", c=6)
        gs, gv, first_g = rt[:, 464:496], rt[:, 496:528], rt[:, 528:560]
        gm = rt[:, 560:568]
        w4, w16 = rt[:, 568:572], rt[:, 572:588]
        masked, pick, oh1, oh2 = (rt[:, 588 + 128 * i:716 + 128 * i] for i in range(4))
        top = rt[:, 1100:1108]
        ga, gb, gsum = rt[:, 1108:1116], rt[:, 1116:1124], rt[:, 1124:1132]
        slotf = rt[:, 1132:1148]
        rw = at("rw", [P, KT, EXPERTS], F32, RT + 6)
        lgT = at("lgT", [EXPERTS, S], F32, RT + 7)
        mT = at("mT", [EXPERTS, S], F32, RT + 11)
        rank = at("rank", [EXPERTS, S], F32, RT + 15)
        rk = at("rk", [P, 224], F32, RT + 19)
        ones_row = at("ones_row", [EXPERTS, S], F32, RT + 20)
        thr8, upper, tcol = rk[0:16, 0:8], rk[0:16, 8:24], rk[0:16, 24:56]
        ntile, cum, slot0, cmp = rk[0:16, 56:57], rk[0:16, 57:58], rk[0:16, 58:59], rk[0:16, 64:96]
        ones16 = rk[0:16, 59:60]
        expert_row, live_row, fresh_row, loads_row = (rk[0:1, 96 + 32 * i:96 + 32 * i + TILES + 1] for i in range(4))
        tiles_used = rk[0:1, 60:61]
        ri = at("ri", [P, 88], I32, CST + 12.5)
        slot_i, where_i = ri[:, 0:16], ri[:, 16:32]
        tmp_i = ri[:, 72:88]
        entry = ri[:, 32:64].rearrange("p (n c) -> p n c", c=2)
        entry_gate = entry[:, :, 1].bitcast(F32).rearrange("p (i t) -> p i t", i=2)
        tile_row = at("tile_row", [1, 128], I32, END + 0.75)
        expert_of, fresh_of, loads_of = (tile_row[:, 32 * i:32 * i + TILES + 1] for i in range(3))
        last_tile = tile_row[:, 96:97]
        table = at("table", [P, TILES + 1, 2], I32, END)
        slot_gate = table[:, :, 1].bitcast(F32)
        idx_now = at("idx_now", [P, 1], I32, END + 0.25)
        zero_i = at("zero_i", [P, 2 * (TILES + 1)], I32, END + 0.5)


        ps = ctx.enter_context(nc.psum_tensor("ps", [P, 8, 512], F32))

        def pair(i):
            return ps[:, 2 * i:2 * i + 2, :].rearrange("p b n -> p (b n)")

        x1_d = nc.dram_tensor("x1_d", (S, D), F32, kind="Internal").ap()
        slots_d = nc.dram_tensor("slots_d", (SLOTS, 2), I32, kind="Internal").ap()
        y_d = nc.dram_tensor("y_d", (TILES * P, D), F32, kind="Internal").ap()

        par_in, wuk_in, wuv_in, wpool_in = sem("par_in"), sem("wuk_in"), sem("wuv_in"), sem("wpool_in")
        x_in = [sem(f"x_in{i}") for i in range(NT)]
        w_in_s = [sem(f"w_in{i}") for i in range(2)]
        ident_set, zeros_set, dve_set = sem("ident_set"), sem("zeros_set"), sem("dve_set")
        x_tr, x_hi, x_lo, w_hi_s, w_lo_s = (sem(n) for n in ("x_tr", "x_hi", "x_lo", "w_hi_s", "w_lo_s"))
        wuk_tr, wuk_set = sem("wuk_tr"), sem("wuk_set")
        unit_mm, unit_act, unit_dve = sem("unit_mm"), sem("unit_act"), sem("unit_dve")
        kv_sq, kv_sd, kv_norm, c_hi, c_lo = (sem(n) for n in ("kv_sq", "kv_sd", "kv_norm", "c_hi", "c_lo"))
        ik_hi, ik_lo, stack_in = sem("ik_hi"), sem("ik_lo"), sem("stack_in")
        idx_mm, idx_relu, idx_sum = sem("idx_mm"), sem("idx_relu"), sem("idx_sum")
        bound, masked_s, cand_set = sem("bound"), sem("masked_s"), sem("cand_set")
        counted_dve, counted_act, dve_chain = sem("counted_dve"), sem("counted_act"), sem("dve_chain")
        tri_set, pads_set = sem("tri_set"), sem("pads_set")
        diag_set, conv0_mm, conv0, conv1, conv1_mul, pooled, pool_chain = (
            sem(n) for n in ("diag_set", "conv0_mm", "conv0", "conv1", "conv1_mul", "pooled", "pool_chain"))
        ring_mm, ring_act, ring_dve = sem("ring_mm"), sem("ring_act"), sem("ring_dve")
        qk_mm, masked_max, exped, rl_set = sem("qk_mm"), sem("masked_max"), sem("exped"), sem("rl_set")
        pv_mm, olat_set = sem("pv_mm"), sem("olat_set")
        conv_c, conv_sq, conv_n, conv_y = (sem(n) for n in ("conv_c", "conv_sq", "conv_n", "conv_y"))
        mix_hi_s, mix_lo_s = sem("mix_hi_s"), sem("mix_lo_s")
        wo_in = [sem(f"wo_in{i}") for i in range(4)]
        xr_in = [sem(f"xr_in{i}") for i in range(4)]
        ln_in, wo_hi_s, wo_lo_s, wo_mm = sem("ln_in"), sem("wo_hi_s"), sem("wo_lo_s"), sem("wo_mm")
        y1_set, stat, ln_sd, ln_scaled, x1_set = (sem(n) for n in ("y1_set", "stat", "ln_sd", "ln_scaled", "x1_set"))
        x1_tr, x1T_set, x1_out = sem("x1_tr"), sem("x1T_set"), sem("x1_out")
        route_in, lg_mm, lgT_set, lg_tr, aff_set = (sem(n) for n in ("route_in", "lg_mm", "lgT_set", "lg_tr", "aff_set"))
        routed, oh_set, m_tr, mT_set, ntile_set = (sem(n) for n in ("routed", "oh_set", "m_tr", "mT_set", "ntile_set"))
        cum_mm, slotT_set, cmp_set, te_mm, s_tr = (sem(n) for n in ("cum_mm", "slotT_set", "cmp_set", "te_mm", "s_tr"))
        experts_set, places_set, rconst = sem("experts_set"), sem("places_set"), sem("rconst")
        table_set, idx0_set = sem("table_set"), sem("idx0_set")
        table_zero, scattered, table_in = sem("table_zero"), sem("scattered"), sem("table_in")
        raw_in = [sem(f"raw_in{i}") for i in range(6)]
        idx_set, xg_in, xg_tr, xgT_hi_s, xgT_lo_s = (sem(n) for n in ("idx_set", "xg_in", "xg_tr", "xgT_hi_s", "xgT_lo_s"))
        gu_hi, gu_lo, dn_hi, dn_lo = (sem(n) for n in ("gu_hi", "gu_lo", "dn_hi", "dn_lo"))
        gu_used, dn_used = sem("gu_used"), sem("dn_used")
        silu_set, hid_set, h_tr, hT_hi_s, hT_lo_s = (sem(n) for n in ("silu_set", "hid_set", "h_tr", "hT_hi_s", "hT_lo_s"))
        y_filled, y_set, y_out, experts_done = sem("y_filled"), sem("y_set"), sem("y_out"), sem("experts_done")
        y_added = [sem(f"y_added{i}") for i in range(NT)]
        ln2_in, x1_scaled, ln_shift, ln_unit, fin_done, out_done = (sem(n) for n in ("ln2_in", "x1_scaled", "ln_shift", "ln_unit", "fin_done", "out_done"))

        def f32(t):
            return t.bitcast(F32)

        def three(pe, out, l_hi, l_lo, r_hi, r_lo, start, stop):
            pe.matmul(out, l_hi, r_hi, start=start, stop=False)
            pe.matmul(out, l_hi, r_lo, start=False, stop=False)
            return pe.matmul(out, l_lo, r_hi, start=False, stop=stop)

        def x1_tile(t):
            return xa[:, t, :] if t < 4 else xb[:, t - 4, :]

        N_UNITS = len(UNITS)
        POOL_UNITS = seen(BY_ACT, UNITS.index(("pool1", 1, [c[0] for c in COLS].index("pool1"))))
        LATER = [k for k, u in enumerate(UNITS) if u[0] == "gate0"][0]

        def plan():
            u = 0
            for k in range(N_UNITS):
                yield "unit", k
                if k >= LATER + IDX_FROM - 1:
                    for _ in range(IDX_PER_UNIT):
                        if u < len(IDX):
                            yield "idx", u
                            u += 1
        PLAN = list(plan())
        LAST_IDX = max(i for i, p in enumerate(PLAN) if p[0] == "idx")

        block = ctx.enter_context(nc.Block())

        @block.sync
        def _(sp):
            def w_tile(j):
                if j >= 2:
                    sp.wait_ge(w_lo_s, j - 1)
                c = COLS[j][1]
                sp.dma_start(w_raw[:, j % 2], a["w_in"][0].rearrange("(k p) n -> p k n", p=P)[:, :, c:c + P]
                             ).then_inc(w_in_s[j % 2], 16)

            for t in range(NT):
                sp.dma_start(x_tok[:, t], a["x"][0, t * P:(t + 1) * P, :]).then_inc(x_in[t], 16)
                if t in (3, 7):
                    w_tile(t // 4)
            for j in range(2, 6):
                w_tile(j)
            sp.wait_ge(unit_dve, seen(BY_DVE, UNITS.index(("iq1", 1, 3))))
            sp.wait_ge(ik_lo, 1)
            for part in range(4):
                rows = slice(part * IDIM, (part + 1) * IDIM)
                src = iqT_hi if part < 2 else iqT_lo
                for h4 in range(4):
                    sp.dma_start(f32(stack_iq[rows]).rearrange("p (i h) n -> p i h n", i=2)[:, :, h4, :],
                                 f32(src[h4 * IDIM:(h4 + 1) * IDIM, :, :])).then_inc(stack_in, 16)
                sp.dma_start(f32(stack_ik[rows, :]), f32((ikT_lo if part % 2 else ikT_hi)[0:IDIM, :])
                             ).then_inc(stack_in, 16)
            for j in range(6, len(COLS)):
                w_tile(j)
            for r0 in range(MIN_TILES * P, TILES * P, S):
                n = min(S, TILES * P - r0)
                sp.dma_start(y_d[r0:r0 + n, :], a["x"][0, 0:n, :]).then_inc(y_filled, 16)
            sp.wait_ge(masked_max, NT * HEADS)
            for hf in range(2):
                for k in range(KT):
                    n = hf * KT + k
                    if n >= 4:
                        sp.wait_ge(wo_lo_s, n - 3)
                    kk = MIX_ORDER[k]
                    sp.dma_start(wo_raw[:, n % 4], a["w_o"][0, kk * P:(kk + 1) * P, hf * 512:(hf + 1) * 512]
                                 ).then_inc(wo_in[n % 4], 16)
            for hf in range(2):
                for t in range(NT):
                    n = hf * NT + t
                    if n >= 4:
                        sp.wait_ge(y1_set, n - 3)
                    sp.dma_start(x_res[:, n % 4], a["x"][0, t * P:(t + 1) * P, hf * 512:(hf + 1) * 512]
                                 ).then_inc(xr_in[n % 4], 16)
            sp.wait_ge(wo_mm, 2 * NT)
            sp.wait_ge(y1_set, 2 * NT)
            sp.dma_start(rbias, a["router_bias"].partition_broadcast(P)).then_inc(route_in, 16)
            sp.dma_start(rw[:], a["router_w"].rearrange("(k p) e -> p k e", p=P)).then_inc(route_in, 16)
            for t in range(NT):
                sp.wait_ge(x1_set, t + 1)
                sp.dma_start(x1_d[t * P:(t + 1) * P, :], x1_tile(t)).then_inc(x1_out, 16)
            sp.wait_ge(experts_set, 1)
            sp.wait_ge(places_set, 2)

            def expert(t):
                return sp.value_load(expert_of[0:1, bass.ds(t, 1)], min_val=0, max_val=EXPERTS - 1)

            def gate_up(e, loaded):
                for n, (w, half) in enumerate((("w_gate", 0), ("w_up", 0), ("w_gate", 1), ("w_up", 1))):
                    if loaded is not None:
                        sp.wait_ge(gu_lo, loaded * 4 + (n + 1))
                    src = a[w][0].rearrange("e (p k) n -> e p (k n)", p=P)[
                        bass.ds(e, 1), :, half * 4 * DE:(half + 1) * 4 * DE]
                    sp.dma_start(raw[:, n, :], src.rearrange("e p n -> (e p) n")).then_inc(raw_in[n], 16)

            def down(e, loaded):
                for n in range(2):
                    if loaded is not None:
                        sp.wait_ge(dn_lo, loaded * 2 + (n + 1))
                    src = a["w_down"][0].rearrange("e (p k) n -> e p (k n)", p=P)[
                        bass.ds(e, 1), :, n * 4 * DE:(n + 1) * 4 * DE]
                    sp.dma_start(raw[:, 4 + n, :], src.rearrange("e p n -> (e p) n")).then_inc(raw_in[4 + n], 16)

            def if_fresh(t, load):
                fresh = sp.value_load(fresh_of[0:1, bass.ds(t, 1)], min_val=0, max_val=1)
                with sp.If(fresh == 1):
                    load(expert(t), sp.value_load(loads_of[0:1, bass.ds(t - 1, 1)], min_val=0, max_val=EXPERTS - 1))

            e = expert(0)
            gate_up(e, None)
            if_fresh(1, gate_up)
            down(e, None)
            with sp.Fori(2, TILES) as t:
                if_fresh(t, gate_up)
                if_fresh(t - 1, down)
            if_fresh(TILES - 1, down)
            sp.wait_ge(experts_done, 1)
            sp.dma_start(ln2_g[:], a["ln2_g"][0].partition_broadcast(P)).then_inc(ln2_in, 16)
            sp.dma_start(ln2_b[:], a["ln2_b"][0].partition_broadcast(P)).then_inc(ln2_in, 16)
            for t in range(NT):
                sp.wait_ge(fin_done, t + 1)
                sp.dma_start(a["out"][0, t * P:(t + 1) * P, :], x1_tile(t)).then_inc(out_done, 16)
            sp.wait_ge(out_done, 16 * NT)

        @block.tensor
        def _(pe):
            pe.wait_ge(ident_set, 2)
            for g in range(2 * NT):
                t, half = divmod(g, 2)
                if half == 0:
                    pe.wait_ge(x_in[t], 16)
                if g >= 4:
                    pe.wait_ge(x_lo, g - 3)
                for k in range(4):
                    kk = half * 4 + k
                    last = pe.transpose(ps[:, g % 4, k * P:(k + 1) * P], x_tok[:, t, kk * P:(kk + 1) * P], ident[:])
                last.then_inc(x_tr, 1)
            pe.wait_ge(wuk_in, 16)
            pe.wait_ge(x_lo, 2 * NT)
            for j in range(4):
                last = pe.transpose(ps[:, 0, j * P:(j + 1) * P],
                                    wuk_raw[:, 2 * j:2 * j + 2, :].rearrange("p h d -> p (h d)"), ident[:])
            last.then_inc(wuk_tr, 1)
            pe.wait_ge(dve_set, 1)

            def bank_free(k):
                if k >= 4:
                    if seen(BY_ACT, k - 4):
                        pe.wait_ge(unit_act, seen(BY_ACT, k - 4))
                    if seen(BY_DVE, k - 4):
                        pe.wait_ge(unit_dve, seen(BY_DVE, k - 4))

            def unit(k):
                name, i, j = UNITS[k]
                out = ps[:, 4 + k % 4, :]
                bank_free(k)
                if j is not None:
                    t0, n = COLS[j][2][i]
                    pe.wait_ge(w_lo_s, j + 1)
                    for kk in range(KT):
                        last = three(pe, out[:, 0:n], w_hi[:, j % 2, kk, :], w_lo[:, j % 2, kk, :],
                                     xT_hi[:, kk, t0:t0 + n], xT_lo[:, kk, t0:t0 + n], kk == 0, kk == KT - 1)
                elif name == "ms":
                    pe.wait_ge(kv_sq, 2)
                    last = pe.matmul(out, ones_rank[:], sq[:, i * 512:(i + 1) * 512], start=True, stop=True)
                elif name == "cT":
                    pe.wait_ge(kv_norm, 2 + 2)
                    for t in range(4):
                        c = (4 * i + t) * P
                        last = pe.transpose(out[:, t * P:(t + 1) * P], cT[:, c:c + P], ident[:])
                elif name == "iwT":
                    for t in range(4):
                        c = (4 * i + t) * P
                        last = pe.transpose(out[:, t * P:(t + 1) * P], iT[:, c:c + P], ident[:])
                last.then_inc(unit_mm, 1)

            def index(u):
                b, h = IDX[u]
                if u == 0:
                    pe.wait_ge(stack_in, 16 * 20)
                    pe.wait_ge(wuk_set, 8)
                if u >= 2:
                    pe.wait_ge(idx_relu, u - 1)
                for c in range(0, WIDTH[b], 512):
                    n = min(512, WIDTH[b] - c)
                    last = pe.matmul(pair(u % 2)[:, c:c + n], stack_iq[:, h, (b - 2) * P:(b - 1) * P],
                                     stack_ik[:, c:c + n], start=True, stop=True)
                last.then_inc(idx_mm, 1)

            for what, n in PLAN:
                (unit if what == "unit" else index)(n)

            pe.wait_ge(unit_act, sum(BY_ACT))
            pe.wait_ge(unit_dve, sum(BY_DVE))
            pe.wait_ge(idx_relu, len(IDX))
            pe.wait_ge(pads_set, 1)
            for w in range(TAPS):
                pe.wait_ge(diag_set, w + 1)
                for c in range(2):
                    last = pe.matmul(ps[:, 4 + c, :], diag[:, w, :], hpad[:, 0, c * 512 + w:c * 512 + w + 512],
                                     start=w == 0, stop=w == TAPS - 1)
            last.then_inc(conv0_mm, 1)

            for step in STEPS:
                kind = step[0]
                if kind in RING:
                    r = step[-1]
                    out = ps[:, 4 + r % 3, :]
                    if r < 2:
                        pe.wait_ge(conv0, 1)
                    if r >= 3:
                        if seen(RING_ACT, r - 3):
                            pe.wait_ge(ring_act, seen(RING_ACT, r - 3))
                        if seen(RING_DVE, r - 3):
                            pe.wait_ge(ring_dve, seen(RING_DVE, r - 3))
                if kind == "ql":
                    _, half, h, r = step
                    pe.matmul(out, wuk[:, h, :], qT[:, h // 2, half * 512:(half + 1) * 512],
                              start=True, stop=True).then_inc(ring_mm, 1)
                elif kind == "qk":
                    _, b, h = step
                    u = b * HEADS + h
                    if u >= 2:
                        pe.wait_ge(masked_max, u - 1)
                    pe.wait_ge(ring_dve, seen(RING_DVE, RING_OF["ql", b // 4, h]))
                    q0 = (b % 4) * P
                    for c in range(0, WIDTH[b], 512):
                        n = min(512, WIDTH[b] - c)
                        last = three(pe, pair(u % 2)[:, c:c + n], ql_hi[:, h, q0:q0 + P], ql_lo[:, h, q0:q0 + P],
                                     cT_hi[:, c:c + n], cT_lo[:, c:c + n], True, True)
                    last.then_inc(qk_mm, 1)
                elif kind == "pt":
                    _, b, j, n, r = step
                    pe.wait_ge(exped, b * HEADS + 2 * j + 2)
                    for k in range(2 * n, min(2 * n + 2, b + 1)):
                        for h in range(2):
                            c = (k - 2 * n) * 256 + h * P
                            last = pe.transpose(out[:, c:c + P],
                                                probs[:, (2 * j + h) % 4, k * P:(k + 1) * P], ident[:])
                    last.then_inc(ring_mm, 1)
                elif kind == "pv":
                    _, b, j, n = step
                    acc = ps[:, 7, 0:256]
                    if n == 0 and b * 4 + j:
                        pe.wait_ge(olat_set, b * 4 + j)
                    r = RING_OF["pt", b, j, n]
                    if RING_ACT[r]:
                        pe.wait_ge(ring_act, seen(RING_ACT, r))
                    else:
                        pe.wait_ge(ring_dve, seen(RING_DVE, r))
                    for k in range(2 * n, min(2 * n + 2, b + 1)):
                        c = (k - 2 * n) * 256
                        last = pe.matmul(acc, c_nat[:, k, :], pT[:, PT_NO[b, j, n] % 2, c:c + 256],
                                         start=k == 0, stop=k == b)
                    last.then_inc(pv_mm, 1)
                elif kind == "rl":
                    _, b, r = step
                    pe.wait_ge(rl_set, b + 1)
                    for j in range(4):
                        last = pe.transpose(out[:, j * P:(j + 1) * P],
                                            rlrep[:, 2 * j:2 * j + 2, :].rearrange("p h d -> p (h d)"), ident[:])
                    last.then_inc(ring_mm, 1)
                elif kind == "uv":
                    _, q, j, r = step
                    if j == 0:
                        pe.wait_ge(olat_set, 4 * (2 * q + 2))
                        pe.wait_ge(wuv_in, 32)
                    for h in range(2):
                        last = pe.matmul(out[:, 0:256], wuv[:, 2 * j + h, :], olat[:, q % 2, 2 * j + h, :],
                                         start=h == 0, stop=h == 1)
                    last.then_inc(ring_mm, 1)
                elif kind == "pw":
                    _, i, c, r = step
                    pe.wait_ge(pooled, 4)
                    pe.wait_ge(wpool_in, 32)
                    pe.matmul(out, wpool[:, i, :], sums[:, i, PAD_U + c * 512:PAD_U + (c + 1) * 512],
                              start=True, stop=True).then_inc(ring_mm, 1)
                elif kind in ("cm", "cv"):
                    _, c, r = step
                    if kind == "cm":
                        pe.wait_ge(conv0, 1)
                        pe.wait_ge(conv1, TAPS)
                    else:
                        pe.wait_ge(conv_sq, 2 * c + 2)
                    src = conv if kind == "cm" else csq
                    for i in range(2):
                        last = pe.matmul(out, ones_conv[:], src[:, i, c * 512:(c + 1) * 512], start=i == 0, stop=i == 1)
                    last.then_inc(ring_mm, 1)

            pe.wait_ge(olat_set, 4 * NT)
            pe.wait_ge(ring_act, sum(RING_ACT))
            pe.wait_ge(ring_dve, sum(RING_DVE))
            for n in range(2 * NT):
                hf, t = divmod(n, NT)
                if n >= 8:
                    pe.wait_ge(y1_set, n - 7)
                for i, k in enumerate(MIX_ORDER):
                    if t == 0:
                        pe.wait_ge(wo_lo_s, hf * KT + i + 1)
                        if hf == 0:
                            pe.wait_ge(mix_lo_s, i + 1)
                    last = three(pe, ps[:, n % 8, :], mix_hi[:, k, t * P:(t + 1) * P], mix_lo[:, k, t * P:(t + 1) * P],
                                 wo_hi[hf][:, k, :], wo_lo[hf][:, k, :], i == 0, i == KT - 1)
                last.then_inc(wo_mm, 1)

            pe.wait_ge(y1_set, NT + 4)
            for g in range(2 * NT):
                t, half = divmod(g, 2)
                if half == 0:
                    pe.wait_ge(x1_set, t + 1)
                if g >= 4:
                    pe.wait_ge(x1T_set, g - 3)
                for k in range(4):
                    kk = half * 4 + k
                    last = pe.transpose(ps[:, g % 4, k * P:(k + 1) * P], x1_tile(t)[:, kk * P:(kk + 1) * P], ident[:])
                last.then_inc(x1_tr, 1)
            pe.wait_ge(route_in, 32)
            pe.wait_ge(y1_set, 2 * NT)
            for c in range(2):
                pe.wait_ge(x1T_set, 8 * (c + 1))
                for k in range(KT):
                    last = pe.matmul(ps[0:EXPERTS, 4 + c, :], rw[:, k, :], x1T[:, k, c * 512:(c + 1) * 512],
                                     start=k == 0, stop=k == KT - 1)
                last.then_inc(lg_mm, 1)
            pe.wait_ge(lgT_set, 2)
            for t in range(NT):
                last = pe.transpose(ps[:, 6, t * 16:(t + 1) * 16], lgT[:, t * P:(t + 1) * P], ident[0:16, 0:16])
            last.then_inc(lg_tr, 1)
            pe.wait_ge(oh_set, 1)
            for t in range(NT):
                last = pe.transpose(pair(0)[0:16, t * P:(t + 1) * P], pick[:, t * 16:(t + 1) * 16], ident[:])
            last.then_inc(m_tr, 1)
            pe.wait_ge(ntile_set, 1)
            pe.wait_ge(rconst, 4)
            pe.matmul(ps[0:16, 4, 0:1], upper, ntile, start=True, stop=True).then_inc(cum_mm, 1)
            pe.wait_ge(cmp_set, 1)
            pe.matmul(ps[0:1, 5, 0:TILES + 1], ones16, cmp, start=True, stop=True).then_inc(te_mm, 1)
            pe.wait_ge(slotT_set, 1)
            for t in range(NT):
                last = pe.transpose(ps[:, 7, t * 16:(t + 1) * 16], rank[:, t * P:(t + 1) * P], ident[0:16, 0:16])
            last.then_inc(s_tr, 1)

            def xgT(t):
                pe.wait_ge(xg_in, t * 16 + 16)
                for k in range(KT):
                    last = pe.transpose(pair(2)[:, k * P:(k + 1) * P], xg[:, k::KT], ident[:])
                last.then_inc(xg_tr, 1)

            def loads(t):
                return pe.value_load(loads_of[0:1, bass.ds(t, 1)], min_val=0, max_val=EXPERTS - 1)

            def gate_up(t, loaded):
                pe.wait_ge(xgT_lo_s, t + 1)
                for n in range(4):
                    out = ps[:, n % 2, :]
                    pe.wait_ge(gu_lo, loaded * 4 + (n + 1))
                    for k in range(4):
                        kk = 4 * (n // 2) + k
                        last = three(pe, out, xgT_hi[:, kk, :], xgT_lo[:, kk, :], whi[:, n, k * DE:(k + 1) * DE],
                                     wlo[:, n, k * DE:(k + 1) * DE], kk == 0, kk == KT - 1)
                    last.then_inc(gu_used, 1)

            def down(t, loaded):
                pe.wait_ge(hT_lo_s, t + 1)
                if not (isinstance(t, int) and t == 0):
                    pe.wait_ge(y_set, t)
                for n in range(2):
                    pe.wait_ge(dn_lo, loaded * 2 + (n + 1))
                    for k in range(2):
                        for c in range(2):
                            col = k * D + c * 512
                            ft = 2 * n + k
                            last = three(pe, pair(1)[:, c * 512:(c + 1) * 512], hT_hi[:, ft, :], hT_lo[:, ft, :],
                                         whi[:, 4 + n, col:col + 512], wlo[:, 4 + n, col:col + 512],
                                         ft == 0, ft == FT - 1)
                    last.then_inc(dn_used, 1)

            def hidT(t):
                pe.wait_ge(hid_set, t + 1)
                for f in range(FT):
                    last = pe.transpose(ps[:, 6, f * P:(f + 1) * P], hid[:, f::FT], ident[:])
                last.then_inc(h_tr, 1)

            pe.wait_ge(places_set, 2)
            last_t = pe.value_load(last_tile, min_val=MIN_TILES - 1, max_val=TILES - 1)
            xgT(0)
            gate_up(0, 0)
            xgT(1)
            hidT(0)

            def tile(t):
                gate_up(t, loads(t))
                xgT(t + 1)
                down(t - 1, loads(t - 1))
                hidT(t)

            tile(1)
            with pe.Fori(2, TILES) as t:
                with pe.If(t <= last_t):
                    tile(t)
            down(last_t, loads(last_t))

        @block.scalar
        def _(act):
            with nc.allow_non_contiguous_dma(reason="small parameters, one element to a partition"):
                act.dma_start(kvg, a["kv_norm_g"][0].rearrange("(p o) -> p o", o=1)).then_inc(par_in, 16)
                act.dma_start(pscale, a["pool_scale"][0].rearrange("(i p) -> p i", p=P)).then_inc(par_in, 16)
                for i in range(2):
                    act.dma_start(convw[:, i * TAPS:(i + 1) * TAPS],
                                  a["conv_w"][0, :, 0, i * P:(i + 1) * P].rearrange("w p -> p w")).then_inc(par_in, 16)
                act.dma_start(convb, a["conv_b"][0].rearrange("(i p) -> p i", p=P)).then_inc(par_in, 16)
                act.dma_start(cvg, a["conv_ln_g"][0].rearrange("(i p) -> p i", p=P)).then_inc(par_in, 16)
                act.dma_start(cvb, a["conv_ln_b"][0].rearrange("(i p) -> p i", p=P)).then_inc(par_in, 16)
            act.dma_start(wuk_raw[:], a["w_uk"][0].rearrange("h r d -> r h d")).then_inc(wuk_in, 16)
            act.wait_ge(zeros_set, 2)
            for h in range(2):
                act.dma_start(wuv[:, h::2, h * HD:(h + 1) * HD], a["w_uv"][0, h::2].rearrange("h r d -> r h d")
                              ).then_inc(wuv_in, 16)
                act.dma_start(wpool[h * HD:(h + 1) * HD, :, h * HD:(h + 1) * HD],
                              a["w_pool"][0, h::2].rearrange("g c d -> c g d")).then_inc(wpool_in, 16)

            def w_split(j):
                act.wait_ge(w_in_s[j % 2], 16 * (j // 2 + 1))
                if j >= 2:
                    act.wait_ge(unit_mm, max(k for k, u in enumerate(UNITS) if u[2] == j - 2) + 1)
                act.copy(w_hi[:, j % 2], w_raw[:, j % 2]).then_inc(w_hi_s, 1)

            w_split(0)
            for g in range(2 * NT):
                t, half = divmod(g, 2)
                act.wait_ge(x_tr, g + 1)
                act.copy(xT_hi[:, half * 4:half * 4 + 4, t * P:(t + 1) * P],
                         ps[:, g % 4, :].rearrange("p (k n) -> p k n", k=4)).then_inc(x_hi, 1)

            def unit(k):
                name, i, j = UNITS[k]
                if not BY_ACT[k]:
                    return
                src = ps[:, 4 + k % 4, :]
                act.wait_ge(unit_mm, k + 1)
                t0, n = COLS[j][2][i] if j is not None else (i * 512, 512)
                tok = slice(t0, t0 + n)
                if name == "kv":
                    if i == 0:
                        act.wait_ge(x_tr, 2 * NT)
                    act.activation(sq[:, tok], src, ACT.Square).then_inc(kv_sq, 1)
                    act.copy(kvT[:, tok], src).then_inc(unit_act, 1)
                elif name == "ikw":
                    act.copy(iT[:, tok], src).then_inc(unit_act, 1)
                    if i == 1:
                        act.wait_ge(unit_act, seen(BY_ACT, k))
                        act.copy(ikT_hi[0:IDIM, :], iT[0:IDIM, :]).then_inc(ik_hi, 1)
                elif name[:2] == "iq":
                    act.copy(iqT_hi[:, int(name[2]), t0 - 256:t0 - 256 + n], src[:, 0:n]).then_inc(unit_act, 1)
                elif name == "ms":
                    act.activation(rstd_kv[:, tok], src, ACT.Sqrt, bias=eps).then_inc(unit_act, 1)
                elif name == "cT":
                    act.copy(c_nat[:, 4 * i:4 * i + 4, :].rearrange("p t r -> p (t r)"), src).then_inc(unit_act, 1)
                    if i == 1:
                        act.copy(cT_hi[:], cT[:]).then_inc(c_hi, 1)
                elif name[:4] == "gate":
                    if name == "gate0" and i == 0:
                        act.wait_ge(kv_norm, 4)
                        act.wait_ge(unit_mm, UNITS.index(("iwT", 1, None)) + 1)
                        act.wait_ge(ik_lo, 1)
                    act.activation(sig[:, int(name[4]), tok], src, ACT.Sigmoid).then_inc(unit_act, 1)
                elif name[:4] == "pool":
                    if name == "pool0" and i == 0:
                        act.wait_ge(c_hi, 1)
                        act.wait_ge(c_lo, 1)
                    act.copy(uT[:, int(name[4]), PAD_U + t0:PAD_U + t0 + n], src).then_inc(unit_act, 1)
                elif name[0] == "q":
                    act.copy(qT[:, int(name[1]), tok], src).then_inc(unit_act, 1)

            def index(u):
                b, h = IDX[u]
                act.wait_ge(idx_mm, u + 1)
                if u >= 2:
                    act.wait_ge(idx_sum, u - 1)
                act.activation(relu[:, u % 2, 0:WIDTH[b]], pair(u % 2)[:, 0:WIDTH[b]], ACT.Relu).then_inc(idx_relu, 1)

            def item(what, n):
                if what == "idx":
                    index(n)
                else:
                    j = UNITS[n][2]
                    if j is not None and UNITS[n][1] == 0 and j + 1 < len(COLS):
                        w_split(j + 1)
                    unit(n)

            for p in PLAN[:LAST_IDX + 1]:
                item(*p)
            rest = PLAN[LAST_IDX + 1:]

            def count(r):
                act.wait_ge(cand_set, r + 1)
                for i, b in enumerate(COUNT_ACT):
                    c = COLUMN[b]
                    if r + i:
                        act.wait_ge(counted_act, len(COUNT_ACT) * r + i)
                    act.activation(junk_act[:, 0:WIDTH[b]], bias[:, AT[b]:AT[b] + WIDTH[b]], ACT.Sign,
                                   bias=cand[:, c:c + 1], scale=-1.0, accum_out=res[:, c:c + 1]
                                   ).then_inc(counted_act, 1)

            act.wait_ge(masked_s, len(BLOCKS))
            act.wait_ge(table_zero, 16)
            for r in range(ROUNDS):
                count(r)
                if rest:
                    item(*rest.pop(0))
            for p in rest:
                item(*p)

            act.wait_ge(conv0_mm, 1)
            act.activation(conv[:, 0, :], pair(2), ACT.Identity, bias=convb[:, 0:1]).then_inc(conv0, 1)

            for step in STEPS:
                kind = step[0]
                if kind in RING:
                    r = step[-1]
                    src = ps[:, 4 + r % 3, :]
                    if not RING_ACT[r]:
                        continue
                    act.wait_ge(ring_mm, r + 1)
                if kind == "ql":
                    _, half, h, r = step
                    act.copy(ql_hi[:, h, :], src).then_inc(ring_act, 1)
                elif kind == "qk":
                    _, b, h = step
                    u = b * HEADS + h
                    act.wait_ge(masked_max, u + 1)
                    act.activation(probs[:, u % 4, 0:WIDTH[b]], probs[:, u % 4, 0:WIDTH[b]], ACT.Exp,
                                   bias=negmax[:, u:u + 1], scale=-1.0, accum_out=rowsum[:, u:u + 1]).then_inc(exped, 1)
                elif kind == "pt":
                    _, b, j, n, r = step
                    no = PT_NO[b, j, n]
                    if no >= 2:
                        act.wait_ge(pv_mm, no - 1)
                    w = 256 * (min(2 * n + 2, b + 1) - 2 * n)
                    act.copy(pT[:, no % 2, 0:w], src[:, 0:w]).then_inc(ring_act, 1)
                elif kind == "pv" and step[3] == step[1] // 2:
                    _, b, j, n = step
                    q = b // 2
                    act.wait_ge(pv_mm, PT_NO[b, j, n] + 1)
                    if q >= 2:
                        act.wait_ge(ring_mm, RING_OF["uv", q - 2, 3] + 1)
                    act.copy(olat[:, q % 2, 2 * j:2 * j + 2, (b % 2) * P:(b % 2) * P + P],
                             ps[:, 7, 0:256].rearrange("p (h n) -> p h n", h=2)
                             ).then_inc(olat_set, 1)
                elif kind == "rl":
                    _, b, r = step
                    if b >= 2:
                        act.wait_ge(ring_dve, seen(RING_DVE, RING_OF["uv", b // 2 - 1, 3]))
                    act.copy(rlT[:, :, (b % 2) * P:(b % 2) * P + P],
                             src.rearrange("p (j n) -> p j n", j=4)).then_inc(ring_act, 1)
                elif kind == "pw":
                    _, i, c, r = step
                    act.activation(mix[:, 4 + i, c * 512:(c + 1) * 512], src, ACT.Copy, scale=pscale[:, i:i + 1]
                                   ).then_inc(ring_act, 1)
                elif kind == "csq":
                    _, c = step
                    act.wait_ge(ring_dve, seen(RING_DVE, RING_OF["cm", c]))
                    for i in range(2):
                        act.activation(csq[:, i, c * 512:(c + 1) * 512], conv[:, i, c * 512:(c + 1) * 512], ACT.Square
                                       ).then_inc(conv_sq, 1)
                elif kind == "cv":
                    _, c, r = step
                    act.activation(crstd[:, c * 512:(c + 1) * 512], src, ACT.Sqrt, bias=eps).then_inc(ring_act, 1)
                elif kind == "cn":
                    for i in range(2):
                        act.wait_ge(conv_n, i + 2)
                        act.activation(mix[:, 6 + i, :], conv[:, i, :], ACT.Silu, bias=cvb[:, i:i + 1],
                                       scale=cvg[:, i:i + 1]).then_inc(conv_y, 1)

            act.wait_ge(conv_y, 2)
            act.wait_ge(ring_act, sum(RING_ACT))
            act.wait_ge(ring_dve, sum(RING_DVE))
            for n in range(2 * KT):
                k = MIX_ORDER[n % KT]
                if n < KT:
                    if n == 0:
                        act.wait_ge(ring_mm, len(RING_ACT))
                    act.copy(mix_hi[:, k, :], mix[:, k, :]).then_inc(mix_hi_s, 1)
                if n == KT:
                    act.wait_ge(mix_lo_s, KT)
                act.wait_ge(wo_in[n % 4], 16 * (n // 4 + 1))
                act.copy(wo_hi[n // KT][:, k, :], wo_raw[:, n % 4]).then_inc(wo_hi_s, 1)
            act.dma_start(ln_g[:], a["ln1_g"][0].partition_broadcast(P)).then_inc(ln_in, 16)
            act.dma_start(ln_b[:], a["ln1_b"][0].partition_broadcast(P)).then_inc(ln_in, 16)
            def x1T_copy(t):
                for g in (2 * t, 2 * t + 1):
                    act.wait_ge(x1_tr, g + 1)
                    act.copy(x1T[:, (g % 2) * 4:(g % 2) * 4 + 4, t * P:(t + 1) * P],
                             ps[:, g % 4, :].rearrange("p (k n) -> p k n", k=4)).then_inc(x1T_set, 1)

            def norm(n, x):
                act.wait_ge(stat, 3 * n + 3)
                act.activation(rstd, mv[:, 1:2], ACT.Sqrt, bias=eps).then_inc(ln_sd, 1)
                act.wait_ge(ln_shift, n + 1)
                act.activation(x, x, ACT.Identity, bias=shift, scale=rstd).then_inc(ln_unit, 1)

            for t in range(NT):
                norm(t, x1_tile(t))
                if t >= 4:
                    x1T_copy(t - 4)
            for t in range(NT - 4, NT):
                x1T_copy(t)
            for c in range(2):
                act.wait_ge(lg_mm, c + 1)
                act.copy(lgT[:, c * 512:(c + 1) * 512], ps[0:EXPERTS, 4 + c, :]).then_inc(lgT_set, 1)
            act.wait_ge(lg_tr, 1)
            act.activation(aff, ps[:, 6, 0:128], ACT.Sigmoid).then_inc(aff_set, 1)

            def split(t, pieces, loaded):
                for n in pieces:
                    act.wait_ge(raw_in[n], loaded * 16 + 16)
                    if not (isinstance(t, int) and t == 0):
                        if n < 4:
                            act.wait_ge(gu_used, t * 4 + (n - 3))
                        else:
                            act.wait_ge(dn_used, t * 2 + (n - 5))
                    act.copy(whi[:, n, :], raw[:, n, :]).then_inc(gu_hi if n < 4 else dn_hi, 1)

            def split_new(t, pieces):
                fresh = act.value_load(fresh_of[0:1, bass.ds(t, 1)], min_val=0, max_val=1)
                with act.If(fresh == 1):
                    split(t, pieces, act.value_load(loads_of[0:1, bass.ds(t, 1)], min_val=0, max_val=EXPERTS - 1))

            def x_hi_part(t):
                act.wait_ge(xg_tr, t + 1)
                if not (isinstance(t, int) and t == 0):
                    act.wait_ge(gu_used, t * 4)
                act.copy(xgT_hi[:].rearrange("p k n -> p (k n)"), pair(2)).then_inc(xgT_hi_s, 1)

            def gated(t):
                act.wait_ge(gu_used, t * 4 + 4)
                if not (isinstance(t, int) and t == 0):
                    act.wait_ge(hid_set, t)
                act.activation(silu[:], ps[:, 0, :], ACT.Silu).then_inc(silu_set, 1)

            def h_hi_part(t):
                act.wait_ge(h_tr, t + 1)
                act.copy(hT_hi[:].rearrange("p f n -> p (f n)"), ps[:, 6, :]).then_inc(hT_hi_s, 1)

            def y_part(t):
                act.wait_ge(dn_used, t * 2 + 2)
                if not (isinstance(t, int) and t == 0):
                    act.wait_ge(y_out, t * 16)
                act.copy(ysb[:], pair(1)).then_inc(y_set, 1)

            def y_store(t):
                act.wait_ge(y_set, t + 1)
                act.dma_start(y_d[bass.ds(t * P, P), :], ysb[:]).then_inc(y_out, 16)

            act.wait_ge(places_set, 2)
            act.wait_ge(y_filled, 16 * -(-(TILES - MIN_TILES) // NT))
            last_t = act.value_load(last_tile, min_val=MIN_TILES - 1, max_val=TILES - 1)
            x_hi_part(0)
            split(0, range(4), 0)
            split_new(1, range(3))
            gated(0)
            x_hi_part(1)
            split_new(1, [3])
            h_hi_part(0)
            split(0, (4, 5), 0)

            def tile(t):
                split_new(t + 1, range(3))
                gated(t)
                x_hi_part(t + 1)
                split_new(t + 1, [3])
                y_part(t - 1)
                h_hi_part(t)
                y_store(t - 1)
                split_new(t, (4, 5))

            tile(1)
            with act.Fori(2, TILES) as t:
                with act.If(t <= last_t):
                    tile(t)
            y_part(last_t)
            y_store(last_t)
            act.wait_ge(y_out, last_t * 16 + 16)
            act.sem_inc(experts_done, 1)

            for t in range(NT):
                norm(NT + t, x1_tile(t))

        @block.vector
        def _(dve):
            own = [0]

            def link(ins):
                own[0] += 1
                ins.then_inc(dve_chain, 1)
                dve.wait_ge(dve_chain, own[0])

            dve.memset(ones_rank[:], 1.0 / RANK)
            dve.memset(ones_conv[:], 1.0 / 256).then_inc(dve_set, 1)
            dve.memset(wuv[:], 0.0).then_inc(zeros_set, 1)
            dve.memset(wpool[:], 0.0).then_inc(zeros_set, 1)
            link(dve.memset(wuk[:], 0.0))
            link(dve.memset(eps, EPS))
            for i in range(2):
                for h in range(2):
                    rows, w = slice(h * HD, (h + 1) * HD), WINDOWS[2 * i + h]
                    link(dve.memset(invw[rows, i:i + 1], 1.0 / w))
                    if w < 16:
                        dve.memset(corr[rows, i, w:16], 1.0)
                    for c in range(w):
                        last = dve.memset(corr[rows, i, c:c + 1], w / (c + 1.0))
                    link(last)

            def w_split(j):
                dve.wait_ge(w_hi_s, j + 1)
                dve.tensor_tensor(w_lo[:, j % 2], w_raw[:, j % 2], f32(w_hi[:, j % 2]), ALU.subtract).then_inc(w_lo_s, 1)

            w_split(0)
            for g in range(2 * NT):
                t, half = divmod(g, 2)
                part = (slice(None), slice(half * 4, half * 4 + 4), slice(t * P, (t + 1) * P))
                dve.wait_ge(x_hi, g + 1)
                dve.tensor_tensor(xT_lo[part], ps[:, g % 4, :].rearrange("p (k n) -> p k n", k=4), f32(xT_hi[part]),
                                  ALU.subtract).then_inc(x_lo, 1)
            dve.wait_ge(wuk_tr, 1)
            for h in range(HEADS):
                rows = slice((h % 2) * HD, (h % 2 + 1) * HD)
                dve.tensor_scalar(wuk[rows, h, :], ps[rows, 0, (h // 2) * P:(h // 2 + 1) * P], HD ** -0.5, None,
                                  ALU.mult).then_inc(wuk_set, 1)
            dve.wait_ge(par_in, 16 * 7)

            def unit(k):
                name, i, j = UNITS[k]
                if name == "cT" and i == 1:
                    dve.wait_ge(c_hi, 1)
                    dve.tensor_tensor(cT_lo[:], cT[:], f32(cT_hi[:]), ALU.subtract).then_inc(c_lo, 1)
                if name == "ms" and i == 1:
                    dve.wait_ge(unit_act, seen(BY_ACT, k))
                    dve.reciprocal(rstd_kv[:], rstd_kv[:]).then_inc(kv_norm, 1)
                    dve.wait_ge(kv_norm, 1)
                    dve.scalar_tensor_tensor(cT[:], kvT[:], kvg, rstd_kv[:], ALU.mult, ALU.mult).then_inc(kv_norm, 3)
                if name == "ikw" and i == 1:
                    dve.wait_ge(ik_hi, 1)
                    dve.tensor_tensor(ikT_lo[0:IDIM, :], iT[0:IDIM, :], f32(ikT_hi[0:IDIM, :]), ALU.subtract
                                      ).then_inc(ik_lo, 1)
                if not BY_DVE[k]:
                    return
                src = ps[:, 4 + k % 4, :]
                t0, n = COLS[j][2][i] if j is not None else (i * 512, 512)
                if name[:2] == "iq":
                    part = (slice(None), int(name[2]), slice(t0 - 256, t0 - 256 + n))
                    dve.wait_ge(unit_act, seen(BY_ACT, k))
                    dve.tensor_tensor(iqT_lo[part], src[:, 0:n], f32(iqT_hi[part]), ALU.subtract).then_inc(unit_dve, 1)
                elif name == "iwT":
                    dve.wait_ge(unit_mm, k + 1)
                    dve.tensor_scalar(iw[:, 4 * i:4 * i + 4, :],
                                      src.rearrange("p (t c) -> p t c", t=4)[:, :, IDIM:IDIM + IHEADS],
                                      (IHEADS * IDIM) ** -0.5, None, ALU.mult).then_inc(unit_dve, 1)
                elif name[0] == "a":
                    ti = int(name[1])
                    if k == UNITS.index(("a0", 0, 6)):
                        dve.memset(hpad[:, :, 0:PAD_H], 0.0).then_inc(pads_set, 1)
                    dve.wait_ge(unit_mm, k + 1)
                    dve.wait_ge(unit_act, seen(BY_ACT, [q for q, u in enumerate(UNITS) if u[0] == "gate1"][1]))
                    dve.tensor_tensor(hpad[:, ti, PAD_H + t0:PAD_H + t0 + n], src, sig[:, ti, t0:t0 + n], ALU.mult
                                      ).then_inc(unit_dve, 1)

            def index(u):
                b, h = IDX[u]
                acc, r = bias[:, AT[b]:AT[b] + WIDTH[b]], relu[:, u % 2, 0:WIDTH[b]]
                dve.wait_ge(idx_relu, u + 1)
                if h == 0:
                    dve.wait_ge(unit_dve, seen(BY_DVE, UNITS.index(("iwT", 1, None))))
                    dve.tensor_scalar(acc, r, iw[:, b, h:h + 1], None, ALU.mult).then_inc(idx_sum, 1)
                else:
                    dve.wait_ge(idx_sum, u)
                    dve.scalar_tensor_tensor(acc, r, iw[:, b, h:h + 1], acc, ALU.mult, ALU.add).then_inc(idx_sum, 1)
                if h == IHEADS - 1:
                    c = COLUMN[b]
                    dve.wait_ge(idx_sum, u + 1)
                    dve.tensor_reduce(top_score[:, c:c + 1], acc, AX.X, ALU.max, apply_absolute_value=True).then_inc(bound, 1)

            def item(what, n):
                if what == "idx":
                    index(n)
                else:
                    j = UNITS[n][2]
                    if j is not None and UNITS[n][1] == 0 and j + 1 < len(COLS):
                        w_split(j + 1)
                    unit(n)

            for p in PLAN[:LAST_IDX + 1]:
                item(*p)
            rest = PLAN[LAST_IDX + 1:]

            dve.wait_ge(bound, len(BLOCKS))
            for b in BLOCKS:
                c = COLUMN[b]
                dve.memset(thr[:, c:c + 1], float(WIDTH[b] - (TOPK if b in COUNT_DVE else 2 * TOPK)))
            link(dve.memset(low, -1.0))
            dve.memset(cand, 0.0).then_inc(cand_set, 1)
            dve.wait_ge(cand_set, 1)
            dve.wait_ge(masked_s, len(BLOCKS))
            taps = 0
            for r in range(ROUNDS):
                step = 2.0 ** -r
                for i, b in enumerate(COUNT_DVE):
                    c = COLUMN[b]
                    if i:
                        dve.wait_ge(counted_dve, len(COUNT_DVE) * r + i)
                    dve.tensor_scalar(junk_dve[:, 0:WIDTH[b]], bias[:, AT[b]:AT[b] + WIDTH[b]], cand[:, c:c + 1], 0.0,
                                      ALU.is_lt, ALU.add, accum_out=res[:, c:c + 1]).then_inc(counted_dve, 1)
                if rest:
                    item(*rest.pop(0))
                elif taps < TAPS:
                    if taps == 0:
                        dve.wait_ge(unit_mm, N_UNITS)
                    for w in range(taps, min(taps + 5, TAPS)):
                        dve.tensor_scalar(diag[:, w, :], ident[:], convw[:, w:w + 1], None, ALU.mult
                                          ).then_inc(diag_set, 1)
                    taps = min(taps + 5, TAPS)
                dve.wait_ge(counted_dve, len(COUNT_DVE) * (r + 1))
                dve.wait_ge(counted_act, len(COUNT_ACT) * (r + 1))
                link(dve.tensor_tensor(passed, res, thr, ALU.is_le))
                link(dve.scalar_tensor_tensor(low, passed, step, low, ALU.mult, ALU.add))
                if r + 1 < ROUNDS:
                    dve.scalar_tensor_tensor(cand, low, step / 2, top_score, ALU.add, ALU.mult).then_inc(cand_set, 1)
                    dve.wait_ge(cand_set, r + 2)
            link(dve.scalar_tensor_tensor(hi, low, 2.0 ** (1 - ROUNDS), top_score, ALU.add, ALU.mult))
            link(dve.tensor_tensor(lo, low, top_score, ALU.mult))
            assert not rest and taps == TAPS

            def choose(b):
                c, w = COLUMN[b], WIDTH[b]
                x = bias[:, AT[b]:AT[b] + w]
                A, T, N = above[:, 0:w], tied[:, 0:w], tie_no[:, 0:w]
                link(dve.tensor_scalar(A, x, hi[:, c:c + 1], 0.0, ALU.is_gt, ALU.add, accum_out=need[:, c:c + 1]))
                link(dve.tensor_scalar(need[:, c:c + 1], need[:, c:c + 1], -1.0, float(TOPK), ALU.mult, ALU.add))
                link(dve.scalar_tensor_tensor(T, x, lo[:, c:c + 1], A, ALU.is_ge, ALU.subtract))
                link(dve.tensor_tensor_scan(N, T, T, 0.0, ALU.add, ALU.max))
                link(dve.scalar_tensor_tensor(T, N, need[:, c:c + 1], T, ALU.is_le, ALU.mult))
                link(dve.scalar_tensor_tensor(T, T, -1.0, A, ALU.add, ALU.add))
                link(dve.tensor_scalar(x, T, BIG, None, ALU.mult))

            for step in STEPS:
                kind = step[0]
                if kind in RING:
                    r = step[-1]
                    src = ps[:, 4 + r % 3, :]
                    if not RING_DVE[r]:
                        continue
                    dve.wait_ge(ring_mm, r + 1)
                if kind == "choose":
                    choose(step[1])
                elif kind == "ql":
                    _, half, h, r = step
                    dve.wait_ge(ring_act, seen(RING_ACT, r))
                    dve.tensor_tensor(ql_lo[:, h, :], src, f32(ql_hi[:, h, :]), ALU.subtract).then_inc(ring_dve, 1)
                elif kind == "qk":
                    _, b, h = step
                    u = b * HEADS + h
                    dve.wait_ge(qk_mm, u + 1)
                    if u == 0:
                        dve.wait_ge(tri_set, 3)
                        dve.wait_ge(ring_mm, RING_OF["pw", 1, 1] + 1)
                    if u >= 4:
                        bb, jj = divmod((u - 4) // 2, 4)
                        dve.wait_ge(ring_mm, RING_OF["pt", bb, jj, bb // 2] + 1)
                    dve.tensor_tensor_reduce(out=probs[:, u % 4, 0:WIDTH[b]], in0=pair(u % 2)[:, 0:WIDTH[b]],
                                             in1=bias[:, AT[b]:AT[b] + WIDTH[b]], scale=-1.0, scalar=3.0e38,
                                             op0=ALU.add, op1=ALU.min, accum_out=negmax[:, u:u + 1]).then_inc(masked_max, 1)
                elif kind == "pt":
                    _, b, j, n, r = step
                    no = PT_NO[b, j, n]
                    if no >= 2:
                        dve.wait_ge(pv_mm, no - 1)
                    w = 256 * (min(2 * n + 2, b + 1) - 2 * n)
                    dve.tensor_copy(pT[:, no % 2, 0:w], src[:, 0:w]).then_inc(ring_dve, 1)
                elif kind == "rl_set":
                    _, b = step
                    dve.wait_ge(exped, HEADS * (b + 1))
                    if b:
                        dve.wait_ge(ring_mm, RING_OF["rl", b - 1] + 1)
                    sums_b = rowsum[:, b * HEADS:(b + 1) * HEADS]
                    link(dve.reciprocal(sums_b, sums_b))
                    dve.tensor_copy(rlrep[:], sums_b.unsqueeze(2).to_broadcast([P, HEADS, HD])).then_inc(rl_set, 1)
                elif kind == "uv":
                    _, q, j, r = step
                    dve.wait_ge(ring_act, seen(RING_ACT, RING_OF["rl", 2 * q + 1]))
                    dve.tensor_tensor(mix[:, j, q * 256:(q + 1) * 256], src[:, 0:256], rlT[:, j, :], ALU.mult
                                      ).then_inc(ring_dve, 1)
                elif kind == "cm":
                    _, c, r = step
                    for i in range(2):
                        ch = conv[:, i, c * 512:(c + 1) * 512]
                        dve.tensor_tensor(ch, ch, src, ALU.subtract).then_inc(ring_dve if i else conv_c, 1)
                elif kind == "cn":
                    dve.wait_ge(ring_act, seen(RING_ACT, RING_OF["cv", 1]))
                    dve.wait_ge(conv_sq, 4)
                    dve.reciprocal(crstd[:], crstd[:]).then_inc(conv_n, 1)
                    dve.wait_ge(conv_n, 1)
                    for i in range(2):
                        dve.tensor_tensor(conv[:, i, :], conv[:, i, :], crstd[:], ALU.mult).then_inc(conv_n, 1)

            def wo_split(n):
                k = MIX_ORDER[n % KT]
                if n < KT:
                    dve.wait_ge(mix_hi_s, n + 1)
                    dve.tensor_tensor(mix_lo[:, k, :], mix[:, k, :], f32(mix_hi[:, k, :]), ALU.subtract).then_inc(mix_lo_s, 1)
                dve.wait_ge(wo_hi_s, n + 1)
                dve.tensor_tensor(wo_lo[n // KT][:, k, :], wo_raw[:, n % 4], f32(wo_hi[n // KT][:, k, :]), ALU.subtract
                                  ).then_inc(wo_lo_s, 1)

            def norm_stats(n, x):
                if n:
                    dve.wait_ge(ln_unit, n)
                for c in range(2):
                    dve.bn_stats(stats[:, c, :], x[:, c * 512:(c + 1) * 512]).then_inc(stat, 1)
                dve.wait_ge(stat, 3 * n + 2)
                dve.bn_aggr(mv, stats).then_inc(stat, 1)
                dve.wait_ge(stat, 3 * n + 3)
                dve.wait_ge(ln_sd, n + 1)
                link(dve.reciprocal(rstd, rstd))
                dve.scalar_tensor_tensor(shift, mv[:, 0:1], -1.0, rstd, ALU.mult, ALU.mult).then_inc(ln_shift, 1)

            def norm_gain(n, x, g):
                dve.wait_ge(ln_unit, n + 1)
                dve.tensor_tensor(x, x, g[:], ALU.mult).then_inc(ln_scaled, 1)

            dve.wait_ge(ring_mm, len(RING_ACT))
            dve.wait_ge(ring_act, sum(RING_ACT))
            for n in range(2 * KT):
                wo_split(n)
            for n in range(2 * NT):
                hf, t = divmod(n, NT)
                y = x1_tile(t)[:, hf * 512:(hf + 1) * 512]
                dve.wait_ge(wo_mm, n + 1)
                dve.wait_ge(xr_in[n % 4], 16 * (n // 4 + 1))
                dve.scalar_tensor_tensor(y, x_res[:, n % 4], ALPHA, ps[:, n % 8, :], ALU.mult, ALU.add).then_inc(y1_set, 1)
                if hf:
                    dve.wait_ge(y1_set, n + 1)
                    norm_stats(t, x1_tile(t))
                    if t:
                        dve.wait_ge(ln_in, 32)
                        norm_gain(t - 1, x1_tile(t - 1), ln_g)
            norm_gain(NT - 1, x1_tile(NT - 1), ln_g)

            dve.wait_ge(route_in, 32)
            dve.wait_ge(rconst, 5)
            dve.wait_ge(aff_set, 1)
            aff3 = aff.rearrange("p (t e) -> p t e", t=NT)
            score3 = score.rearrange("p (t e) -> p t e", t=NT)
            link(dve.tensor_tensor(score3, aff3, rbias.unsqueeze(1).to_broadcast([P, NT, EXPERTS]), ALU.add))
            s4 = score.rearrange("p (n c) -> p n c", c=PER_GROUP)
            dve.tensor_tensor(pairs[:, :, 0:3], s4[:, :, 0:3], s4[:, :, 1:4], ALU.add)
            dve.tensor_tensor(pairs[:, :, 3:5], s4[:, :, 0:2], s4[:, :, 2:4], ALU.add)
            link(dve.tensor_tensor(pairs[:, :, 5:6], s4[:, :, 0:1], s4[:, :, 3:4], ALU.add))
            link(dve.tensor_reduce(gs, pairs, AX.X, ALU.max))
            gs3, gv3 = gs.rearrange("p (t g) -> p t g", t=NT), gv.rearrange("p (t g) -> p t g", t=NT)
            fg3 = first_g.rearrange("p (t g) -> p t g", t=NT)

            def first_best(values, weights, scratch, onehot, n):
                wide = [P, NT, n]
                link(dve.tensor_reduce(top, values, AX.X, ALU.max))
                link(dve.tensor_tensor(scratch, values, top.unsqueeze(2).to_broadcast(wide), ALU.is_equal))
                link(dve.tensor_tensor(scratch, scratch, weights.unsqueeze(1).to_broadcast(wide), ALU.mult))
                link(dve.tensor_reduce(top, scratch, AX.X, ALU.max))
                link(dve.tensor_tensor(onehot, scratch, top.unsqueeze(2).to_broadcast(wide), ALU.is_equal))

            first_best(gs3, w4, gv3, fg3, GROUPS)
            link(dve.tensor_scalar(first_g, first_g, BIG, -BIG, ALU.mult, ALU.add))
            link(dve.tensor_tensor(masked.rearrange("p (n c) -> p n c", c=PER_GROUP), s4,
                                   first_g.unsqueeze(2).to_broadcast([P, NT * GROUPS, PER_GROUP]), ALU.add))
            masked3, pick3 = masked.rearrange("p (t e) -> p t e", t=NT), pick.rearrange("p (t e) -> p t e", t=NT)
            oh3 = [oh.rearrange("p (t e) -> p t e", t=NT) for oh in (oh1, oh2)]
            first_best(masked3, w16, pick3, oh3[0], EXPERTS)
            link(dve.scalar_tensor_tensor(masked, oh1, -BIG, masked, ALU.mult, ALU.add))
            first_best(masked3, w16, pick3, oh3[1], EXPERTS)
            for oh, g_ in ((oh3[0], ga), (oh3[1], gb)):
                link(dve.tensor_tensor(pick3, aff3, oh, ALU.mult))
                link(dve.tensor_reduce(g_, pick3, AX.X, ALU.add))
            dve.tensor_tensor(pick, oh1, oh2, ALU.add).then_inc(oh_set, 1)
            link(dve.tensor_tensor(gsum, ga, gb, ALU.add))
            link(dve.reciprocal(gsum, gsum))
            link(dve.tensor_tensor(entry_gate[:, 0, :], ga, gsum, ALU.mult))
            link(dve.tensor_tensor(entry_gate[:, 1, :], gb, gsum, ALU.mult))
            dve.wait_ge(m_tr, 1)
            link(dve.tensor_copy(mT[:], pair(0)[0:16, :]))
            link(dve.tensor_tensor_scan(rank[:], ones_row[:], mT[:], 0.0, ALU.mult, ALU.add))
            dve.tensor_scalar(cmp[:, 0:8], thr8, rank[:, S - 1:S], 0.0, ALU.is_lt, ALU.add, accum_out=ntile
                              ).then_inc(ntile_set, 1)
            dve.wait_ge(ntile_set, 1)
            dve.wait_ge(cum_mm, 1)
            link(dve.tensor_scalar(slot0, ps[0:16, 4, 0:1], float(P), -1.0, ALU.mult, ALU.add))
            link(dve.tensor_tensor(cum, ps[0:16, 4, 0:1], ntile, ALU.add))
            dve.tensor_scalar(cmp, tcol, cum, None, ALU.is_ge).then_inc(cmp_set, 1)
            dve.tensor_scalar(rank[:], rank[:], slot0, None, ALU.add).then_inc(slotT_set, 1)
            dve.wait_ge(te_mm, 1)
            link(dve.tensor_copy(expert_row, ps[0:1, 5, 0:TILES + 1]))
            link(dve.tensor_scalar(live_row, expert_row, float(EXPERTS), 0.0, ALU.is_lt, ALU.add, accum_out=tiles_used))
            link(dve.tensor_tensor(fresh_row[:, 1:], expert_row[:, 1:], expert_row[:, :TILES], ALU.is_gt))
            link(dve.memset(fresh_row[:, 0:1], 1.0))
            link(dve.tensor_tensor(fresh_row, fresh_row, live_row, ALU.mult))
            link(dve.tensor_tensor_scan(loads_row, ones_row[0:1, 0:TILES + 1], fresh_row, -1.0, ALU.mult, ALU.add))
            dve.tensor_scalar(expert_of, expert_row, float(EXPERTS - 1), None, ALU.min)
            dve.tensor_copy(fresh_of, fresh_row)
            dve.tensor_copy(loads_of, loads_row)
            dve.tensor_scalar(last_tile, tiles_used, -1.0, None, ALU.add).then_inc(experts_set, 1)
            dve.wait_ge(s_tr, 1)
            for i in range(2):
                link(dve.tensor_tensor(pick3, ps[:, 7, 0:128].rearrange("p (t e) -> p t e", t=NT), oh3[i], ALU.mult))
                link(dve.tensor_reduce(slotf[:, i * NT:(i + 1) * NT], pick3, AX.X, ALU.add))
            dve.tensor_copy(slot_i, slotf).then_inc(places_set, 1)
            dve.wait_ge(places_set, 1)
            link(dve.tensor_scalar(where_i, slot_i, P - 1, 5, ALU.bitwise_and, ALU.logical_shift_left))
            link(dve.tensor_scalar(tmp_i, slot_i, 7, None, ALU.logical_shift_right))
            dve.tensor_tensor(where_i, where_i, tmp_i, ALU.bitwise_or).then_inc(places_set, 1)
            dve.wait_ge(places_set, 2)

            def split(pieces, loaded):
                for n in pieces:
                    if n < 4:
                        dve.wait_ge(gu_hi, loaded * 4 + (n + 1))
                    else:
                        dve.wait_ge(dn_hi, loaded * 2 + (n - 3))
                    dve.tensor_tensor(wlo[:, n, :], raw[:, n, :], f32(whi[:, n, :]), ALU.subtract
                                      ).then_inc(gu_lo if n < 4 else dn_lo, 1)

            def split_new(t, pieces):
                fresh = dve.value_load(fresh_of[0:1, bass.ds(t, 1)], min_val=0, max_val=1)
                with dve.If(fresh == 1):
                    split(pieces, dve.value_load(loads_of[0:1, bass.ds(t, 1)], min_val=0, max_val=EXPERTS - 1))

            def x_lo_part(t):
                dve.wait_ge(xgT_hi_s, t + 1)
                dve.tensor_tensor(xgT_lo[:].rearrange("p k n -> p (k n)"), pair(2),
                                  f32(xgT_hi[:]).rearrange("p k n -> p (k n)"), ALU.subtract).then_inc(xgT_lo_s, 1)

            def hidden(t):
                dve.wait_ge(silu_set, t + 1)
                if not (isinstance(t, int) and t == 0):
                    dve.wait_ge(h_tr, t)
                dve.scalar_tensor_tensor(hid[:], silu[:], slot_gate[:, bass.ds(t, 1)], ps[:, 1, :], ALU.mult, ALU.mult
                                         ).then_inc(hid_set, 1)

            def h_lo_part(t):
                dve.wait_ge(hT_hi_s, t + 1)
                dve.tensor_tensor(hT_lo[:].rearrange("p f n -> p (f n)"), ps[:, 6, :],
                                  f32(hT_hi[:]).rearrange("p f n -> p (f n)"), ALU.subtract).then_inc(hT_lo_s, 1)

            last_t = dve.value_load(last_tile, min_val=MIN_TILES - 1, max_val=TILES - 1)
            dve.wait_ge(table_in, 16)
            x_lo_part(0)
            split(range(4), 0)
            split_new(1, range(3))
            hidden(0)
            x_lo_part(1)
            split_new(1, [3])
            h_lo_part(0)
            split((4, 5), 0)

            def tile(t):
                split_new(t + 1, range(3))
                hidden(t)
                x_lo_part(t + 1)
                split_new(t + 1, [3])
                h_lo_part(t)
                split_new(t, (4, 5))

            tile(1)
            with dve.Fori(2, TILES) as t:
                with dve.If(t <= last_t):
                    tile(t)

            dve.wait_ge(ln2_in, 32)
            for t in range(NT):
                dve.wait_ge(y_added[t], 32)
                norm_stats(NT + t, x1_tile(t))
                if t:
                    norm_gain(NT + t - 1, x1_tile(t - 1), ln2_g)
            norm_gain(2 * NT - 1, x1_tile(NT - 1), ln2_g)

        @block.gpsimd
        def _(pool):
            small = dict(allow_small_or_imprecise_dtypes=True)
            pool.memset(ident[:], 0.0).then_inc(ident_set, 1)
            pool.wait_ge(ident_set, 1)
            pool.affine_select(ident[:], ident[:], [[-1, P]], ALU.not_equal, 1.0, 0, 1).then_inc(ident_set, 1)
            pool.memset(zero_i[:], 0).then_inc(table_set, 1)
            pool.wait_ge(table_set, 1)
            pool.dma_start(slots_d.rearrange("(p t) c -> p (t c)", p=P), zero_i[:]).then_inc(table_zero, 16)
            pool.wait_ge(stack_in, 16 * 20)
            pool.memset(bias[:, 0:AT[2]], 0.0).then_inc(tri_set, 1)
            pool.wait_ge(tri_set, 1)
            for b in range(FIRST_TOPK):
                diag = bias[:, AT[b] + b * P:AT[b] + (b + 1) * P]
                pool.affine_select(diag, diag, [[-1, P]], ALU.is_ge, -BIG, 0, 1).then_inc(tri_set, 1)
            for i, b in enumerate(BLOCKS):
                diag = bias[:, AT[b] + b * P:AT[b] + (b + 1) * P]
                pool.wait_ge(bound, i + 1)
                pool.affine_select(diag, diag, [[-1, P]], ALU.is_ge, -3.0e38, 0, 1).then_inc(masked_s, 1)
            pool.wait_ge(unit_dve, sum(BY_DVE))
            pool.wait_ge(pads_set, 1)
            pool.wait_ge(idx_sum, len(IDX))
            pool.wait_ge(par_in, 16 * 7)
            own = [0]

            def link(ins):
                own[0] += 1
                ins.then_inc(pool_chain, 1)
                pool.wait_ge(pool_chain, own[0])

            def tap(w):
                src, by = hpad[:, 1, w:w + S], convw[:, TAPS + w:TAPS + w + 1]
                if w == 0:
                    pool.tensor_scalar(conv[:, 1, :], src, by, convb[:, 1:2], ALU.mult, ALU.add).then_inc(conv1, 1)
                else:
                    pool.wait_ge(conv1, w)
                    pool.tensor_scalar(tapped[:], src, by, None, ALU.mult).then_inc(conv1_mul, 1)
                    pool.wait_ge(conv1_mul, w)
                    pool.tensor_tensor(conv[:, 1, :], conv[:, 1, :], tapped[:], ALU.add).then_inc(conv1, 1)

            for w in range(TAPS_FIRST):
                tap(w)
            pool.wait_ge(unit_act, POOL_UNITS)
            pool.memset(uT[:, :, 0:PAD_U], 0.0)
            pool.memset(doubled[0][:, 0:PAD_U], 0.0)
            link(pool.memset(doubled[1][:, 0:PAD_U], 0.0))
            for i in range(2):
                token, cur, w = uT[:, i, :], uT[:, i, :], 1
                for turn in range(2 * i + 2):
                    rows = slice(0, P) if 2 * w <= WINDOWS[2 * i] else slice(HD, P)
                    out = doubled[turn % 2]
                    link(pool.tensor_tensor(out[rows, w:], cur[rows, w:], cur[rows, 0:PAD_U + S - w], ALU.add))
                    cur, w = out, 2 * w
                    if w in WINDOWS[2 * i:2 * i + 2]:
                        h = WINDOWS[2 * i:2 * i + 2].index(w)
                        hr = slice(h * HD, (h + 1) * HD)
                        link(pool.tensor_tensor(cur[hr, PAD_U:PAD_U + 16], cur[hr, PAD_U:PAD_U + 16], corr[hr, i, :], ALU.mult))
                        link(pool.tensor_scalar(cur[hr, PAD_U:], cur[hr, PAD_U:], invw[hr, i:i + 1], None, ALU.mult))
                        pool.tensor_tensor(sums[hr, i, PAD_U:], cur[hr, PAD_U:], token[hr, PAD_U:], ALU.subtract
                                           ).then_inc(pooled, 1)
                        pool.wait_ge(pooled, 2 * i + h + 1)
            for w in range(TAPS_FIRST, TAPS):
                tap(w)
            for t in range(NT):
                if t == NT - 1:
                    pool.wait_ge(y1_set, 2 * NT)
                    pool.iota(w4, [[-1, GROUPS]], GROUPS, 0, **small).then_inc(rconst, 1)
                    pool.iota(w16, [[-1, EXPERTS]], EXPERTS, 0, **small)
                    pool.iota(thr8, [[P, NT]], 0, 0, **small)
                    pool.iota(tcol, [[1, TILES + 1]], 0, 0, **small)
                    pool.memset(ones16, 1.0)
                    pool.memset(ones_row[:], 1.0)
                    pool.iota(entry[:, :, 0].rearrange("p (i t) -> p i t", i=2), [[0, 2], [P, NT]], 0, 1).then_inc(rconst, 1)
                    pool.memset(upper, 1.0).then_inc(rconst, 1)
                    pool.wait_ge(rconst, 3)
                    pool.affine_select(upper, upper, [[1, EXPERTS]], ALU.is_gt, 0.0, 0, -1).then_inc(rconst, 2)
                pool.wait_ge(ln_scaled, t + 1)
                pool.wait_ge(ln_in, 32)
                pool.tensor_tensor(x1_tile(t), x1_tile(t), ln_b[:], ALU.add).then_inc(x1_set, 1)
            pool.wait_ge(places_set, 2)
            pool.wait_ge(table_zero, 16)
            for i in range(2):
                for t in range(NT):
                    n = i * NT + t
                    pool.indirect_dma_start(slots_d, bass.IndirectOffsetOnAxis(ap=where_i[:, n:n + 1], axis=0),
                                            entry[:, n, :], None).then_inc(scattered, 16)
            pool.wait_ge(scattered, 16 * 2 * NT)
            pool.dma_start(table[:].rearrange("p t c -> p (t c)"), slots_d.rearrange("(p t) c -> p (t c)", p=P)).then_inc(table_in, 16)
            pool.wait_ge(table_in, 16)

            pool.tensor_copy(idx_now[:], table[:, 0:1, 0]).then_inc(idx0_set, 1)
            pool.wait_ge(x1_out, 16 * NT)
            pool.wait_ge(idx0_set, 1)
            pool.indirect_dma_start(xg[:], None, x1_d, bass.IndirectOffsetOnAxis(ap=idx_now[:], axis=0)
                                    ).then_inc(xg_in, 16)

            def fetch(t):
                pool.wait_ge(xg_tr, t)
                pool.tensor_copy(idx_now[:], table[:, bass.ds(t, 1), 0]).then_inc(idx_set, 1)
                pool.wait_ge(x1_out, 16 * NT)
                pool.wait_ge(idx_set, t)
                pool.indirect_dma_start(xg[:], None, x1_d, bass.IndirectOffsetOnAxis(ap=idx_now[:], axis=0)
                                        ).then_inc(xg_in, 16)

            last_t = pool.value_load(last_tile, min_val=MIN_TILES - 1, max_val=TILES - 1)
            for t in range(1, NT + 1):
                fetch(t)
                pool.tensor_scalar(x1_tile(t - 1), x1_tile(t - 1), ALPHA, None, ALU.mult).then_inc(x1_scaled, 1)
            with pool.Fori(NT + 1, TILES + 1) as t:
                with pool.If(t <= last_t + 1):
                    fetch(t)
            pool.wait_ge(experts_done, 1)
            pool.wait_ge(x1_scaled, NT)
            for t, i in sorted(((t, i) for t in range(NT) for i in range(2)), key=lambda p: p[0] + 1.5 * p[1]):
                n = i * NT + t
                if i:
                    pool.wait_ge(y_added[t], 16)
                pool.indirect_dma_start(x1_tile(t), None, y_d,
                                        bass.IndirectOffsetOnAxis(ap=slot_i[:, n:n + 1], axis=0),
                                        compute_op=ALU.add).then_inc(y_added[t], 16)
            pool.wait_ge(ln2_in, 32)
            for t in range(NT):
                pool.wait_ge(ln_scaled, NT + t + 1)
                pool.tensor_tensor(x1_tile(t), x1_tile(t), ln2_b[:], ALU.add).then_inc(fin_done, 1)


_INS = ["x", "w_in", "kv_norm_g", "w_uk", "w_uv", "w_pool", "pool_scale", "conv_w", "conv_b", "conv_ln_g",
        "conv_ln_b", "w_o", "ln1_g", "ln1_b", "router_w", "router_bias", "w_gate", "w_up", "w_down", "ln2_g", "ln2_b"]


def kernel(**inputs):
    import concourse.bacc as bacc
    from concourse.bass_utils import run_bass_kernel_spmd

    nc = bacc.Bacc("TRN2", target_bir_lowering=False, num_devices=1)
    arrays, a = {}, {}
    for name in _INS:
        array = np.ascontiguousarray(inputs[name])
        arrays[f"in_{name}"] = array
        a[name] = nc.dram_tensor(f"in_{name}", array.shape, mybir.dt.from_np(array.dtype), kind="ExternalInput").ap()
    a["out"] = nc.dram_tensor("out_0", (1, S, D), F32, kind="ExternalOutput").ap()
    program(nc, a)
    return run_bass_kernel_spmd(nc, [arrays], core_ids=[0]).results[0]["out_0"]
```

```python
from contextlib import ExitStack

import numpy as np
import concourse.bass as bass
from concourse import mybir

F32, F32R, I32, BF16 = mybir.dt.float32, mybir.dt.float32r, mybir.dt.int32, mybir.dt.bfloat16
ALU, ACT, AX = mybir.AluOpType, mybir.ActivationFunctionType, mybir.AxisListType

P = 128
S, D = 1024, 1024
NT, KT = S // P, D // P
HEADS, HD, RANK = 8, 64, 128
IHEADS, IDIM, TOPK = 8, 32, 256
FIRST_TOPK = TOPK // P
TAPS = 31
WINDOWS = (2, 4, 8, 16)
EXPERTS, GROUPS, PER_GROUP, DE = 16, 4, 4, 512
FT = DE // P
ALPHA = 2.0 ** 0.25
EPS = 1e-5
COL_KV, COL_IQ, COL_IK, COL_POOL, COL_CONV = 512, 640, 896, 936, 1192
TILES = 2 * S // P + EXPERTS - 1
MIN_TILES = 2 * S // P
BIG = 1e30
ROUNDS = 25
PAD_H, PAD_U = TAPS - 1, 16
KB = 1024

HALVES = [(0, 512), (512, 512)]
COLS = ([("kv", COL_KV, HALVES), ("ikw", COL_IK, HALVES)]
        + [(f"iq{i}", COL_IQ + P * i, [(256, 256), (512, 512)]) for i in range(2)]
        + [(f"gate{i}", COL_CONV + 256 + P * i, HALVES) for i in range(2)]
        + [(f"a{i}", COL_CONV + P * i, HALVES) for i in range(2)]
        + [(f"pool{i}", COL_POOL + P * i, HALVES) for i in range(2)]
        + [(f"q{i}", P * i, HALVES) for i in range(4)])
UNITS = []
for _j, (_n, _c, _r) in enumerate(COLS):
    UNITS += [(_n, i, _j) for i in range(len(_r))]
    if _n == "iq1":
        UNITS += [("ms", 0, None), ("ms", 1, None), ("iwT", 0, None), ("iwT", 1, None)]
    if _n == "gate0":
        UNITS += [("cT", 0, None), ("cT", 1, None)]
BY_ACT = [n[:2] in ("kv", "ik", "iq", "ga", "po", "ms", "cT") or n[0] == "q" for n, _, _ in UNITS]
BY_DVE = [n[:2] in ("iq", "a0", "a1", "iw") for n, _, _ in UNITS]
MIX_ORDER = [4, 5, 6, 7, 0, 1, 2, 3]
WIDTH = [(b + 1) * P for b in range(NT)]
AT = [sum(WIDTH[:b]) for b in range(NT)]
BLOCKS = [7, 6, 5, 4, 3, 2]
COLUMN = {b: i for i, b in enumerate(BLOCKS)}
COUNT_DVE, COUNT_ACT = [7, 6], [5, 4, 3, 2]
ADDS_BEHIND = 4
TAPS_FIRST = 8
IDX_PER_UNIT, IDX_FROM = 6, 2
CHOICES = 7
IDX = [(b, h) for b in BLOCKS for h in range(IHEADS)]


PAIRS = ([(0, 0), (0, 1), (3, 0), (0, 2), (3, 1), (0, 3), (3, 2), (1, 0), (3, 3), (1, 1), (2, 0), (1, 2), (2, 1), (1, 3),
          (2, 2), (2, 3)] + [(b, j) for b in range(4, NT) for j in range(HEADS // 2)])
PAIR_NO = {p: i for i, p in enumerate(PAIRS)}
SHORT_PAIRS = 16


def score_no(b, h):
    return 2 * PAIR_NO[b, h // 2] + h % 2


def last_no(*blocks):
    return max(PAIR_NO[b, j] for b in blocks for j in range(HEADS // 2))


def attention_steps():
    pairs = PAIRS
    steps, ring, r_of = [], [], {}
    blocks = sorted(range(FIRST_TOPK, NT), key=lambda b: PAIR_NO[b, 0])
    choices = [("choose", b, k) for b in blocks for k in range(CHOICES)]

    def unit(*step, act, dve):
        r_of[step] = len(ring)
        steps.append((*step, len(ring)))
        ring.append((act, dve))

    def latents(half, j):
        for h in (2 * j, 2 * j + 1):
            unit("ql", half, h, act=True, dve=True)

    def rowsums(p):
        b = pairs[p][0]
        q = b // 2
        if p >= 0 and p == last_no(2 * q, 2 * q + 1):
            steps.extend(("rl_set", bb) for bb in (2 * q, 2 * q + 1))

    def scores(p):
        b, j = pairs[p]
        if PAIR_NO[b, j] == min(PAIR_NO[bb, j] for bb in range(NT // 2)):
            latents(0, j)
        while choices and any(x[1] == b for x in choices):
            steps.append(choices.pop(0))
        for h in range(2):
            steps.append(("qk", b, 2 * j + h))
        rowsums(p - 1)
        if PAIR_NO[b, j] == max(PAIR_NO[bb, j] for bb in range(NT // 2)):
            latents(1, j)
        for _ in range(min(4 if p < 2 else 1 if p < SHORT_PAIRS else 2, len(choices))):
            steps.append(choices.pop(0))

    def after_block(b):
        q = b // 2
        if b != max((2 * q, 2 * q + 1), key=lambda bb: PAIR_NO[bb, HEADS // 2 - 1]):
            return
        for bb in (2 * q, 2 * q + 1):
            unit("rl", bb, act=True, dve=False)
        for jj in range(4):
            unit("uv", q, jj, act=False, dve=True)

    scores(0)
    scores(1)
    for i in range(2):
        for c in range(2):
            unit("pw", i, c, act=True, dve=False)
    ahead = 2
    turn, waiting = 0, []

    def product():
        b, j, n = waiting.pop(0)
        steps.append(("pv", b, j, n))
        return b if n == b // 2 and j == HEADS // 2 - 1 else None

    for p, (b, j) in enumerate(pairs):
        ended = None
        for n in range(b // 2 + 1):
            turn += 1
            unit("pt", b, j, n, act=turn % 2 == 0, dve=turn % 2 == 1)
            if len(waiting) == 2:
                got = product()
                ended = got if got is not None else ended
            waiting.append((b, j, n))
            if n == min(1, b // 2):
                until = p + 2 if p + 2 < SHORT_PAIRS else p + 1
                while ahead <= min(until, len(pairs) - 1):
                    scores(ahead)
                    ahead += 1
                if ended is not None:
                    after_block(ended)
                    ended = None
        if ended is not None:
            after_block(ended)
        if (b, j) == (NT - 2, HEADS // 2 - 1):
            assert not choices
            for c in range(2):
                unit("cm", c, act=False, dve=True)
                steps.append(("csq", c))
            for c in range(2):
                unit("cv", c, act=True, dve=False)
        if b == NT - 1:
            steps.extend(("cr", c) for c in ((0, 1), (2, 3), (), ())[j])
            if j == 2:
                steps.append(("cn",))
    rowsums(len(pairs) - 1)
    while waiting:
        product()
    after_block(NT - 1)
    return steps, [x for x, _ in ring], [x for _, x in ring], r_of


STEPS, RING_ACT, RING_DVE, RING_OF = attention_steps()
RING = {"ql", "pt", "rl", "uv", "pw", "cm", "cv"}
PT = [x for x in STEPS if x[0] == "pt"]
PT_NO = {x[1:4]: i for i, x in enumerate(PT)}


def seen(flags, k):
    return sum(flags[:k + 1])


def program(nc, a):
    ctx = ExitStack()
    with ctx:
        base = 16640

        def at(name, shape, dt, kb):
            return nc.alloc_sbuf_tensor_at(name, shape, dt, offset=base + int(kb * KB))

        def sem(name):
            return ctx.enter_context(nc.semaphore(name))

        CST, CC, SC, R1, R2, R3, END = 0, 13, 29, 47, 80, 116, 204
        ident = at("ident", [P, P], F32, CST)
        ones_rank = at("ones_rank", [P, P], F32, CST + 0.5)
        ones_conv = at("ones_conv", [P, P], F32, CST + 1)
        wuk = at("wuk", [P, HEADS, P], F32, CST + 1.5)
        wuv = at("wuv", [P, HEADS, P], F32, CST + 5.5)
        wpool = at("wpool", [P, 2, P], F32, CST + 9.5)
        par = at("par", [P, 112], F32, CST + 10.5)
        junk_dve = at("junk_dve", [P, S], BF16, CST + 11)
        kvg, pscale, convw = par[:, 0:1], par[:, 1:3], par[:, 3:65]
        convb, cvg, cvb = par[:, 65:67], par[:, 67:69], par[:, 69:71]
        invw, corr = par[:, 72:74], par[:, 76:108].rearrange("p (i c) -> p i c", i=2)
        cT_hi = at("cT_hi", [P, S], F32R, CC)
        cT_lo = at("cT_lo", [P, S], F32R, CC + 4)
        c_nat = at("c_nat", [P, NT, P], F32, CC + 8)
        cT = at("cT", [P, S], F32, CC + 12)
        rlT = at("rlT", [P, 4, 256], F32, CC + 12)
        bias = at("bias", [P, sum(WIDTH)], F32, SC)
        iqT_hi = at("iqT_hi", [P, 2, 768], F32R, SC)
        iqT_lo = at("iqT_lo", [P, 2, 768], F32R, SC + 6)
        x_tok = at("x_tok", [P, NT, D], F32, R1)
        kvT = at("kvT", [P, S], F32, R1)
        sq = at("sq", [P, S], F32, R1 + 4)
        rstd_kv = at("rstd_kv", [P, S], F32, R1 + 8)
        iT = at("iT", [P, S], F32, R1 + 12)
        ikT_hi = at("ikT_hi", [P, S], F32R, R1 + 16.25)
        ikT_lo = at("ikT_lo", [P, S], F32R, R1 + 20.25)
        uT = at("uT", [P, 2, PAD_U + S], F32, R1)
        sums = at("sums", [P, 2, PAD_U + S], F32, R1 + 8.125)
        sig = at("sig", [P, 2, S], F32, R1 + 8.125)
        hpad = at("hpad", [P, 2, 1056], F32, R1 + 16.25)
        conv = at("conv", [P, 2, S], F32, R1 + 24.5)
        csq = at("csq", [P, 2, S], F32, R2 + 16)
        crstd = at("crstd", [P, S], F32, R2 + 24)
        probs = at("probs", [P, 4, S], F32, R1)
        stack_iq = at("stack_iq", [P, IHEADS, 768], F32R, R2)
        stack_ik = at("stack_ik", [P, S], F32R, R2 + 24)
        relu = at("relu", [P, 2, S], F32, R2 + 28)
        tapped = at("tapped", [P, S], F32, R2 + 32)
        above = at("above", [P, S], F32, R2 + 16)
        tied = at("tied", [P, S], F32, R2 + 20)
        tie_no = at("tie_no", [P, S], F32, R2 + 24)
        qT = at("qT", [P, 4, S], F32, R2)
        wuk_raw = at("wuk_raw", [P, HEADS, HD], F32, R2)
        doubled = [at(f"doubled{i}", [P, PAD_U + S], F32, R2 + 16 + 4.25 * i) for i in range(2)]
        xT_hi = at("xT_hi", [P, KT, S], F32R, R3)
        xT_lo = at("xT_lo", [P, KT, S], F32R, R3 + 32)
        w_raw = at("w_raw", [P, 2, KT, P], F32, R3 + 64)
        w_hi = at("w_hi", [P, 2, KT, P], F32R, R3 + 72)
        w_lo = at("w_lo", [P, 2, KT, P], F32R, R3 + 80)
        ql_hi = at("ql_hi", [P, HEADS, 512], F32R, R3)
        ql_lo = at("ql_lo", [P, HEADS, 512], F32R, R3 + 16)
        diag = at("diag", [P, TAPS, P], F32, R3 + 32)
        mix = at("mix", [P, KT, S], F32, R3 + 32)
        olat = at("olat", [P, 2, HEADS, 256], F32, R3 + 64)
        pT = at("pT", [P, 3, 512], F32, R3 + 80)
        rlrep = [at("rlrep0", [P, HEADS, HD], F32, R3 + 86), at("rlrep1", [P, HEADS, HD], F32, CST + 11)]
        mix_hi = at("mix_hi", [P, KT, S], F32R, R1)
        mix_lo = at("mix_lo", [P, KT, S], F32R, 96)
        wo_hi = [at("wo_hi0", [P, KT, 512], F32R, 128), at("wo_hi1", [P, KT, 512], F32R, 148)]
        wo_lo = [at("wo_lo0", [P, KT, 512], F32R, 180), at("wo_lo1", [P, KT, 512], F32R, 164)]
        wo_raw = at("wo_raw", [P, 4, 512], F32, SC)
        x_res = at("x_res", [P, 4, 512], F32, SC + 8)
        ln_g = at("ln_g", [P, D], F32, R3 + 80)
        ln_b = at("ln_b", [P, D], F32, R3 + 84)
        xa = at("xa", [P, 4, D], F32, CC)
        xb = at("xb", [P, 4, D], F32, R2)
        x1T = at("x1T", [P, KT, S], F32, R3)
        raw = at("raw", [P, 6, 4 * DE], F32, SC)
        whi = at("whi", [P, 6, 4 * DE], F32R, 96)
        wlo = at("wlo", [P, 6, 4 * DE], F32R, 144)
        xg = at("xg", [P, D], F32, 192)
        xgT_hi = at("xgT_hi", [P, KT, P], F32R, 196)
        xgT_lo = at("xgT_lo", [P, KT, P], F32R, 200)
        silu = at("silu", [P, DE], F32, CST + 0.5)
        hid = at("hid", [P, DE], F32, CST + 2.5)
        hT_hi = at("hT_hi", [P, FT, P], F32R, CST + 4.5)
        hT_lo = at("hT_lo", [P, FT, P], F32R, CST + 6.5)
        ysb = at("ysb", [P, D], F32, CST + 8.5)
        ln2_g = at("ln2_g", [P, D], F32, 112)
        ln2_b = at("ln2_b", [P, D], F32, 116)
        junk_act = at("junk_act", [P, S], BF16, END)
        sm = at("sm", [P, 432], F32, END + 2)
        iw = sm[:, 0:64].rearrange("p (t h) -> p t h", t=NT)
        lo, hi, cand, res, thr, low = (sm[:, 64 + 6 * i:70 + 6 * i] for i in range(6))
        top_score, cands, if_passed = sm[:, 272:278], (cand, sm[:, 278:284]), sm[:, 284:290]
        passed = at("passed", [P, 6], I32, END + 3.6875)
        need = sm[:, 100:106]
        negmax = sm[:, 106:170]
        rowsum = sm[:, 170:234]
        stats = sm[:, 234:246].rearrange("p (c s) -> p c s", c=2)
        mv = sm[:, 246:248]
        rstd = sm[:, 248:249]
        eps = sm[:, 249:250]
        shift = sm[:, 250:251]
        rbias = sm[:, 251:267]
        rw = sm[:, 290:418].rearrange("p (k e) -> p k e", k=KT)

        RT = 160
        rt = at("rt", [P, 1536], F32, RT)
        aff, score = rt[:, 16:144], rt[:, 144:272]
        pairs = rt[:, 272:464].rearrange("p (n c) -> p n c", c=6)
        gs, gv, first_g = rt[:, 464:496], rt[:, 496:528], rt[:, 528:560]
        w4, w16 = rt[:, 568:572], rt[:, 572:588]
        masked, pick, oh1, oh2 = (rt[:, 588 + 128 * i:716 + 128 * i] for i in range(4))
        top = rt[:, 1100:1108]
        ga, gb, gsum = rt[:, 1108:1116], rt[:, 1116:1124], rt[:, 1124:1132]
        slotf, rowf, colf = (rt[:, 1132 + 16 * i:1148 + 16 * i] for i in range(3))
        place_no, tile_no = rt[:, 1180:1308], rt[:, 1308:1308 + TILES + 1]
        token_of, gate_of = rt[:, 1340:1356], rt[:, 1356:1372]
        slot_row = at("slot_row", [P, 2 * NT, P], F32, 192)
        slot_col = at("slot_col", [P, 2 * NT, TILES + 1, 2], F32, 200)
        lgT = at("lgT", [EXPERTS, S], F32, RT + 7)
        mT = at("mT", [EXPERTS, S], F32, RT + 11)
        rank = at("rank", [EXPERTS, S], F32, RT + 15)
        rk = at("rk", [P, 224], F32, RT + 19)
        ones_row = at("ones_row", [EXPERTS, S], F32, RT + 20)
        thr8, upper, tcol = rk[0:16, 0:8], rk[0:16, 8:24], rk[0:16, 24:56]
        ntile, cum, slot0, cmp = rk[0:16, 56:57], rk[0:16, 57:58], rk[0:16, 58:59], rk[0:16, 64:96]
        ones16 = rk[0:16, 59:60]
        expert_row, live_row, fresh_row, loads_row = (rk[0:1, 96 + 32 * i:96 + 32 * i + TILES + 1] for i in range(4))
        tiles_used = rk[0:1, 60:61]
        ri = at("ri", [P, 88], I32, CST + 12.5)
        slot_i, row_i, col_i = (ri[:, 16 * i:16 * i + 16] for i in range(3))
        tile_row = at("tile_row", [1, 128], I32, END + 0.75)
        expert_of, fresh_of, loads_of = (tile_row[:, 32 * i:32 * i + TILES + 1] for i in range(3))
        last_tile = tile_row[:, 96:97]
        slot_token = at("slot_token", [P, TILES + 1], I32, END)
        slot_gate = at("slot_gate", [P, TILES + 1], F32, END + 0.125)
        idx_now = at("idx_now", [P, 1], I32, END + 0.25)

        ps = ctx.enter_context(nc.psum_tensor("ps", [P, 8, 512], F32))

        def pair(i):
            return ps[:, 2 * i:2 * i + 2, :].rearrange("p b n -> p (b n)")

        def scores_at(u, width):
            return (ps[:, u % 4, :] if u < 2 * SHORT_PAIRS else pair(u % 2))[:, 0:width]

        def probs_at(u):
            return probs[:, (u % 8) // 2, (u % 2) * 512:(u % 2) * 512 + 512] if u < 2 * SHORT_PAIRS else probs[:, u % 4, :]

        x1_d = nc.dram_tensor("x1_d", (S, D), F32, kind="Internal").ap()
        y_d = nc.dram_tensor("y_d", (TILES * P, D), F32, kind="Internal").ap()

        par_in, wuk_in, wuv_in, wpool_in = sem("par_in"), sem("wuk_in"), sem("wuv_in"), sem("wpool_in")
        x_in = [sem(f"x_in{i}") for i in range(NT)]
        w_in_s = [sem(f"w_in{i}") for i in range(2)]
        ident_set, zeros_set, dve_set = sem("ident_set"), sem("zeros_set"), sem("dve_set")
        x_tr, x_hi, x_lo, w_hi_s, w_lo_s = (sem(n) for n in ("x_tr", "x_hi", "x_lo", "w_hi_s", "w_lo_s"))
        wuk_tr, wuk_set = sem("wuk_tr"), sem("wuk_set")
        unit_mm, unit_act, unit_dve = sem("unit_mm"), sem("unit_act"), sem("unit_dve")
        kv_sq, kv_norm, c_hi, c_lo = (sem(n) for n in ("kv_sq", "kv_norm", "c_hi", "c_lo"))
        ik_hi, ik_lo, stack_in = sem("ik_hi"), sem("ik_lo"), sem("stack_in")
        idx_mm, idx_relu, idx_sum = sem("idx_mm"), sem("idx_relu"), sem("idx_sum")
        bound, masked_s, cand_set = sem("bound"), sem("masked_s"), sem("cand_set")
        counted_dve, counted_act, dve_chain = sem("counted_dve"), sem("counted_act"), sem("dve_chain")
        tri_set, pads_set = sem("tri_set"), sem("pads_set")
        diag_set, conv0_mm, conv0, conv1, conv1_mul, pooled, pool_chain = (
            sem(n) for n in ("diag_set", "conv0_mm", "conv0", "conv1", "conv1_mul", "pooled", "pool_chain"))
        ring_mm, ring_act, ring_dve = sem("ring_mm"), sem("ring_act"), sem("ring_dve")
        qk_mm, masked_max, exped, rl_set = sem("qk_mm"), sem("masked_max"), sem("exped"), sem("rl_set")
        pv_mm, olat_set = sem("pv_mm"), sem("olat_set")
        conv_c, conv_sq, conv_n, conv_y = (sem(n) for n in ("conv_c", "conv_sq", "conv_n", "conv_y"))
        mix_hi_s, mix_lo_s = sem("mix_hi_s"), sem("mix_lo_s")
        wo_in = [sem(f"wo_in{i}") for i in range(4)]
        xr_in = [sem(f"xr_in{i}") for i in range(4)]
        ln_in, wo_hi_s, wo_lo_s, wo_mm = sem("ln_in"), sem("wo_hi_s"), sem("wo_lo_s"), sem("wo_mm")
        y1_set, stat, ln_sd, ln_scaled, x1_set = (sem(n) for n in ("y1_set", "stat", "ln_sd", "ln_scaled", "x1_set"))
        x1_tr, x1T_set, x1_out = sem("x1_tr"), sem("x1T_set"), sem("x1_out")
        route_in, lg_mm, lgT_set, lg_tr, aff_set = (sem(n) for n in ("route_in", "lg_mm", "lgT_set", "lg_tr", "aff_set"))
        oh_set, m_tr, ntile_set = (sem(n) for n in ("oh_set", "m_tr", "ntile_set"))
        cum_mm, slotT_set, cmp_set, te_mm, s_tr = (sem(n) for n in ("cum_mm", "slotT_set", "cmp_set", "te_mm", "s_tr"))
        experts_set, places_set, rconst = sem("experts_set"), sem("places_set"), sem("rconst")
        hot_set, table_mm, table_set, idx0_set = (sem(n) for n in ("hot_set", "table_mm", "table_set", "idx0_set"))
        raw_in = [sem(f"raw_in{i}") for i in range(6)]
        idx_set, xg_in, xg_tr, xgT_hi_s, xgT_lo_s = (sem(n) for n in ("idx_set", "xg_in", "xg_tr", "xgT_hi_s", "xgT_lo_s"))
        gu_hi, gu_lo, dn_hi, dn_lo = (sem(n) for n in ("gu_hi", "gu_lo", "dn_hi", "dn_lo"))
        gu_used, dn_used = sem("gu_used"), sem("dn_used")
        silu_set, hid_set, h_tr, hT_hi_s, hT_lo_s = (sem(n) for n in ("silu_set", "hid_set", "h_tr", "hT_hi_s", "hT_lo_s"))
        y_filled, y_set, y_out, experts_done = sem("y_filled"), sem("y_set"), sem("y_out"), sem("experts_done")
        y_added = [sem(f"y_added{i}") for i in range(NT)]
        ln_shift, ln_unit = sem("ln_shift"), sem("ln_unit")
        ln2_in, x1_scaled, fin_done, out_done = (sem(n) for n in ("ln2_in", "x1_scaled", "fin_done", "out_done"))

        def f32(t):
            return t.bitcast(F32)

        def three(pe, out, l_hi, l_lo, r_hi, r_lo, start, stop):
            pe.matmul(out, l_hi, r_hi, start=start, stop=False)
            pe.matmul(out, l_hi, r_lo, start=False, stop=False)
            return pe.matmul(out, l_lo, r_hi, start=False, stop=stop)

        def x1_tile(t):
            return xa[:, t, :] if t < 4 else xb[:, t - 4, :]

        N_UNITS = len(UNITS)
        POOL_UNITS = seen(BY_ACT, UNITS.index(("pool1", 1, [c[0] for c in COLS].index("pool1"))))
        LATER = [k for k, u in enumerate(UNITS) if u[0] == "gate0"][0]

        def plan():
            u = 0
            for k, (name, _, j) in enumerate(UNITS):
                n = 0 if k < LATER + IDX_FROM else IDX_PER_UNIT if j is not None else 1
                yield k, range(u, min(u + n, len(IDX)))
                u = min(u + n, len(IDX))
        PLAN = list(plan())
        LAST_IDX = max(i for i, p in enumerate(PLAN) if len(p[1]))

        block = ctx.enter_context(nc.Block())

        @block.sync
        def _(sp):
            def w_tile(j):
                if j >= 2:
                    sp.wait_ge(w_lo_s, j - 1)
                c = COLS[j][1]
                sp.dma_start(w_raw[:, j % 2], a["w_in"][0].rearrange("(k p) n -> p k n", p=P)[:, :, c:c + P]
                             ).then_inc(w_in_s[j % 2], 16)

            for t in range(NT):
                sp.dma_start(x_tok[:, t], a["x"][0, t * P:(t + 1) * P, :]).then_inc(x_in[t], 16)
                if t in (3, 7):
                    w_tile(t // 4)
            with nc.allow_non_contiguous_dma(reason="small parameters, one element to a partition"):
                sp.dma_start(kvg, a["kv_norm_g"][0].rearrange("(p o) -> p o", o=1)).then_inc(par_in, 16)
                sp.dma_start(pscale, a["pool_scale"][0].rearrange("(i p) -> p i", p=P)).then_inc(par_in, 16)
                for i in range(2):
                    sp.dma_start(convw[:, i * TAPS:(i + 1) * TAPS],
                                 a["conv_w"][0, :, 0, i * P:(i + 1) * P].rearrange("w p -> p w")).then_inc(par_in, 16)
                sp.dma_start(convb, a["conv_b"][0].rearrange("(i p) -> p i", p=P)).then_inc(par_in, 16)
                sp.dma_start(cvg, a["conv_ln_g"][0].rearrange("(i p) -> p i", p=P)).then_inc(par_in, 16)
                sp.dma_start(cvb, a["conv_ln_b"][0].rearrange("(i p) -> p i", p=P)).then_inc(par_in, 16)
            sp.dma_start(wuk_raw[:], a["w_uk"][0].rearrange("h r d -> r h d")).then_inc(wuk_in, 16)
            sp.wait_ge(zeros_set, 2)
            for h in range(2):
                sp.dma_start(wuv[:, h::2, h * HD:(h + 1) * HD], a["w_uv"][0, h::2].rearrange("h r d -> r h d")
                             ).then_inc(wuv_in, 16)
                sp.dma_start(wpool[h * HD:(h + 1) * HD, :, h * HD:(h + 1) * HD],
                              a["w_pool"][0, h::2].rearrange("g c d -> c g d")).then_inc(wpool_in, 16)
            sp.dma_start(rbias, a["router_bias"].partition_broadcast(P)).then_inc(route_in, 16)
            sp.dma_start(rw, a["router_w"].rearrange("(k p) e -> p k e", p=P)).then_inc(route_in, 16)
            for j in range(2, 6):
                w_tile(j)
            sp.wait_ge(unit_dve, seen(BY_DVE, UNITS.index(("iq1", 1, 3))))
            sp.wait_ge(ik_lo, 1)
            for part in range(4):
                rows = slice(part * IDIM, (part + 1) * IDIM)
                src = iqT_hi if part < 2 else iqT_lo
                for h4 in range(4):
                    sp.dma_start(f32(stack_iq[rows]).rearrange("p (i h) n -> p i h n", i=2)[:, :, h4, :],
                                 f32(src[h4 * IDIM:(h4 + 1) * IDIM, :, :])).then_inc(stack_in, 16)
                sp.dma_start(f32(stack_ik[rows, :]), f32((ikT_lo if part % 2 else ikT_hi)[0:IDIM, :])
                             ).then_inc(stack_in, 16)
            for j in range(6, len(COLS)):
                w_tile(j)
            for r0 in range(MIN_TILES * P, TILES * P, S):
                n = min(S, TILES * P - r0)
                sp.dma_start(y_d[r0:r0 + n, :], a["x"][0, 0:n, :]).then_inc(y_filled, 16)
            sp.wait_ge(masked_max, NT * HEADS)
            for hf in range(2):
                for k in range(KT):
                    n = hf * KT + k
                    if n >= 4:
                        sp.wait_ge(wo_lo_s, n - 3)
                    kk = MIX_ORDER[k]
                    sp.dma_start(wo_raw[:, n % 4], a["w_o"][0, kk * P:(kk + 1) * P, hf * 512:(hf + 1) * 512]
                                 ).then_inc(wo_in[n % 4], 16)
            for hf in range(2):
                for t in range(NT):
                    n = hf * NT + t
                    if n >= 4:
                        sp.wait_ge(y1_set, n - 3)
                    sp.dma_start(x_res[:, n % 4], a["x"][0, t * P:(t + 1) * P, hf * 512:(hf + 1) * 512]
                                 ).then_inc(xr_in[n % 4], 16)
            for t in range(NT):
                sp.wait_ge(x1_set, t + 1)
                sp.dma_start(x1_d[t * P:(t + 1) * P, :], x1_tile(t)).then_inc(x1_out, 16)
            sp.wait_ge(experts_set, 1)

            def expert(t):
                return sp.value_load(expert_of[0:1, bass.ds(t, 1)], min_val=0, max_val=EXPERTS - 1)

            def gate_up(e, loaded):
                for n, (w, half) in enumerate((("w_gate", 0), ("w_up", 0), ("w_gate", 1), ("w_up", 1))):
                    if loaded is not None:
                        sp.wait_ge(gu_lo, loaded * 4 + (n + 1))
                    src = a[w][0].rearrange("e (p k) n -> e p (k n)", p=P)[
                        bass.ds(e, 1), :, half * 4 * DE:(half + 1) * 4 * DE]
                    sp.dma_start(raw[:, n, :], src.rearrange("e p n -> (e p) n")).then_inc(raw_in[n], 16)

            def down(e, loaded):
                for n in range(2):
                    if loaded is not None:
                        sp.wait_ge(dn_lo, loaded * 2 + (n + 1))
                    src = a["w_down"][0].rearrange("e (p k) n -> e p (k n)", p=P)[
                        bass.ds(e, 1), :, n * 4 * DE:(n + 1) * 4 * DE]
                    sp.dma_start(raw[:, 4 + n, :], src.rearrange("e p n -> (e p) n")).then_inc(raw_in[4 + n], 16)

            def if_fresh(t, load):
                fresh = sp.value_load(fresh_of[0:1, bass.ds(t, 1)], min_val=0, max_val=1)
                with sp.If(fresh == 1):
                    load(expert(t), sp.value_load(loads_of[0:1, bass.ds(t - 1, 1)], min_val=0, max_val=EXPERTS - 1))

            e = expert(0)
            gate_up(e, None)
            if_fresh(1, gate_up)
            down(e, None)
            with sp.Fori(2, TILES) as t:
                if_fresh(t, gate_up)
                if_fresh(t - 1, down)
            if_fresh(TILES - 1, down)
            sp.wait_ge(experts_done, 1)
            sp.dma_start(ln2_g[:], a["ln2_g"][0].partition_broadcast(P)).then_inc(ln2_in, 16)
            sp.dma_start(ln2_b[:], a["ln2_b"][0].partition_broadcast(P)).then_inc(ln2_in, 16)
            for t in range(NT):
                sp.wait_ge(fin_done, t + 1)
                sp.dma_start(a["out"][0, t * P:(t + 1) * P, :], x1_tile(t)).then_inc(out_done, 16)
            sp.wait_ge(out_done, 16 * NT)

        @block.tensor
        def _(pe):
            pe.wait_ge(ident_set, 2)

            def bank_free(k):
                if k >= 4:
                    if seen(BY_ACT, k - 4):
                        pe.wait_ge(unit_act, seen(BY_ACT, k - 4))
                    if seen(BY_DVE, k - 4):
                        pe.wait_ge(unit_dve, seen(BY_DVE, k - 4))

            def unit(k, between):
                name, i, j = UNITS[k]
                out = ps[:, 4 + k % 4, :]
                bank_free(k)
                scores = list(between)
                if j is not None:
                    t0, n = COLS[j][2][i]
                    pe.wait_ge(w_lo_s, j + 1)
                    for kk in range(KT):
                        last = three(pe, out[:, 0:n], w_hi[:, j % 2, kk, :], w_lo[:, j % 2, kk, :],
                                     xT_hi[:, kk, t0:t0 + n], xT_lo[:, kk, t0:t0 + n], kk == 0, kk == KT - 1)
                        if scores and kk < KT - 1 and (kk + 1) * len(between) // KT > kk * len(between) // KT:
                            index(scores.pop(0))
                elif name == "ms":
                    pe.wait_ge(kv_sq, 2)
                    last = pe.matmul(out, ones_rank[:], sq[:, i * 512:(i + 1) * 512], start=True, stop=True)
                elif name == "cT":
                    pe.wait_ge(kv_norm, 2 + 2)
                    for t in range(4):
                        c = (4 * i + t) * P
                        last = pe.transpose(out[:, t * P:(t + 1) * P], cT[:, c:c + P], ident[:])
                elif name == "iwT":
                    for t in range(4):
                        c = (4 * i + t) * P
                        last = pe.transpose(out[:, t * P:(t + 1) * P], iT[:, c:c + P], ident[:])
                for u in scores:
                    index(u)
                last.then_inc(unit_mm, 1)

            def index(u):
                b, h = IDX[u]
                if u == 0:
                    pe.wait_ge(stack_in, 16 * 20)
                    pe.wait_ge(wuk_set, 8)
                if u >= 2:
                    pe.wait_ge(idx_relu, u - 1)
                for c in range(0, WIDTH[b], 512):
                    n = min(512, WIDTH[b] - c)
                    last = pe.matmul(pair(u % 2)[:, c:c + n], stack_iq[:, h, (b - 2) * P:(b - 1) * P],
                                     stack_ik[:, c:c + n], start=True, stop=True)
                last.then_inc(idx_mm, 1)
            for g in range(2 * NT):
                t, half = divmod(g, 2)
                if g == NT:
                    pe.wait_ge(x_lo, NT)
                    unit(0, ())
                if half == 0:
                    pe.wait_ge(x_in[t], 16)
                if g >= 4:
                    pe.wait_ge(x_lo, g - 3)
                for k in range(4):
                    kk = half * 4 + k
                    last = pe.transpose(ps[:, g % 4, k * P:(k + 1) * P], x_tok[:, t, kk * P:(kk + 1) * P], ident[:])
                last.then_inc(x_tr, 1)
            pe.wait_ge(wuk_in, 16)
            pe.wait_ge(x_lo, 2 * NT)
            for j in range(4):
                last = pe.transpose(ps[:, 0, j * P:(j + 1) * P],
                                    wuk_raw[:, 2 * j:2 * j + 2, :].rearrange("p h d -> p (h d)"), ident[:])
            last.then_inc(wuk_tr, 1)
            pe.wait_ge(dve_set, 1)

            for k, between in PLAN[1:]:
                unit(k, between)

            pe.wait_ge(unit_act, sum(BY_ACT))
            pe.wait_ge(unit_dve, sum(BY_DVE))
            pe.wait_ge(idx_relu, len(IDX))
            pe.wait_ge(pads_set, 1)
            for w in range(TAPS):
                pe.wait_ge(diag_set, w + 1)
                for c in range(2):
                    last = pe.matmul(ps[:, 4 + c, :], diag[:, w, :], hpad[:, 0, c * 512 + w:c * 512 + w + 512],
                                     start=w == 0, stop=w == TAPS - 1)
            last.then_inc(conv0_mm, 1)

            for step in STEPS:
                kind = step[0]
                if kind in RING:
                    r = step[-1]
                    out = ps[:, 4 + r % 3, :]
                    if r < 2:
                        pe.wait_ge(conv0, 1)
                    if r >= 3:
                        if seen(RING_ACT, r - 3):
                            pe.wait_ge(ring_act, seen(RING_ACT, r - 3))
                        if seen(RING_DVE, r - 3):
                            pe.wait_ge(ring_dve, seen(RING_DVE, r - 3))
                if kind == "ql":
                    _, half, h, r = step
                    pe.matmul(out, wuk[:, h, :], qT[:, h // 2, half * 512:(half + 1) * 512],
                              start=True, stop=True).then_inc(ring_mm, 1)
                elif kind == "qk":
                    _, b, h = step
                    u = score_no(b, h)
                    if u >= 4:
                        pe.wait_ge(masked_max, u - 3 if u < 2 * SHORT_PAIRS else u - 1)
                    pe.wait_ge(ring_dve, seen(RING_DVE, RING_OF["ql", b // 4, h]))
                    q0 = (b % 4) * P
                    for c in range(0, WIDTH[b], 512):
                        n = min(512, WIDTH[b] - c)
                        last = three(pe, scores_at(u, WIDTH[b])[:, c:c + n], ql_hi[:, h, q0:q0 + P], ql_lo[:, h, q0:q0 + P],
                                     cT_hi[:, c:c + n], cT_lo[:, c:c + n], True, True)
                    last.then_inc(qk_mm, 1)
                elif kind == "pt":
                    _, b, j, n, r = step
                    pe.wait_ge(exped, score_no(b, 2 * j + 1) + 1)
                    for k in range(2 * n, min(2 * n + 2, b + 1)):
                        for h in range(2):
                            c = (k - 2 * n) * 256 + h * P
                            last = pe.transpose(out[:, c:c + P],
                                                probs_at(score_no(b, 2 * j + h))[:, k * P:(k + 1) * P], ident[:])
                    last.then_inc(ring_mm, 1)
                elif kind == "pv":
                    _, b, j, n = step
                    acc = ps[:, 7, 0:256]
                    if n == 0 and PAIR_NO[b, j]:
                        pe.wait_ge(olat_set, PAIR_NO[b, j])
                    r = RING_OF["pt", b, j, n]
                    if RING_ACT[r]:
                        pe.wait_ge(ring_act, seen(RING_ACT, r))
                    else:
                        pe.wait_ge(ring_dve, seen(RING_DVE, r))
                    for k in range(2 * n, min(2 * n + 2, b + 1)):
                        c = (k - 2 * n) * 256
                        last = pe.matmul(acc, c_nat[:, k, :], pT[:, PT_NO[b, j, n] % 3, c:c + 256],
                                         start=k == 0, stop=k == b)
                    last.then_inc(pv_mm, 1)
                elif kind == "rl":
                    _, b, r = step
                    pe.wait_ge(rl_set, b + 1)
                    for j in range(4):
                        last = pe.transpose(out[:, j * P:(j + 1) * P],
                                            rlrep[b % 2][:, 2 * j:2 * j + 2, :].rearrange("p h d -> p (h d)"), ident[:])
                    last.then_inc(ring_mm, 1)
                elif kind == "uv":
                    _, q, j, r = step
                    if j == 0:
                        pe.wait_ge(olat_set, last_no(2 * q, 2 * q + 1) + 1)
                        pe.wait_ge(wuv_in, 32)
                    for h in range(2):
                        last = pe.matmul(out[:, 0:256], wuv[:, 2 * j + h, :], olat[:, q % 2, 2 * j + h, :],
                                         start=h == 0, stop=h == 1)
                    last.then_inc(ring_mm, 1)
                elif kind == "pw":
                    _, i, c, r = step
                    pe.wait_ge(pooled, 4)
                    pe.wait_ge(wpool_in, 32)
                    pe.matmul(out, wpool[:, i, :], sums[:, i, PAD_U + c * 512:PAD_U + (c + 1) * 512],
                              start=True, stop=True).then_inc(ring_mm, 1)
                elif kind in ("cm", "cv"):
                    _, c, r = step
                    if kind == "cm":
                        pe.wait_ge(conv0, 1)
                        pe.wait_ge(conv1, TAPS)
                    else:
                        pe.wait_ge(conv_sq, 2 * c + 2)
                    src = conv if kind == "cm" else csq
                    for i in range(2):
                        last = pe.matmul(out, ones_conv[:], src[:, i, c * 512:(c + 1) * 512], start=i == 0, stop=i == 1)
                    last.then_inc(ring_mm, 1)

            pe.wait_ge(olat_set, 4 * NT)
            pe.wait_ge(ring_act, sum(RING_ACT))
            pe.wait_ge(ring_dve, sum(RING_DVE))
            for n in range(2 * NT):
                hf, t = divmod(n, NT)
                if n >= 8:
                    pe.wait_ge(y1_set, n - 7)
                for i, k in enumerate(MIX_ORDER):
                    if t == 0:
                        pe.wait_ge(wo_lo_s, hf * KT + i + 1)
                        if hf == 0:
                            pe.wait_ge(mix_lo_s, i + 1)
                    last = three(pe, ps[:, n % 8, :], mix_hi[:, k, t * P:(t + 1) * P], mix_lo[:, k, t * P:(t + 1) * P],
                                 wo_hi[hf][:, k, :], wo_lo[hf][:, k, :], i == 0, i == KT - 1)
                last.then_inc(wo_mm, 1)

            pe.wait_ge(y1_set, NT + 4)
            def logits(c):
                pe.wait_ge(x1T_set, 8 * c + 8)
                pe.wait_ge(route_in, 32)
                pe.wait_ge(y1_set, 2 * NT)
                for k in range(KT):
                    last = pe.matmul(ps[0:EXPERTS, 4 + c, :], rw[:, k, :], x1T[:, k, c * 512:(c + 1) * 512],
                                     start=k == 0, stop=k == KT - 1)
                last.then_inc(lg_mm, 1)

            for g in range(2 * NT):
                t, half = divmod(g, 2)
                if half == 0:
                    pe.wait_ge(x1_set, t + 1)
                if g >= 4:
                    pe.wait_ge(x1T_set, g - 3)
                for k in range(4):
                    kk = half * 4 + k
                    last = pe.transpose(ps[:, g % 4, k * P:(k + 1) * P], x1_tile(t)[:, kk * P:(kk + 1) * P], ident[:])
                last.then_inc(x1_tr, 1)
                if g == NT + 1:
                    logits(0)
            logits(1)
            pe.wait_ge(lgT_set, 2)
            for t in range(NT):
                last = pe.transpose(ps[:, 6, t * 16:(t + 1) * 16], lgT[:, t * P:(t + 1) * P], ident[0:16, 0:16])
            last.then_inc(lg_tr, 1)
            pe.wait_ge(oh_set, 1)
            for t in range(NT):
                last = pe.transpose(pair(0)[0:16, t * P:(t + 1) * P], pick[:, t * 16:(t + 1) * 16], ident[:])
            last.then_inc(m_tr, 1)
            pe.wait_ge(ntile_set, 1)
            pe.wait_ge(rconst, 4)
            pe.matmul(ps[0:16, 4, 0:1], upper, ntile, start=True, stop=True).then_inc(cum_mm, 1)
            pe.wait_ge(cmp_set, 1)
            pe.matmul(ps[0:1, 5, 0:TILES + 1], ones16, cmp, start=True, stop=True).then_inc(te_mm, 1)
            pe.wait_ge(slotT_set, 1)
            for t in range(NT):
                last = pe.transpose(ps[:, 7, t * 16:(t + 1) * 16], rank[:, t * P:(t + 1) * P], ident[0:16, 0:16])
            last.then_inc(s_tr, 1)
            pe.wait_ge(hot_set, 1)
            for n in range(2 * NT):
                last = pe.matmul(ps[:, 6, 0:2 * (TILES + 1)], slot_row[:, n, :],
                                 slot_col[:, n].rearrange("p t c -> p (t c)"), start=n == 0, stop=n == 2 * NT - 1)
            last.then_inc(table_mm, 1)

            def xgT(t):
                pe.wait_ge(xg_in, t * 16 + 16)
                for k in range(KT):
                    last = pe.transpose(pair(2)[:, k * P:(k + 1) * P], xg[:, k::KT], ident[:])
                last.then_inc(xg_tr, 1)

            def loads(t):
                return pe.value_load(loads_of[0:1, bass.ds(t, 1)], min_val=0, max_val=EXPERTS - 1)

            def gate_up(t, loaded):
                pe.wait_ge(xgT_lo_s, t + 1)
                for n in range(4):
                    out = ps[:, n % 2, :]
                    pe.wait_ge(gu_lo, loaded * 4 + (n + 1))
                    for k in range(4):
                        kk = 4 * (n // 2) + k
                        last = three(pe, out, xgT_hi[:, kk, :], xgT_lo[:, kk, :], whi[:, n, k * DE:(k + 1) * DE],
                                     wlo[:, n, k * DE:(k + 1) * DE], kk == 0, kk == KT - 1)
                    last.then_inc(gu_used, 1)

            def down(t, loaded):
                pe.wait_ge(hT_lo_s, t + 1)
                if not (isinstance(t, int) and t == 0):
                    pe.wait_ge(y_set, t)
                for n in range(2):
                    pe.wait_ge(dn_lo, loaded * 2 + (n + 1))
                    for k in range(2):
                        for c in range(2):
                            col = k * D + c * 512
                            ft = 2 * n + k
                            last = three(pe, pair(1)[:, c * 512:(c + 1) * 512], hT_hi[:, ft, :], hT_lo[:, ft, :],
                                         whi[:, 4 + n, col:col + 512], wlo[:, 4 + n, col:col + 512],
                                         ft == 0, ft == FT - 1)
                    last.then_inc(dn_used, 1)

            def hidT(t):
                pe.wait_ge(hid_set, t + 1)
                for f in range(FT):
                    last = pe.transpose(ps[:, 6, f * P:(f + 1) * P], hid[:, f::FT], ident[:])
                last.then_inc(h_tr, 1)

            pe.wait_ge(table_set, 1)
            last_t = pe.value_load(last_tile, min_val=MIN_TILES - 1, max_val=TILES - 1)
            xgT(0)
            gate_up(0, 0)
            xgT(1)
            hidT(0)

            def tile(t):
                gate_up(t, loads(t))
                xgT(t + 1)
                down(t - 1, loads(t - 1))
                hidT(t)

            tile(1)
            with pe.Fori(2, TILES) as t:
                with pe.If(t <= last_t):
                    tile(t)
            down(last_t, loads(last_t))

        @block.scalar
        def _(act):
            def w_split(j):
                act.wait_ge(w_in_s[j % 2], 16 * (j // 2 + 1))
                if j >= 2:
                    act.wait_ge(unit_mm, max(k for k, u in enumerate(UNITS) if u[2] == j - 2) + 1)
                act.copy(w_hi[:, j % 2], w_raw[:, j % 2]).then_inc(w_hi_s, 1)

            for g in range(2 * NT):
                t, half = divmod(g, 2)
                if g == NT:
                    w_split(0)
                act.wait_ge(x_tr, g + 1)
                act.copy(xT_hi[:, half * 4:half * 4 + 4, t * P:(t + 1) * P],
                         ps[:, g % 4, :].rearrange("p (k n) -> p k n", k=4)).then_inc(x_hi, 1)

            def unit(k):
                name, i, j = UNITS[k]
                if not BY_ACT[k]:
                    return
                src = ps[:, 4 + k % 4, :]
                act.wait_ge(unit_mm, k + 1)
                t0, n = COLS[j][2][i] if j is not None else (i * 512, 512)
                tok = slice(t0, t0 + n)
                if name == "kv":
                    if i == 0:
                        act.wait_ge(x_tr, 2 * NT)
                    act.activation(sq[:, tok], src, ACT.Square).then_inc(kv_sq, 1)
                    act.copy(kvT[:, tok], src).then_inc(unit_act, 1)
                elif name == "ikw":
                    act.copy(iT[:, tok], src).then_inc(unit_act, 1)
                    if i == 1:
                        act.wait_ge(unit_act, seen(BY_ACT, k))
                        act.copy(ikT_hi[0:IDIM, :], iT[0:IDIM, :]).then_inc(ik_hi, 1)
                elif name[:2] == "iq":
                    act.copy(iqT_hi[:, int(name[2]), t0 - 256:t0 - 256 + n], src[:, 0:n]).then_inc(unit_act, 1)
                elif name == "ms":
                    act.activation(rstd_kv[:, tok], src, ACT.Sqrt, bias=eps).then_inc(unit_act, 1)
                elif name == "cT":
                    act.copy(c_nat[:, 4 * i:4 * i + 4, :].rearrange("p t r -> p (t r)"), src).then_inc(unit_act, 1)
                    if i == 1:
                        act.copy(cT_hi[:], cT[:]).then_inc(c_hi, 1)
                elif name[:4] == "gate":
                    if name == "gate0" and i == 0:
                        act.wait_ge(kv_norm, 4)
                        act.wait_ge(unit_mm, UNITS.index(("iwT", 1, None)) + 1)
                        act.wait_ge(ik_lo, 1)
                    act.activation(sig[:, int(name[4]), tok], src, ACT.Sigmoid).then_inc(unit_act, 1)
                elif name[:4] == "pool":
                    if name == "pool0" and i == 0:
                        act.wait_ge(c_hi, 1)
                        act.wait_ge(c_lo, 1)
                    act.copy(uT[:, int(name[4]), PAD_U + t0:PAD_U + t0 + n], src).then_inc(unit_act, 1)
                elif name[0] == "q":
                    act.copy(qT[:, int(name[1]), tok], src).then_inc(unit_act, 1)

            def index(u):
                b, h = IDX[u]
                act.wait_ge(idx_mm, u + 1)
                if u >= 2:
                    act.wait_ge(idx_sum, u - 1)
                act.activation(relu[:, u % 2, 0:WIDTH[b]], pair(u % 2)[:, 0:WIDTH[b]], ACT.Relu).then_inc(idx_relu, 1)

            def item(k, between):
                _, i, j = UNITS[k]
                if j is not None and i == 0 and j + 1 < len(COLS):
                    w_split(j + 1)
                for u in between:
                    index(u)
                unit(k)

            for p in PLAN[:LAST_IDX + 1]:
                item(*p)
            rest = PLAN[LAST_IDX + 1:]

            def count(r):
                act.wait_ge(cand_set, r + 1)
                for i, b in enumerate(COUNT_ACT):
                    c = COLUMN[b]
                    if r + i:
                        act.wait_ge(counted_act, len(COUNT_ACT) * r + i)
                    act.activation(junk_act[:, 0:WIDTH[b]], bias[:, AT[b]:AT[b] + WIDTH[b]], ACT.Sign,
                                   bias=cands[r % 2][:, c:c + 1], scale=-1.0, accum_out=res[:, c:c + 1]
                                   ).then_inc(counted_act, 1)

            act.wait_ge(masked_s, len(BLOCKS))
            for r in range(ROUNDS):
                count(r)
                if rest:
                    item(*rest.pop(0))
            for p in rest:
                item(*p)

            act.wait_ge(conv0_mm, 1)
            act.activation(conv[:, 0, :], pair(2), ACT.Identity, bias=convb[:, 0:1]).then_inc(conv0, 1)

            for step in STEPS:
                kind = step[0]
                if kind in RING:
                    r = step[-1]
                    src = ps[:, 4 + r % 3, :]
                    if not RING_ACT[r]:
                        continue
                    act.wait_ge(ring_mm, r + 1)
                if kind == "ql":
                    _, half, h, r = step
                    act.copy(ql_hi[:, h, :], src).then_inc(ring_act, 1)
                elif kind == "qk":
                    _, b, h = step
                    u = score_no(b, h)
                    c = b * HEADS + h
                    act.wait_ge(masked_max, u + 1)
                    row = probs_at(u)[:, 0:WIDTH[b]]
                    act.activation(row, row, ACT.Exp,
                                   bias=negmax[:, c:c + 1], scale=-1.0, accum_out=rowsum[:, c:c + 1]).then_inc(exped, 1)
                elif kind == "pt":
                    _, b, j, n, r = step
                    no = PT_NO[b, j, n]
                    if no >= 3:
                        act.wait_ge(pv_mm, no - 2)
                    w = 256 * (min(2 * n + 2, b + 1) - 2 * n)
                    act.copy(pT[:, no % 3, 0:w], src[:, 0:w]).then_inc(ring_act, 1)
                elif kind == "pv" and step[3] == step[1] // 2:
                    _, b, j, n = step
                    q = b // 2
                    act.wait_ge(pv_mm, PT_NO[b, j, n] + 1)
                    if q >= 2:
                        act.wait_ge(ring_mm, RING_OF["uv", q - 2, 3] + 1)
                    act.copy(olat[:, q % 2, 2 * j:2 * j + 2, (b % 2) * P:(b % 2) * P + P],
                             ps[:, 7, 0:256].rearrange("p (h n) -> p h n", h=2)
                             ).then_inc(olat_set, 1)
                elif kind == "rl":
                    _, b, r = step
                    if b >= 2:
                        act.wait_ge(ring_dve, seen(RING_DVE, RING_OF["uv", b // 2 - 1, 3]))
                    act.copy(rlT[:, :, (b % 2) * P:(b % 2) * P + P],
                             src.rearrange("p (j n) -> p j n", j=4)).then_inc(ring_act, 1)
                elif kind == "pw":
                    _, i, c, r = step
                    act.activation(mix[:, 4 + i, c * 512:(c + 1) * 512], src, ACT.Copy, scale=pscale[:, i:i + 1]
                                   ).then_inc(ring_act, 1)
                elif kind == "csq":
                    _, c = step
                    act.wait_ge(ring_dve, seen(RING_DVE, RING_OF["cm", c]))
                    for i in range(2):
                        act.activation(csq[:, i, c * 512:(c + 1) * 512], conv[:, i, c * 512:(c + 1) * 512], ACT.Square
                                       ).then_inc(conv_sq, 1)
                elif kind == "cv":
                    _, c, r = step
                    act.activation(crstd[:, c * 512:(c + 1) * 512], src, ACT.Sqrt, bias=eps).then_inc(ring_act, 1)
                elif kind == "cn":
                    for i in range(2):
                        act.wait_ge(conv_n, 4 + i + 1)
                        act.activation(mix[:, 6 + i, :], conv[:, i, :], ACT.Silu, bias=cvb[:, i:i + 1],
                                       scale=cvg[:, i:i + 1]).then_inc(conv_y, 1)

            act.wait_ge(conv_y, 2)
            act.wait_ge(ring_act, sum(RING_ACT))
            act.wait_ge(ring_dve, sum(RING_DVE))
            for n in range(2 * KT):
                k = MIX_ORDER[n % KT]
                if n < KT:
                    if n == 0:
                        act.wait_ge(ring_mm, len(RING_ACT))
                    act.copy(mix_hi[:, k, :], mix[:, k, :]).then_inc(mix_hi_s, 1)
                if n == KT:
                    act.wait_ge(mix_lo_s, KT)
                act.wait_ge(wo_in[n % 4], 16 * (n // 4 + 1))
                act.copy(wo_hi[n // KT][:, k, :], wo_raw[:, n % 4]).then_inc(wo_hi_s, 1)
            act.dma_start(ln_g[:], a["ln1_g"][0].partition_broadcast(P)).then_inc(ln_in, 16)
            act.dma_start(ln_b[:], a["ln1_b"][0].partition_broadcast(P)).then_inc(ln_in, 16)
            def x1T_copy(t):
                for g in (2 * t, 2 * t + 1):
                    act.wait_ge(x1_tr, g + 1)
                    act.copy(x1T[:, (g % 2) * 4:(g % 2) * 4 + 4, t * P:(t + 1) * P],
                             ps[:, g % 4, :].rearrange("p (k n) -> p k n", k=4)).then_inc(x1T_set, 1)

            def norm(n, x):
                act.wait_ge(stat, 3 * n + 3)
                if n:
                    act.wait_ge(ln_unit, n)
                act.activation(rstd, mv[:, 1:2], ACT.Sqrt, bias=eps).then_inc(ln_sd, 1)
                act.wait_ge(ln_shift, n + 1)
                act.activation(x, x, ACT.Identity, bias=shift, scale=rstd).then_inc(ln_unit, 1)

            for t in range(NT):
                norm(t, x1_tile(t))
                if t == NT - 2:
                    for early in range(NT // 2):
                        x1T_copy(early)
            for t in range(NT // 2, NT):
                x1T_copy(t)
            for c in range(2):
                act.wait_ge(lg_mm, c + 1)
                act.copy(lgT[:, c * 512:(c + 1) * 512], ps[0:EXPERTS, 4 + c, :]).then_inc(lgT_set, 1)
            act.wait_ge(lg_tr, 1)
            act.activation(aff, ps[:, 6, 0:128], ACT.Sigmoid).then_inc(aff_set, 1)

            def split(t, pieces, loaded):
                for n in pieces:
                    act.wait_ge(raw_in[n], loaded * 16 + 16)
                    if not (isinstance(t, int) and t == 0):
                        if n < 4:
                            act.wait_ge(gu_used, t * 4 + (n - 3))
                        else:
                            act.wait_ge(dn_used, t * 2 + (n - 5))
                    act.copy(whi[:, n, :], raw[:, n, :]).then_inc(gu_hi if n < 4 else dn_hi, 1)

            def split_new(t, pieces):
                fresh = act.value_load(fresh_of[0:1, bass.ds(t, 1)], min_val=0, max_val=1)
                with act.If(fresh == 1):
                    split(t, pieces, act.value_load(loads_of[0:1, bass.ds(t, 1)], min_val=0, max_val=EXPERTS - 1))

            def x_hi_part(t):
                act.wait_ge(xg_tr, t + 1)
                if not (isinstance(t, int) and t == 0):
                    act.wait_ge(gu_used, t * 4)
                act.copy(xgT_hi[:].rearrange("p k n -> p (k n)"), pair(2)).then_inc(xgT_hi_s, 1)

            def gated(t):
                act.wait_ge(gu_used, t * 4 + 4)
                if not (isinstance(t, int) and t == 0):
                    act.wait_ge(hid_set, t)
                act.activation(silu[:], ps[:, 0, :], ACT.Silu).then_inc(silu_set, 1)

            def h_hi_part(t):
                act.wait_ge(h_tr, t + 1)
                act.copy(hT_hi[:].rearrange("p f n -> p (f n)"), ps[:, 6, :]).then_inc(hT_hi_s, 1)

            def y_part(t):
                act.wait_ge(dn_used, t * 2 + 2)
                if not (isinstance(t, int) and t == 0):
                    act.wait_ge(y_out, t * 16)
                act.copy(ysb[:], pair(1)).then_inc(y_set, 1)

            def y_store(t):
                act.wait_ge(y_set, t + 1)
                act.dma_start(y_d[bass.ds(t * P, P), :], ysb[:]).then_inc(y_out, 16)

            act.wait_ge(experts_set, 1)
            act.wait_ge(y_filled, 16 * -(-(TILES - MIN_TILES) // NT))
            last_t = act.value_load(last_tile, min_val=MIN_TILES - 1, max_val=TILES - 1)
            split(0, range(4), 0)
            x_hi_part(0)
            split_new(1, range(3))
            gated(0)
            x_hi_part(1)
            split_new(1, [3])
            h_hi_part(0)
            split(0, (4, 5), 0)

            def tile(t):
                split_new(t + 1, range(3))
                gated(t)
                x_hi_part(t + 1)
                split_new(t + 1, [3])
                y_part(t - 1)
                h_hi_part(t)
                y_store(t - 1)
                split_new(t, (4, 5))

            tile(1)
            with act.Fori(2, TILES) as t:
                with act.If(t <= last_t):
                    tile(t)
            y_part(last_t)
            y_store(last_t)
            act.wait_ge(y_out, last_t * 16 + 16)
            act.sem_inc(experts_done, 1)

            for t in range(NT):
                norm(NT + t, x1_tile(t))

        @block.vector
        def _(dve):
            own = [0]

            def link(ins):
                own[0] += 1
                ins.then_inc(dve_chain, 1)
                dve.wait_ge(dve_chain, own[0])

            dve.memset(ones_rank[:], 1.0 / RANK)
            dve.memset(ones_conv[:], 1.0 / 256).then_inc(dve_set, 1)
            dve.memset(wuv[:], 0.0).then_inc(zeros_set, 1)
            dve.memset(wpool[:], 0.0).then_inc(zeros_set, 1)
            link(dve.memset(wuk[:], 0.0))
            link(dve.memset(eps, EPS))
            for i in range(2):
                for h in range(2):
                    rows, w = slice(h * HD, (h + 1) * HD), WINDOWS[2 * i + h]
                    link(dve.memset(invw[rows, i:i + 1], 1.0 / w))
                    if w < 16:
                        dve.memset(corr[rows, i, w:16], 1.0)
                    for c in range(w):
                        last = dve.memset(corr[rows, i, c:c + 1], w / (c + 1.0))
                    link(last)

            def w_split(j):
                dve.wait_ge(w_hi_s, j + 1)
                dve.tensor_tensor(w_lo[:, j % 2], w_raw[:, j % 2], f32(w_hi[:, j % 2]), ALU.subtract).then_inc(w_lo_s, 1)

            for g in range(2 * NT):
                t, half = divmod(g, 2)
                if g == NT:
                    w_split(0)
                part = (slice(None), slice(half * 4, half * 4 + 4), slice(t * P, (t + 1) * P))
                dve.wait_ge(x_hi, g + 1)
                dve.tensor_tensor(xT_lo[part], ps[:, g % 4, :].rearrange("p (k n) -> p k n", k=4), f32(xT_hi[part]),
                                  ALU.subtract).then_inc(x_lo, 1)
            dve.wait_ge(wuk_tr, 1)
            for h in range(HEADS):
                rows = slice((h % 2) * HD, (h % 2 + 1) * HD)
                dve.tensor_scalar(wuk[rows, h, :], ps[rows, 0, (h // 2) * P:(h // 2 + 1) * P], HD ** -0.5, None,
                                  ALU.mult).then_inc(wuk_set, 1)
            dve.wait_ge(par_in, 16 * 7)

            def unit(k):
                name, i, j = UNITS[k]
                if name == "cT" and i == 1:
                    dve.wait_ge(c_hi, 1)
                    dve.tensor_tensor(cT_lo[:], cT[:], f32(cT_hi[:]), ALU.subtract).then_inc(c_lo, 1)
                if name == "ms" and i == 1:
                    dve.wait_ge(unit_act, seen(BY_ACT, k))
                    dve.reciprocal(rstd_kv[:], rstd_kv[:]).then_inc(kv_norm, 1)
                    dve.wait_ge(kv_norm, 1)
                    dve.scalar_tensor_tensor(cT[:], kvT[:], kvg, rstd_kv[:], ALU.mult, ALU.mult).then_inc(kv_norm, 3)
                if name == "ikw" and i == 1:
                    dve.wait_ge(ik_hi, 1)
                    dve.tensor_tensor(ikT_lo[0:IDIM, :], iT[0:IDIM, :], f32(ikT_hi[0:IDIM, :]), ALU.subtract
                                      ).then_inc(ik_lo, 1)
                if not BY_DVE[k]:
                    return
                src = ps[:, 4 + k % 4, :]
                t0, n = COLS[j][2][i] if j is not None else (i * 512, 512)
                if name[:2] == "iq":
                    part = (slice(None), int(name[2]), slice(t0 - 256, t0 - 256 + n))
                    dve.wait_ge(unit_act, seen(BY_ACT, k))
                    dve.tensor_tensor(iqT_lo[part], src[:, 0:n], f32(iqT_hi[part]), ALU.subtract).then_inc(unit_dve, 1)
                elif name == "iwT":
                    dve.wait_ge(unit_mm, k + 1)
                    dve.tensor_scalar(iw[:, 4 * i:4 * i + 4, :],
                                      src.rearrange("p (t c) -> p t c", t=4)[:, :, IDIM:IDIM + IHEADS],
                                      (IHEADS * IDIM) ** -0.5, None, ALU.mult).then_inc(unit_dve, 1)
                elif name[0] == "a":
                    ti = int(name[1])
                    if k == UNITS.index(("a0", 0, 6)):
                        dve.memset(hpad[:, :, 0:PAD_H], 0.0).then_inc(pads_set, 1)
                    dve.wait_ge(unit_mm, k + 1)
                    dve.wait_ge(unit_act, seen(BY_ACT, [q for q, u in enumerate(UNITS) if u[0] == "gate1"][1]))
                    dve.tensor_tensor(hpad[:, ti, PAD_H + t0:PAD_H + t0 + n], src, sig[:, ti, t0:t0 + n], ALU.mult
                                      ).then_inc(unit_dve, 1)

            def index(u):
                b, h = IDX[u]
                acc, r = bias[:, AT[b]:AT[b] + WIDTH[b]], relu[:, u % 2, 0:WIDTH[b]]
                dve.wait_ge(idx_relu, u + 1)
                if h == 0:
                    dve.wait_ge(unit_dve, seen(BY_DVE, UNITS.index(("iwT", 1, None))))
                    dve.tensor_scalar(acc, r, iw[:, b, h:h + 1], None, ALU.mult).then_inc(idx_sum, 1)
                else:
                    dve.wait_ge(idx_sum, u)
                    dve.scalar_tensor_tensor(acc, r, iw[:, b, h:h + 1], acc, ALU.mult, ALU.add).then_inc(idx_sum, 1)
                if h == IHEADS - 1:
                    c = COLUMN[b]
                    dve.wait_ge(idx_sum, u + 1)
                    dve.tensor_reduce(top_score[:, c:c + 1], acc, AX.X, ALU.max, apply_absolute_value=True
                                      ).then_inc(bound, 1)

            def item(k, between):
                _, i, j = UNITS[k]
                if j is not None and i == 0 and j + 1 < len(COLS):
                    w_split(j + 1)
                for u in between:
                    index(u)
                unit(k)

            for p in PLAN[:LAST_IDX + 1]:
                item(*p)
            rest = PLAN[LAST_IDX + 1:]

            dve.wait_ge(bound, len(BLOCKS))
            for b in BLOCKS:
                c = COLUMN[b]
                dve.memset(thr[:, c:c + 1], float(WIDTH[b] - (TOPK if b in COUNT_DVE else 2 * TOPK)))
            dve.memset(low, -1.0)
            dve.memset(cand, 0.0).then_inc(cand_set, 1)
            dve.wait_ge(cand_set, 1)
            dve.wait_ge(masked_s, len(BLOCKS))
            taps = 0
            for r in range(ROUNDS):
                step, now, then = 2.0 ** -r, cands[r % 2], cands[(r + 1) % 2]
                for i, b in enumerate(COUNT_DVE):
                    c = COLUMN[b]
                    if i:
                        dve.wait_ge(counted_dve, len(COUNT_DVE) * r + i)
                    dve.tensor_scalar(junk_dve[:, 0:WIDTH[b]], bias[:, AT[b]:AT[b] + WIDTH[b]], now[:, c:c + 1], 0.0,
                                      ALU.is_lt, ALU.add, accum_out=res[:, c:c + 1]).then_inc(counted_dve, 1)
                if rest:
                    item(*rest.pop(0))
                elif taps < TAPS:
                    if taps == 0:
                        dve.wait_ge(unit_mm, N_UNITS)
                    for w in range(taps, min(taps + 5, TAPS)):
                        dve.tensor_scalar(diag[:, w, :], ident[:], convw[:, w:w + 1], None, ALU.mult
                                          ).then_inc(diag_set, 1)
                    taps = min(taps + 5, TAPS)
                dve.scalar_tensor_tensor(then, low, step / 2, top_score, ALU.add, ALU.mult)
                link(dve.scalar_tensor_tensor(if_passed, low, 1.5 * step, top_score, ALU.add, ALU.mult))
                dve.wait_ge(counted_dve, len(COUNT_DVE) * (r + 1))
                dve.wait_ge(counted_act, len(COUNT_ACT) * (r + 1))
                link(dve.tensor_tensor(passed[:], res, thr, ALU.is_le))
                if r + 1 < ROUNDS:
                    dve.copy_predicated(then, passed[:], if_passed).then_inc(cand_set, 1)
                    dve.wait_ge(cand_set, r + 2)
                link(dve.scalar_tensor_tensor(low, passed[:], step, low, ALU.mult, ALU.add))
            link(dve.scalar_tensor_tensor(hi, low, 2.0 ** (1 - ROUNDS), top_score, ALU.add, ALU.mult))
            link(dve.tensor_tensor(lo, low, top_score, ALU.mult))
            assert not rest and taps == TAPS

            def choose(b, k):
                c, w = COLUMN[b], WIDTH[b]
                x = bias[:, AT[b]:AT[b] + w]
                A, T, N = above[:, 0:w], tied[:, 0:w], tie_no[:, 0:w]
                if k == 0:
                    link(dve.tensor_scalar(A, x, hi[:, c:c + 1], 0.0, ALU.is_gt, ALU.add, accum_out=need[:, c:c + 1]))
                elif k == 1:
                    link(dve.tensor_scalar(need[:, c:c + 1], need[:, c:c + 1], -1.0, float(TOPK), ALU.mult, ALU.add))
                elif k == 2:
                    link(dve.scalar_tensor_tensor(T, x, lo[:, c:c + 1], A, ALU.is_ge, ALU.subtract))
                elif k == 3:
                    link(dve.tensor_tensor_scan(N, T, T, 0.0, ALU.add, ALU.max))
                elif k == 4:
                    link(dve.scalar_tensor_tensor(T, N, need[:, c:c + 1], T, ALU.is_le, ALU.mult))
                elif k == 5:
                    link(dve.scalar_tensor_tensor(T, T, -1.0, A, ALU.add, ALU.add))
                elif k == 6:
                    link(dve.tensor_scalar(x, T, BIG, None, ALU.mult))

            for step in STEPS:
                kind = step[0]
                if kind in RING:
                    r = step[-1]
                    src = ps[:, 4 + r % 3, :]
                    if not RING_DVE[r]:
                        continue
                    dve.wait_ge(ring_mm, r + 1)
                if kind == "choose":
                    choose(step[1], step[2])
                elif kind == "ql":
                    _, half, h, r = step
                    dve.wait_ge(ring_act, seen(RING_ACT, r))
                    dve.tensor_tensor(ql_lo[:, h, :], src, f32(ql_hi[:, h, :]), ALU.subtract).then_inc(ring_dve, 1)
                elif kind == "qk":
                    _, b, h = step
                    col = b * HEADS + h
                    u = score_no(b, h)
                    dve.wait_ge(qk_mm, u + 1)
                    if u == 0:
                        dve.wait_ge(tri_set, 3)
                        dve.wait_ge(pooled, 4)
                    if u == 4:
                        dve.wait_ge(ring_mm, RING_OF["pw", 1, 1] + 1)
                    if u >= 8:
                        if u < 2 * SHORT_PAIRS:
                            bb, jj = PAIRS[u // 2 - 4]
                        elif u < 2 * SHORT_PAIRS + 4:
                            bb, jj = PAIRS[SHORT_PAIRS - 4 + u - 2 * SHORT_PAIRS]
                        else:
                            bb, jj = PAIRS[u // 2 - 2]
                        dve.wait_ge(ring_mm, RING_OF["pt", bb, jj, bb // 2] + 1)
                    dve.tensor_tensor_reduce(out=probs_at(u)[:, 0:WIDTH[b]], in0=scores_at(u, WIDTH[b]),
                                             in1=bias[:, AT[b]:AT[b] + WIDTH[b]], scale=-1.0, scalar=3.0e38,
                                             op0=ALU.add, op1=ALU.min, accum_out=negmax[:, col:col + 1]
                                             ).then_inc(masked_max, 1)
                elif kind == "pt":
                    _, b, j, n, r = step
                    no = PT_NO[b, j, n]
                    if no >= 3:
                        dve.wait_ge(pv_mm, no - 2)
                    w = 256 * (min(2 * n + 2, b + 1) - 2 * n)
                    dve.tensor_copy(pT[:, no % 3, 0:w], src[:, 0:w]).then_inc(ring_dve, 1)
                elif kind == "rl_set":
                    _, b = step
                    dve.wait_ge(exped, 2 * last_no(b) + 2)
                    if b >= 2:
                        dve.wait_ge(ring_mm, RING_OF["rl", b - 2] + 1)
                    sums_b = rowsum[:, b * HEADS:(b + 1) * HEADS]
                    link(dve.reciprocal(sums_b, sums_b))
                    dve.tensor_copy(rlrep[b % 2][:], sums_b.unsqueeze(2).to_broadcast([P, HEADS, HD])).then_inc(rl_set, 1)
                elif kind == "uv":
                    _, q, j, r = step
                    dve.wait_ge(ring_act, seen(RING_ACT, RING_OF["rl", 2 * q + 1]))
                    dve.tensor_tensor(mix[:, j, q * 256:(q + 1) * 256], src[:, 0:256], rlT[:, j, :], ALU.mult
                                      ).then_inc(ring_dve, 1)
                elif kind == "cm":
                    _, c, r = step
                    for i in range(2):
                        ch = conv[:, i, c * 512:(c + 1) * 512]
                        dve.tensor_tensor(ch, ch, src, ALU.subtract).then_inc(ring_dve if i else conv_c, 1)
                elif kind == "cr":
                    part = crstd[:, step[1] * 256:(step[1] + 1) * 256]
                    dve.wait_ge(ring_act, seen(RING_ACT, RING_OF["cv", step[1] // 2]))
                    dve.reciprocal(part, part).then_inc(conv_n, 1)
                elif kind == "cn":
                    dve.wait_ge(conv_sq, 4)
                    dve.wait_ge(conv_n, 4)
                    for i in range(2):
                        dve.tensor_tensor(conv[:, i, :], conv[:, i, :], crstd[:], ALU.mult).then_inc(conv_n, 1)

            def wo_split(n):
                k = MIX_ORDER[n % KT]
                if n < KT:
                    dve.wait_ge(mix_hi_s, n + 1)
                    dve.tensor_tensor(mix_lo[:, k, :], mix[:, k, :], f32(mix_hi[:, k, :]), ALU.subtract
                                      ).then_inc(mix_lo_s, 1)
                dve.wait_ge(wo_hi_s, n + 1)
                dve.tensor_tensor(wo_lo[n // KT][:, k, :], wo_raw[:, n % 4], f32(wo_hi[n // KT][:, k, :]), ALU.subtract
                                  ).then_inc(wo_lo_s, 1)

            def norm_stats(n, x, meanwhile):
                for c in range(2):
                    dve.bn_stats(stats[:, c, :], x[:, c * 512:(c + 1) * 512]).then_inc(stat, 1)
                dve.wait_ge(stat, 3 * n + 2)
                dve.bn_aggr(mv, stats).then_inc(stat, 1)
                dve.wait_ge(stat, 3 * n + 3)
                if meanwhile:
                    norm_gain(*meanwhile)
                dve.wait_ge(ln_sd, n + 1)
                link(dve.reciprocal(rstd, rstd))
                dve.scalar_tensor_tensor(shift, mv[:, 0:1], -1.0, rstd, ALU.mult, ALU.mult).then_inc(ln_shift, 1)
                dve.wait_ge(ln_shift, n + 1)

            def norm_gain(n, x, g):
                dve.wait_ge(ln_unit, n + 1)
                dve.tensor_tensor(x, x, g[:], ALU.mult).then_inc(ln_scaled, 1)

            dve.wait_ge(ring_mm, len(RING_ACT))
            dve.wait_ge(ring_act, sum(RING_ACT))
            for n in range(2 * KT):
                wo_split(n)
            for n in range(2 * NT):
                hf, t = divmod(n, NT)
                y = x1_tile(t)[:, hf * 512:(hf + 1) * 512]
                dve.wait_ge(wo_mm, n + 1)
                dve.wait_ge(xr_in[n % 4], 16 * (n // 4 + 1))
                dve.scalar_tensor_tensor(y, x_res[:, n % 4], ALPHA, ps[:, n % 8, :], ALU.mult, ALU.add).then_inc(y1_set, 1)
                if hf:
                    dve.wait_ge(y1_set, n + 1)
                    if t == 1:
                        dve.wait_ge(ln_in, 32)
                    norm_stats(t, x1_tile(t), t and (t - 1, x1_tile(t - 1), ln_g))
            norm_gain(NT - 1, x1_tile(NT - 1), ln_g)

            dve.wait_ge(route_in, 32)
            dve.wait_ge(rconst, 4)
            dve.wait_ge(aff_set, 1)
            aff3 = aff.rearrange("p (t e) -> p t e", t=NT)
            score3 = score.rearrange("p (t e) -> p t e", t=NT)
            link(dve.tensor_tensor(score3, aff3, rbias.unsqueeze(1).to_broadcast([P, NT, EXPERTS]), ALU.add))
            s4 = score.rearrange("p (n c) -> p n c", c=PER_GROUP)
            dve.tensor_tensor(pairs[:, :, 0:3], s4[:, :, 0:3], s4[:, :, 1:4], ALU.add)
            dve.tensor_tensor(pairs[:, :, 3:5], s4[:, :, 0:2], s4[:, :, 2:4], ALU.add)
            link(dve.tensor_tensor(pairs[:, :, 5:6], s4[:, :, 0:1], s4[:, :, 3:4], ALU.add))
            link(dve.tensor_reduce(gs, pairs, AX.X, ALU.max))
            gs3, gv3 = gs.rearrange("p (t g) -> p t g", t=NT), gv.rearrange("p (t g) -> p t g", t=NT)
            fg3 = first_g.rearrange("p (t g) -> p t g", t=NT)

            def first_best(values, weights, scratch, onehot, n):
                wide = [P, NT, n]
                link(dve.tensor_reduce(top, values, AX.X, ALU.max))
                link(dve.tensor_tensor(scratch, values, top.unsqueeze(2).to_broadcast(wide), ALU.is_equal))
                link(dve.tensor_tensor(scratch, scratch, weights.unsqueeze(1).to_broadcast(wide), ALU.mult))
                link(dve.tensor_reduce(top, scratch, AX.X, ALU.max))
                link(dve.tensor_tensor(onehot, scratch, top.unsqueeze(2).to_broadcast(wide), ALU.is_equal))

            first_best(gs3, w4, gv3, fg3, GROUPS)
            link(dve.tensor_scalar(first_g, first_g, BIG, -BIG, ALU.mult, ALU.add))
            link(dve.tensor_tensor(masked.rearrange("p (n c) -> p n c", c=PER_GROUP), s4,
                                   first_g.unsqueeze(2).to_broadcast([P, NT * GROUPS, PER_GROUP]), ALU.add))
            masked3, pick3 = masked.rearrange("p (t e) -> p t e", t=NT), pick.rearrange("p (t e) -> p t e", t=NT)
            oh3 = [oh.rearrange("p (t e) -> p t e", t=NT) for oh in (oh1, oh2)]
            first_best(masked3, w16, pick3, oh3[0], EXPERTS)
            link(dve.scalar_tensor_tensor(masked, oh1, -BIG, masked, ALU.mult, ALU.add))
            first_best(masked3, w16, pick3, oh3[1], EXPERTS)
            for oh, g_ in ((oh3[0], ga), (oh3[1], gb)):
                link(dve.tensor_tensor(pick3, aff3, oh, ALU.mult))
                link(dve.tensor_reduce(g_, pick3, AX.X, ALU.add))
            dve.tensor_tensor(pick, oh1, oh2, ALU.add).then_inc(oh_set, 1)
            link(dve.tensor_tensor(gsum, ga, gb, ALU.add))
            link(dve.reciprocal(gsum, gsum))
            link(dve.tensor_tensor(gate_of[:, 0:NT], ga, gsum, ALU.mult))
            link(dve.tensor_tensor(gate_of[:, NT:2 * NT], gb, gsum, ALU.mult))
            dve.wait_ge(m_tr, 1)
            link(dve.tensor_copy(mT[:], pair(0)[0:16, :]))
            link(dve.tensor_tensor_scan(rank[:], ones_row[:], mT[:], 0.0, ALU.mult, ALU.add))
            dve.tensor_scalar(cmp[:, 0:8], thr8, rank[:, S - 1:S], 0.0, ALU.is_lt, ALU.add, accum_out=ntile
                              ).then_inc(ntile_set, 1)
            dve.wait_ge(ntile_set, 1)
            dve.wait_ge(cum_mm, 1)
            link(dve.tensor_scalar(slot0, ps[0:16, 4, 0:1], float(P), -1.0, ALU.mult, ALU.add))
            link(dve.tensor_tensor(cum, ps[0:16, 4, 0:1], ntile, ALU.add))
            dve.tensor_scalar(cmp, tcol, cum, None, ALU.is_ge).then_inc(cmp_set, 1)
            dve.tensor_scalar(rank[:], rank[:], slot0, None, ALU.add).then_inc(slotT_set, 1)
            dve.wait_ge(te_mm, 1)
            link(dve.tensor_copy(expert_row, ps[0:1, 5, 0:TILES + 1]))
            link(dve.tensor_scalar(live_row, expert_row, float(EXPERTS), 0.0, ALU.is_lt, ALU.add, accum_out=tiles_used))
            link(dve.tensor_tensor(fresh_row[:, 1:], expert_row[:, 1:], expert_row[:, :TILES], ALU.is_gt))
            link(dve.memset(fresh_row[:, 0:1], 1.0))
            link(dve.tensor_tensor(fresh_row, fresh_row, live_row, ALU.mult))
            link(dve.tensor_tensor_scan(loads_row, ones_row[0:1, 0:TILES + 1], fresh_row, -1.0, ALU.mult, ALU.add))
            dve.tensor_scalar(expert_of, expert_row, float(EXPERTS - 1), None, ALU.min)
            dve.tensor_copy(fresh_of, fresh_row)
            dve.tensor_copy(loads_of, loads_row)
            dve.tensor_scalar(last_tile, tiles_used, -1.0, None, ALU.add).then_inc(experts_set, 1)
            dve.wait_ge(s_tr, 1)
            for i in range(2):
                link(dve.tensor_tensor(pick3, ps[:, 7, 0:128].rearrange("p (t e) -> p t e", t=NT), oh3[i], ALU.mult))
                link(dve.tensor_reduce(slotf[:, i * NT:(i + 1) * NT], pick3, AX.X, ALU.add))
            dve.tensor_copy(slot_i, slotf).then_inc(places_set, 1)
            dve.wait_ge(places_set, 1)
            dve.tensor_scalar(row_i, slot_i, P - 1, None, ALU.bitwise_and)
            link(dve.tensor_scalar(col_i, slot_i, 7, None, ALU.logical_shift_right))
            dve.tensor_copy(rowf, row_i)
            link(dve.tensor_copy(colf, col_i))
            hot, wide = [P, 2 * NT, P], [P, 2 * NT, TILES + 1]
            dve.tensor_tensor(slot_row[:], place_no.unsqueeze(1).to_broadcast(hot), rowf.unsqueeze(2).to_broadcast(hot),
                              ALU.is_equal)
            link(dve.tensor_tensor(slot_col[:, :, :, 0], tile_no.unsqueeze(1).to_broadcast(wide),
                                   colf.unsqueeze(2).to_broadcast(wide), ALU.is_equal))
            link(dve.tensor_tensor(slot_col[:, :, :, 1], slot_col[:, :, :, 0], gate_of.unsqueeze(2).to_broadcast(wide),
                                   ALU.mult))
            dve.tensor_tensor(slot_col[:, :, :, 0], slot_col[:, :, :, 0], token_of.unsqueeze(2).to_broadcast(wide),
                              ALU.mult).then_inc(hot_set, 1)
            dve.wait_ge(table_mm, 1)
            filled = ps[:, 6, 0:2 * (TILES + 1)].rearrange("p (t c) -> p t c", c=2)
            dve.tensor_copy(slot_token[:], filled[:, :, 0])
            dve.tensor_copy(slot_gate[:], filled[:, :, 1]).then_inc(table_set, 1)
            dve.wait_ge(table_set, 1)

            def split(pieces, loaded):
                for n in pieces:
                    if n < 4:
                        dve.wait_ge(gu_hi, loaded * 4 + (n + 1))
                    else:
                        dve.wait_ge(dn_hi, loaded * 2 + (n - 3))
                    dve.tensor_tensor(wlo[:, n, :], raw[:, n, :], f32(whi[:, n, :]), ALU.subtract
                                      ).then_inc(gu_lo if n < 4 else dn_lo, 1)

            def split_new(t, pieces):
                fresh = dve.value_load(fresh_of[0:1, bass.ds(t, 1)], min_val=0, max_val=1)
                with dve.If(fresh == 1):
                    split(pieces, dve.value_load(loads_of[0:1, bass.ds(t, 1)], min_val=0, max_val=EXPERTS - 1))

            def x_lo_part(t):
                dve.wait_ge(xgT_hi_s, t + 1)
                dve.tensor_tensor(xgT_lo[:].rearrange("p k n -> p (k n)"), pair(2),
                                  f32(xgT_hi[:]).rearrange("p k n -> p (k n)"), ALU.subtract).then_inc(xgT_lo_s, 1)

            def hidden(t):
                dve.wait_ge(silu_set, t + 1)
                if not (isinstance(t, int) and t == 0):
                    dve.wait_ge(h_tr, t)
                dve.scalar_tensor_tensor(hid[:], silu[:], slot_gate[:, bass.ds(t, 1)], ps[:, 1, :], ALU.mult, ALU.mult
                                         ).then_inc(hid_set, 1)

            def h_lo_part(t):
                dve.wait_ge(hT_hi_s, t + 1)
                dve.tensor_tensor(hT_lo[:].rearrange("p f n -> p (f n)"), ps[:, 6, :],
                                  f32(hT_hi[:]).rearrange("p f n -> p (f n)"), ALU.subtract).then_inc(hT_lo_s, 1)

            last_t = dve.value_load(last_tile, min_val=MIN_TILES - 1, max_val=TILES - 1)
            split(range(4), 0)
            x_lo_part(0)
            split_new(1, range(3))
            hidden(0)
            x_lo_part(1)
            split_new(1, [3])
            h_lo_part(0)
            split((4, 5), 0)

            def tile(t):
                split_new(t + 1, range(3))
                hidden(t)
                x_lo_part(t + 1)
                split_new(t + 1, [3])
                h_lo_part(t)
                split_new(t, (4, 5))

            tile(1)
            with dve.Fori(2, TILES) as t:
                with dve.If(t <= last_t):
                    tile(t)

            dve.wait_ge(ln2_in, 32)
            for t in range(NT):
                dve.wait_ge(y_added[t], 32)
                norm_stats(NT + t, x1_tile(t), t and (NT + t - 1, x1_tile(t - 1), ln2_g))
            norm_gain(2 * NT - 1, x1_tile(NT - 1), ln2_g)

        @block.gpsimd
        def _(pool):
            small = dict(allow_small_or_imprecise_dtypes=True)
            pool.memset(ident[:], 0.0).then_inc(ident_set, 1)
            pool.wait_ge(ident_set, 1)
            pool.affine_select(ident[:], ident[:], [[-1, P]], ALU.not_equal, 1.0, 0, 1).then_inc(ident_set, 1)
            pool.wait_ge(stack_in, 16 * 20)
            pool.memset(bias[:, 0:AT[2]], 0.0).then_inc(tri_set, 1)
            pool.wait_ge(tri_set, 1)
            for b in range(FIRST_TOPK):
                diag = bias[:, AT[b] + b * P:AT[b] + (b + 1) * P]
                pool.affine_select(diag, diag, [[-1, P]], ALU.is_ge, -BIG, 0, 1).then_inc(tri_set, 1)
            for i, b in enumerate(BLOCKS):
                diag = bias[:, AT[b] + b * P:AT[b] + (b + 1) * P]
                pool.wait_ge(bound, i + 1)
                pool.affine_select(diag, diag, [[-1, P]], ALU.is_ge, -3.0e38, 0, 1).then_inc(masked_s, 1)
            pool.wait_ge(unit_dve, sum(BY_DVE))
            pool.wait_ge(pads_set, 1)
            pool.wait_ge(idx_sum, len(IDX))
            pool.wait_ge(par_in, 16 * 7)
            own = [0]

            def link(ins):
                own[0] += 1
                ins.then_inc(pool_chain, 1)
                pool.wait_ge(pool_chain, own[0])

            def tap(w):
                src, by = hpad[:, 1, w:w + S], convw[:, TAPS + w:TAPS + w + 1]
                if w == 0:
                    pool.tensor_scalar(conv[:, 1, :], src, by, convb[:, 1:2], ALU.mult, ALU.add).then_inc(conv1, 1)
                else:
                    pool.wait_ge(conv1, w)
                    pool.tensor_scalar(tapped[:], src, by, None, ALU.mult).then_inc(conv1_mul, 1)
                    pool.wait_ge(conv1_mul, w)
                    pool.tensor_tensor(conv[:, 1, :], conv[:, 1, :], tapped[:], ALU.add).then_inc(conv1, 1)

            for w in range(TAPS_FIRST):
                tap(w)
            pool.wait_ge(unit_act, POOL_UNITS)
            pool.memset(uT[:, :, 0:PAD_U], 0.0)
            pool.memset(doubled[0][:, 0:PAD_U], 0.0)
            link(pool.memset(doubled[1][:, 0:PAD_U], 0.0))
            for i in range(2):
                token, cur, w = uT[:, i, :], uT[:, i, :], 1
                for turn in range(2 * i + 2):
                    rows = slice(0, P) if 2 * w <= WINDOWS[2 * i] else slice(HD, P)
                    out = doubled[turn % 2]
                    link(pool.tensor_tensor(out[rows, w:], cur[rows, w:], cur[rows, 0:PAD_U + S - w], ALU.add))
                    cur, w = out, 2 * w
                    if w in WINDOWS[2 * i:2 * i + 2]:
                        h = WINDOWS[2 * i:2 * i + 2].index(w)
                        hr = slice(h * HD, (h + 1) * HD)
                        start = cur[hr, PAD_U:PAD_U + 16]
                        link(pool.tensor_tensor(start, start, corr[hr, i, :], ALU.mult))
                        link(pool.tensor_scalar(cur[hr, PAD_U:], cur[hr, PAD_U:], invw[hr, i:i + 1], None, ALU.mult))
                        pool.tensor_tensor(sums[hr, i, PAD_U:], cur[hr, PAD_U:], token[hr, PAD_U:], ALU.subtract
                                           ).then_inc(pooled, 1)
                        pool.wait_ge(pooled, 2 * i + h + 1)
            for w in range(TAPS_FIRST, TAPS):
                tap(w)
            for t in range(NT):
                pool.wait_ge(ln_scaled, t + 1)
                pool.wait_ge(ln_in, 32)
                pool.tensor_tensor(x1_tile(t), x1_tile(t), ln_b[:], ALU.add).then_inc(x1_set, 1)
            pool.wait_ge(y1_set, 2 * NT)
            pool.iota(w4, [[-1, GROUPS]], GROUPS, 0, **small).then_inc(rconst, 1)
            pool.iota(w16, [[-1, EXPERTS]], EXPERTS, 0, **small)
            pool.iota(thr8, [[P, NT]], 0, 0, **small)
            pool.iota(tcol, [[1, TILES + 1]], 0, 0, **small)
            pool.memset(ones16, 1.0)
            pool.memset(ones_row[:], 1.0)
            pool.iota(place_no, [[1, P]], 0, 0, **small)
            pool.iota(tile_no, [[1, TILES + 1]], 0, 0, **small)
            pool.iota(token_of.rearrange("p (i t) -> p i t", i=2), [[0, 2], [P, NT]], 0, 1, **small
                      ).then_inc(rconst, 1)
            pool.memset(upper, 1.0).then_inc(rconst, 1)
            pool.wait_ge(rconst, 3)
            pool.affine_select(upper, upper, [[1, EXPERTS]], ALU.is_gt, 0.0, 0, -1).then_inc(rconst, 1)
            pool.wait_ge(table_set, 1)
            pool.tensor_copy(idx_now[:], slot_token[:, 0:1]).then_inc(idx0_set, 1)
            pool.wait_ge(x1_out, 16 * NT)
            pool.wait_ge(idx0_set, 1)
            pool.indirect_dma_start(xg[:], None, x1_d, bass.IndirectOffsetOnAxis(ap=idx_now[:], axis=0)
                                    ).then_inc(xg_in, 16)

            def fetch(t):
                pool.wait_ge(xg_tr, t)
                pool.tensor_copy(idx_now[:], slot_token[:, bass.ds(t, 1)]).then_inc(idx_set, 1)
                pool.wait_ge(x1_out, 16 * NT)
                pool.wait_ge(idx_set, t)
                pool.indirect_dma_start(xg[:], None, x1_d, bass.IndirectOffsetOnAxis(ap=idx_now[:], axis=0)
                                        ).then_inc(xg_in, 16)

            last_t = pool.value_load(last_tile, min_val=MIN_TILES - 1, max_val=TILES - 1)
            for t in range(1, NT + 1):
                fetch(t)
                pool.tensor_scalar(x1_tile(t - 1), x1_tile(t - 1), ALPHA, None, ALU.mult).then_inc(x1_scaled, 1)
            with pool.Fori(NT + 1, TILES + 1) as t:
                with pool.If(t <= last_t + 1):
                    fetch(t)
            pool.wait_ge(experts_done, 1)
            pool.wait_ge(x1_scaled, NT)
            def add_rows(t, i):
                n = i * NT + t
                if i:
                    pool.wait_ge(y_added[t], 16)
                pool.indirect_dma_start(x1_tile(t), None, y_d,
                                        bass.IndirectOffsetOnAxis(ap=slot_i[:, n:n + 1], axis=0),
                                        compute_op=ALU.add).then_inc(y_added[t], 16)

            def add_b(t):
                if t == 0:
                    pool.wait_ge(ln2_in, 32)
                pool.wait_ge(ln_scaled, NT + t + 1)
                pool.tensor_tensor(x1_tile(t), x1_tile(t), ln2_b[:], ALU.add).then_inc(fin_done, 1)

            add_rows(0, 0)
            for t in range(NT):
                if t + 1 < NT:
                    add_rows(t + 1, 0)
                add_rows(t, 1)
                if t >= ADDS_BEHIND:
                    add_b(t - ADDS_BEHIND)
            for t in range(NT - ADDS_BEHIND, NT):
                add_b(t)


_INS = ["x", "w_in", "kv_norm_g", "w_uk", "w_uv", "w_pool", "pool_scale", "conv_w", "conv_b", "conv_ln_g",
        "conv_ln_b", "w_o", "ln1_g", "ln1_b", "router_w", "router_bias", "w_gate", "w_up", "w_down", "ln2_g", "ln2_b"]


def kernel(**inputs):
    import concourse.bacc as bacc
    from concourse.bass_utils import run_bass_kernel_spmd

    nc = bacc.Bacc("TRN2", target_bir_lowering=False, num_devices=1)
    arrays, a = {}, {}
    for name in _INS:
        array = np.ascontiguousarray(inputs[name])
        arrays[f"in_{name}"] = array
        a[name] = nc.dram_tensor(f"in_{name}", array.shape, mybir.dt.from_np(array.dtype), kind="ExternalInput").ap()
    a["out"] = nc.dram_tensor("out_0", (1, S, D), F32, kind="ExternalOutput").ap()
    program(nc, a)
    return run_bass_kernel_spmd(nc, [arrays], core_ids=[0]).results[0]["out_0"]
```
